# Optimizing a Trainium2 kernel written in Bass

```python
import jax
import jax.numpy as jnp
from jax import lax
import numpy as np

D_MODEL = 2048
BATCH = 1
SEQ = 512
DEPTH = 1
DEC_BATCH = 8
DEC_SEQ = 8
PAST_LEN = 4096
PAGE_SIZE = 128

A_HEAD = 64
A_WIDTH = D_MODEL // 2
A_HEADS = A_WIDTH // A_HEAD
A_DECAY_LORA = 64
A_ICL_LORA = 64
A_GATE_LORA = 160
A_GN_EPS = 64e-5
B_HEADS = 8
B_QK_HEAD = (D_MODEL // 2) // B_HEADS
B_V_HEAD = 2 * B_QK_HEAD
B_QK_WIDTH = B_HEADS * B_QK_HEAD
B_V_WIDTH = B_HEADS * B_V_HEAD
RET_CHUNK = 128
ROT_BASE = 10000.0
N_KEYS = 128
N_EXPERTS = N_KEYS * N_KEYS
PEER_HEADS = 8
PEER_QDIM = 256
PEER_TOPK = 16
PEER_BLOCK = 128
NORM_EPS = 1e-6
SHIFT_W = 3 * A_WIDTH + A_DECAY_LORA + A_ICL_LORA + A_GATE_LORA
A_SPLITS = [A_WIDTH, 2 * A_WIDTH, 3 * A_WIDTH, 3 * A_WIDTH + A_DECAY_LORA,
            3 * A_WIDTH + A_DECAY_LORA + A_ICL_LORA]
IN_SPLITS = [SHIFT_W, SHIFT_W + B_QK_WIDTH, SHIFT_W + 2 * B_QK_WIDTH,
             SHIFT_W + 2 * B_QK_WIDTH + B_V_WIDTH, SHIFT_W + 2 * B_QK_WIDTH + 2 * B_V_WIDTH]
IN_W = IN_SPLITS[-1] + 2 * D_MODEL
F32 = jnp.float32

kernel_name = 'rwkv7_retention_peer_hybrid_step'

def rmsnorm(x, g):
    xf = x.astype(F32)
    y = xf * lax.rsqrt(jnp.mean(xf * xf, axis=-1, keepdims=True) + NORM_EPS)
    return y.astype(x.dtype) * g

def token_shift(z, prev, mu):
    z_prev = jnp.concatenate([prev[:, None, :].astype(z.dtype), z[:, :-1]], axis=1)
    return z + (z_prev - z) * mu, z[:, -1]

def rwkv7_scan(s0, r, w, k, v, kk, a):
    def step(s, inp):
        r_t, w_t, k_t, v_t, kk_t, a_t = inp
        sa = jnp.einsum('bhvk,bhk->bhv', s, -kk_t)
        s = (s * w_t[:, :, None, :] + sa[..., None] * (kk_t * a_t)[:, :, None, :]
             + v_t[..., None] * k_t[:, :, None, :])
        return s, jnp.einsum('bhvk,bhk->bhv', s, r_t)
    xs = [jnp.swapaxes(t, 0, 1) for t in (r, w, k, v, kk, a)]
    s_final, y = lax.scan(step, s0, xs)
    return jnp.swapaxes(y, 0, 1), s_final

def rwkv7_branch(z, shift_prev, s0, mu_shift, w0, w_w2, a0, w_a2, w_g2, k_k, k_a, r_k, lnx_w, lnx_b):
    bsz, t, _ = z.shape
    z, shift_new = token_shift(z, shift_prev, mu_shift)
    r, k, v, wl, al, gl = jnp.split(z, A_SPLITS, axis=-1)
    w = -jax.nn.softplus(-(w0 + jnp.tanh(wl) @ w_w2).astype(F32)) - 0.5
    decay = jnp.exp(-jnp.exp(w))
    a = jax.nn.sigmoid(a0 + al @ w_a2)
    g = jax.nn.sigmoid(gl) @ w_g2

    def heads(u):
        return u.reshape(bsz, t, A_HEADS, A_HEAD).astype(F32)

    kk = heads(k * k_k)
    kk = kk / jnp.maximum(jnp.sqrt(jnp.sum(kk * kk, axis=-1, keepdims=True)), 1e-12)
    k = k * (1.0 + (a - 1.0) * k_a)
    rh, kh, vh = heads(r), heads(k), heads(v)
    y, s_new = rwkv7_scan(s0.astype(F32), rh, heads(decay), kh, vh, kk, heads(a))
    mean = jnp.mean(y, axis=-1, keepdims=True)
    var = jnp.mean(jnp.square(y - mean), axis=-1, keepdims=True)
    y = ((y - mean) * lax.rsqrt(var + A_GN_EPS)).reshape(bsz, t, A_WIDTH) * lnx_w + lnx_b
    bonus = jnp.sum(rh * kh * r_k.reshape(A_HEADS, A_HEAD).astype(F32), axis=-1, keepdims=True) * vh
    o = (y + bonus.reshape(bsz, t, A_WIDTH)) * g
    return o.astype(z.dtype), shift_new, s_new

def rotate(x, pos):
    half = x.shape[-1] // 2
    inv = jnp.power(ROT_BASE, -jnp.linspace(0.0, 1.0, half, dtype=F32))
    ang = pos[:, None] * inv[None, :]
    cos = jnp.cos(ang)[None, :, None, :]
    sin = jnp.sin(ang)[None, :, None, :]
    x1, x2 = x[..., :half], x[..., half:]
    return jnp.concatenate([x1 * cos - x2 * sin, x1 * sin + x2 * cos], axis=-1)

def ret_chunk(r_state, q, k, v, log_g):
    length = q.shape[1]
    idx = jnp.arange(length, dtype=F32)
    diff = idx[:, None] - idx[None, :]
    dmask = jnp.where(diff >= 0, jnp.exp(log_g[:, None, None] * jnp.maximum(diff, 0.0)), 0.0)
    s = jnp.einsum('bqhd,bkhd->bhqk', q, k) * dmask
    inner = jnp.einsum('bhqk,bkhv->bqhv', s, v)
    q_dec = jnp.exp(log_g[None, :] * (idx[:, None] + 1.0))[None, :, :, None]
    cross = jnp.einsum('bqhd,bhdv->bqhv', q, r_state) * q_dec
    k_dec = jnp.exp(log_g[None, :] * (length - 1.0 - idx[:, None]))[None, :, :, None]
    r_new = (jnp.exp(log_g * length)[None, :, None, None] * r_state
             + jnp.einsum('bkhd,bkhv->bhdv', k * k_dec, v))
    return r_new, inner + cross

def retention(r0, q, k, v, log_g):
    bsz, t = q.shape[0], q.shape[1]
    c = RET_CHUNK if t % RET_CHUNK == 0 else t
    n = t // c

    def to_chunks(u):
        return jnp.moveaxis(u.reshape(bsz, n, c, u.shape[2], u.shape[3]), 1, 0)

    r_final, o = lax.scan(lambda rs, xs: ret_chunk(rs, xs[0], xs[1], xs[2], log_g), r0,
                          (to_chunks(q), to_chunks(k), to_chunks(v)))
    o = jnp.moveaxis(o, 0, 1).reshape(bsz, t, B_HEADS, B_V_HEAD)
    return o, r_final

def retention_branch(q, k, v, gate, r0, pos):
    bsz, t, _ = q.shape
    log_g = jnp.log(1.0 - jnp.power(2.0, -5.0 - jnp.arange(B_HEADS, dtype=F32)))
    qh = rotate(q.reshape(bsz, t, B_HEADS, B_QK_HEAD).astype(F32), pos)
    kh = rotate(k.reshape(bsz, t, B_HEADS, B_QK_HEAD).astype(F32), pos) * (B_QK_HEAD ** -0.5)
    vh = v.reshape(bsz, t, B_HEADS, B_V_HEAD).astype(F32)
    o, r_new = retention(r0.astype(F32), qh, kh, vh, log_g)
    o = o * lax.rsqrt(jnp.mean(o * o, axis=-1, keepdims=True) + NORM_EPS)
    o = jax.nn.silu(gate.astype(F32)) * o.reshape(bsz, t, B_V_WIDTH)
    return o.astype(q.dtype), r_new

def peer(x, peer_wq, peer_keys, peer_u, peer_v):
    t, d = x.shape
    nb = -(-t // PEER_BLOCK)
    xp = jnp.pad(x, ((0, nb * PEER_BLOCK - t), (0, 0))).reshape(nb, PEER_BLOCK, d)

    def block(xb):
        q = (xb @ peer_wq).reshape(PEER_BLOCK, PEER_HEADS, 2, PEER_QDIM // 2)
        s = jnp.einsum('bhpd,hpnd->bhpn', q, peer_keys).astype(F32)
        sv, si = lax.top_k(s, PEER_TOPK)
        cand = sv[:, :, 0, :, None] + sv[:, :, 1, None, :]
        sc, flat = lax.top_k(cand.reshape(PEER_BLOCK, PEER_HEADS, PEER_TOPK * PEER_TOPK), PEER_TOPK)
        i1 = jnp.take_along_axis(si[:, :, 0], flat // PEER_TOPK, axis=-1)
        i2 = jnp.take_along_axis(si[:, :, 1], flat % PEER_TOPK, axis=-1)
        e = i1 * N_KEYS + i2
        gate = jax.nn.softmax(sc, axis=-1)
        h = jax.nn.gelu(jnp.einsum('bhkd,bd->bhk', peer_u[e], xb).astype(F32), approximate=False)
        return jnp.einsum('bhk,bhkd->bd', (gate * h).astype(xb.dtype), peer_v[e])

    return lax.map(block, xp).reshape(nb * PEER_BLOCK, d)[:t]

def decoder_layer(x, shift0, wkv0, ret0, pos, norm1, w_in, mu_shift, w0, w_w2, a0, w_a2, w_g2,
                  k_k, k_a, r_k, lnx_w, lnx_b, w_pa, w_pb, w_out, norm2, peer_wq, peer_keys,
                  peer_u, peer_v):
    bsz, t, d = x.shape
    hn = rmsnorm(x, norm1)
    z_a, q_b, k_b, v_b, g_b, g_merge = jnp.split(hn @ w_in, IN_SPLITS, axis=-1)
    o_a, shift_new, wkv_new = rwkv7_branch(z_a, shift0, wkv0, mu_shift, w0, w_w2, a0, w_a2, w_g2,
                                           k_k, k_a, r_k, lnx_w, lnx_b)
    o_b, ret_new = retention_branch(q_b, k_b, v_b, g_b, ret0, pos)
    gate_a, gate_b = jnp.split(jax.nn.sigmoid(g_merge), 2, axis=-1)
    x = x + (gate_a * (o_a @ w_pa) + gate_b * (o_b @ w_pb)) @ w_out
    x = x + peer(rmsnorm(x, norm2).reshape(bsz * t, d), peer_wq, peer_keys, peer_u, peer_v).reshape(bsz, t, d)
    return x, shift_new, wkv_new, ret_new

def trunk(x, shift0, wkv0, ret0, pos, weights, norm_f):
    shifts, wkvs, rets = [], [], []
    for layer in range(DEPTH):
        lw = [w[layer] for w in weights]
        x, s_new, wkv_new, ret_new = decoder_layer(x, shift0[layer], wkv0[layer], ret0[layer], pos, *lw)
        shifts.append(s_new.astype(shift0.dtype))
        wkvs.append(wkv_new.astype(wkv0.dtype))
        rets.append(ret_new.astype(ret0.dtype))
    return rmsnorm(x, norm_f), jnp.stack(shifts), jnp.stack(wkvs), jnp.stack(rets)

def setup_inputs(seed: int = 0) -> dict:
    key = jax.random.key(seed)
    ks = jax.random.split(key, 32)

    def nrm(k, shape, scale):
        return jax.random.normal(k, shape, F32) * scale

    L = DEPTH
    return {
        'x_prompt': nrm(ks[0], (BATCH, SEQ, D_MODEL), 1.0),
        'x_sample': nrm(ks[1], (DEC_BATCH, DEC_SEQ, D_MODEL), 1.0),
        'state_shift': nrm(ks[2], (L, DEC_BATCH, SHIFT_W), 1.0),
        'state_wkv': nrm(ks[3], (L, DEC_BATCH, A_HEADS, A_HEAD, A_HEAD), 0.3),
        'state_ret': nrm(ks[4], (L, DEC_BATCH, B_HEADS, B_QK_HEAD, B_V_HEAD), 0.3),
        'norm1': 1.0 + nrm(ks[5], (L, D_MODEL), 0.02),
        'w_in': nrm(ks[6], (L, D_MODEL, IN_W), D_MODEL ** -0.5),
        'mu_shift': jax.random.uniform(ks[7], (L, SHIFT_W), F32),
        'w0': jax.random.uniform(ks[8], (L, A_WIDTH), F32, -4.0, 1.0),
        'w_w2': nrm(ks[9], (L, A_DECAY_LORA, A_WIDTH), 0.1 * A_DECAY_LORA ** -0.5),
        'a0': nrm(ks[10], (L, A_WIDTH), 0.1),
        'w_a2': nrm(ks[11], (L, A_ICL_LORA, A_WIDTH), 0.1 * A_ICL_LORA ** -0.5),
        'w_g2': nrm(ks[12], (L, A_GATE_LORA, A_WIDTH), A_GATE_LORA ** -0.5),
        'k_k': 0.85 + nrm(ks[13], (L, A_WIDTH), 0.05),
        'k_a': 1.0 + nrm(ks[14], (L, A_WIDTH), 0.05),
        'r_k': nrm(ks[15], (L, A_WIDTH), 0.1),
        'lnx_w': 1.0 + nrm(ks[16], (L, A_WIDTH), 0.02),
        'lnx_b': nrm(ks[17], (L, A_WIDTH), 0.02),
        'w_pa': nrm(ks[18], (L, A_WIDTH, D_MODEL), A_WIDTH ** -0.5),
        'w_pb': nrm(ks[19], (L, B_V_WIDTH, D_MODEL), B_V_WIDTH ** -0.5),
        'w_out': nrm(ks[20], (L, D_MODEL, D_MODEL), D_MODEL ** -0.5),
        'norm2': 1.0 + nrm(ks[21], (L, D_MODEL), 0.02),
        'peer_wq': nrm(ks[22], (L, D_MODEL, PEER_HEADS * PEER_QDIM), D_MODEL ** -0.5),
        'peer_keys': nrm(ks[23], (L, PEER_HEADS, 2, N_KEYS, PEER_QDIM // 2), (PEER_QDIM // 2) ** -0.5),
        'peer_u': nrm(ks[24], (L, N_EXPERTS, D_MODEL), D_MODEL ** -0.5),
        'peer_v': nrm(ks[25], (L, N_EXPERTS, D_MODEL), PEER_HEADS ** -0.5),
        'norm_f': 1.0 + nrm(ks[26], (D_MODEL,), 0.02),
    }

def reference(x_prompt, x_sample, state_shift, state_wkv, state_ret, norm1, w_in, mu_shift, w0,
              w_w2, a0, w_a2, w_g2, k_k, k_a, r_k, lnx_w, lnx_b, w_pa, w_pb, w_out, norm2,
              peer_wq, peer_keys, peer_u, peer_v, norm_f):
    weights = (norm1, w_in, mu_shift, w0, w_w2, a0, w_a2, w_g2, k_k, k_a, r_k, lnx_w, lnx_b,
               w_pa, w_pb, w_out, norm2, peer_wq, peer_keys, peer_u, peer_v)
    bp, tp = x_prompt.shape[0], x_prompt.shape[1]
    ts = x_sample.shape[1]
    shift0 = jnp.zeros((DEPTH, bp, SHIFT_W), x_prompt.dtype)
    wkv0 = jnp.zeros((DEPTH, bp, A_HEADS, A_HEAD, A_HEAD), x_prompt.dtype)
    ret0 = jnp.zeros((DEPTH, bp, B_HEADS, B_QK_HEAD, B_V_HEAD), x_prompt.dtype)
    pos_p = jnp.arange(tp, dtype=F32)
    y_prompt, shift_p, wkv_p, ret_p = trunk(x_prompt, shift0, wkv0, ret0, pos_p, weights, norm_f)
    pos_s = PAST_LEN + jnp.arange(ts, dtype=F32)
    y_sample, shift_s, wkv_s, ret_s = trunk(x_sample, state_shift, state_wkv, state_ret, pos_s,
                                            weights, norm_f)
    return (y_prompt, y_sample, shift_p, wkv_p, ret_p, shift_s, wkv_s, ret_s)


_drawn_inputs = setup_inputs


def setup_inputs(seed=0):
    import zlib

    import numpy as np

    out = dict(_drawn_inputs(seed))
    spreads = {}
    factors = {'w_w2': 6.602, 'lnx_w': 10.471, 'lnx_b': 10.995, 'norm_f': 24.264, 'norm2': 9.109}
    for name, (base, spread) in spreads.items():
        noise = np.random.default_rng([zlib.crc32(name.encode()), seed]).standard_normal(out[name].shape)
        drawn = base * np.exp(spread * noise) if base else spread * noise
        out[name] = jnp.asarray(drawn.astype(out[name].dtype))
    for name, factor in factors.items():
        out[name] = (out[name] * factor).astype(out[name].dtype)
    return out
```

```python
from contextlib import ExitStack
import numpy as np
import concourse.bass as bass
from concourse import mybir

F32 = mybir.dt.float32
F32R = mybir.dt.float32r
U32 = mybir.dt.uint32
ALU = mybir.AluOpType
ACT = mybir.ActivationFunctionType
AX = mybir.AxisListType

P = 128
D = 2048
DC = D // P
TP = 512
NSEQ, LSEQ = 8, 8
TS = NSEQ * LSEQ
T = TP + TS
HT = T // 2
HEAD = 64
PAIRS = 8
C = 64
NCH = T // C
GRP = 3
PAST = 4096
PH = 8
NK = 128
TOPK = 16
NTT = -(-T // P)
LEAST = -3.0e38
TC = 48
LORA = 288
HB = 8
RC = 128
NRC = TP // RC
VH = 256
ROWS = 128
RET_CON = T + RC + TS + 3 + NSEQ
DECAY = float(np.exp(-0.5))
EPS = 1e-6
GN_EPS = 64e-5


class Steps:

    def __init__(self, sem, names):
        self.sem, self.names, self.n = sem, {x: k + 1 for k, x in enumerate(names)}, len(names)
        self.told = 0

    def ahead(self, eng):
        eng.sem_inc(self.sem, self.n)

    def of(self, i, name, back=0):
        return (i + (1 - back)) * self.n + self.names[name]

    def last(self, i, names):
        return (i + 1) * self.n + max(self.names[x] for x in names)

    def step(self, name):
        assert self.names[name] == self.told % self.n + 1, (name, self.told)
        self.told += 1
        return self.sem


def halves(ap):
    return ap.rearrange("p (a b) -> p a b", a=2)


def project(pe, out, weight, act, k=DC):
    for c in range(k):
        for h in range(2):
            last = pe.matmul(out[:, h, :], weight[:, c, :], act[:, c, h * HT:(h + 1) * HT],
                             start=(c == 0), stop=(c == k - 1))
    return last


def project3(pe, out, wh, wl, ah, al, k=DC):
    for c in range(k):
        for h in range(2):
            t = slice(h * HT, (h + 1) * HT)
            pe.matmul(out[:, h, :], wh[:, c, :], ah[:, c, t], start=(c == 0), stop=False)
            pe.matmul(out[:, h, :], wh[:, c, :], al[:, c, t], start=False, stop=False)
        for h in range(2):
            t = slice(h * HT, (h + 1) * HT)
            last = pe.matmul(out[:, h, :], wl[:, c, :], ah[:, c, t], start=False, stop=(c == k - 1))
    return last


def norm_stage(nc, K, tag, src, dst, gain, load=None, store=None, parts=None):
    with ExitStack() as ctx:
        ld = ctx.enter_context(nc.semaphore(tag + "_loaded"))
        sq = ctx.enter_context(nc.semaphore(tag + "_squared"))
        ss = ctx.enter_context(nc.semaphore(tag + "_summed"))
        ms = ctx.enter_context(nc.semaphore(tag + "_mean"))
        rs = ctx.enter_context(nc.semaphore(tag + "_rstd"))
        dn = ctx.enter_context(nc.semaphore(tag + "_normed"))
        st = ctx.enter_context(nc.semaphore(tag + "_stored"))
        hi = ctx.enter_context(nc.semaphore(tag + "_high"))
        rstd = ctx.enter_context(nc.sbuf_tensor(tag + "_r", [P, T], F32))
        pz = K.ps[:, 0:2, 0:HT]
        block = ctx.enter_context(nc.Block())

        @block.sync
        def _(sp):
            if load is not None:
                for q in range(4):
                    sp.dma_start(src[:, 4 * q:4 * q + 4, :], load[:, 4 * q:4 * q + 4, :]).then_inc(ld, 16)
            if store is not None:
                for q in range(4):
                    sp.wait_ge(dn, 4 * q + 4)
                    sp.dma_start(store[:, 4 * q:4 * q + 4, :], dst[:, 4 * q:4 * q + 4, :]).then_inc(st, 16)
                sp.wait_ge(st, 64)

        @block.scalar
        def _(act):
            for c in range(DC):
                if load is not None:
                    act.wait_ge(ld, 64)
                act.activation(dst[:, c, :], src[:, c, :], ACT.Square).then_inc(sq, 1)
            act.wait_ge(ms, 1)
            act.activation(rstd[:, :], rstd[:, :], ACT.Ln)
            act.drain()
            act.activation(rstd[:, :], rstd[:, :], ACT.Exp, scale=-0.5).then_inc(rs, 1)
            for c in range(DC if parts else 0):
                act.wait_ge(dn, c + 1)
                act.copy(parts[0][:, c, :], dst[:, c, :]).then_inc(hi, 1)

        @block.tensor
        def _(pe):
            for c in range(DC):
                pe.wait_ge(sq, c + 1)
                for h in range(2):
                    last = pe.matmul(pz[:, h, :], K.ones[:, :], dst[:, c, h * HT:(h + 1) * HT],
                                     start=(c == 0), stop=(c == DC - 1))
            last.then_inc(ss, 1)

        @block.vector
        def _(dve):
            dve.wait_ge(ss, 1)
            dve.tensor_scalar(halves(rstd[:, :]), pz, 1.0 / D, EPS, ALU.mult, ALU.add).then_inc(ms, 1)
            dve.wait_ge(rs, 1)
            for c in range(DC):
                dve.scalar_tensor_tensor(out=dst[:, c, :], in0=src[:, c, :], scalar=gain[:, c:c + 1],
                                         in1=rstd[:, :], op0=ALU.mult, op1=ALU.mult).then_inc(dn, 1)
            for c in range(DC if parts else 0):
                dve.wait_ge(hi, c + 1)
                dve.tensor_tensor(parts[1][:, c, :], dst[:, c, :], parts[0][:, c, :].bitcast(F32), ALU.subtract)


def inverse_plan():
    return [
        ("f2", "F", "f", "A", "G", None),
        ("F2", "f", "F", "B", None, None),
        ("f4", "B", "A", "E", None, None),
        ("F4", "A", "B", "H", "J", None),
        ("D1", "G", "IF", "L", None, None),
        ("f8", "H", "E", None, "A", None),
        ("D2", "J", "A", "B", None, None),
        ("D", "L", "B", "G", None, None),
        ("DT", "B", "L", "E", None, None),
        ("e", "E", "o", "H", None, None),
        ("eT", "o", "E", "A", None, "J"),
        ("e2", "H", "A", None, "L", None),
        ("h", "L", "G", "B", None, None),
        ("Z", "J", "B", "Z", None, None),
    ]


def rwkv_stage(nc, K, a):
    with ExitStack() as ctx:
        def sb(name, shape):
            return ctx.enter_context(nc.sbuf_tensor("rwkv_" + name, shape, F32))

        def sem(name):
            return ctx.enter_context(nc.semaphore("rwkv_" + name))

        ring = sb("weights", [P, 3, DC, P])
        lora_w = ring[:, :, :, :].rearrange("p a b c -> p (a b c)")[:, 0:DC * LORA]\
            .rearrange("p (c n) -> p c n", c=DC)
        low2 = sb("low2", [P, 2 * P])
        low3 = sb("low3", [32, P])
        s0 = sb("s0", [P, NSEQ, HEAD])
        par = sb("par", [P, PAIRS, 10])
        lmu = sb("lmu", [P, 3])
        shin = sb("shin", [P, PAIRS * 3 + 3, NSEQ])
        shout = sb("shout", [P, PAIRS * 3 + 3, 1 + NSEQ])
        one0 = sb("one0", [P, T])
        mask = sb("mask", [P, 2, 4, P])
        moff = sb("moff", [P, P])
        mlow = sb("mlow", [P, 2, P])
        mseq = sb("mseq", [P, NSEQ])
        blk = sb("blk", [P, P])
        sel = sb("sel", [P, C])
        zx = sb("zx", [P, 2, 1 + TP + NSEQ * (LSEQ + 1)])
        dif = sb("dif", [P, T])
        rs, ks, vs = sb("rs", [P, T]), sb("ks", [P, T]), sb("vs", [P, T])
        lo0, lo1, lo2 = sb("lo0", [P, T]), sb("lo1", [P, T]), sb("lo2", [32, T])
        kk, ksq, cs, cse = sb("kk", [P, T]), sb("ksq", [P, T]), sb("cs", [P, T]), sb("cse", [P, T])
        sg, at, winc, gg = sb("sg", [P, T]), sb("at", [P, T]), sb("winc", [P, T]), sb("gg", [P, T])
        kf, bb, rk = sb("kf", [P, T]), sb("bb", [P, T]), sg
        pads = {x: sb("pad_" + x, [P, NCH, P]) for x in "pqbkv"}
        xm = sb("xm", [P, NCH, 4, P])
        off = sb("off", [P, NCH, P])
        low = sb("low", [P, NCH, P])
        ilow = sb("ilow", [P, GRP, P])
        tok = sb("tok", [P, NCH, 320])
        zz = sb("zz", [P, NCH, P])
        mats = {x: sb("m" + x, [P, GRP, P]) for x in "ABEGHJL"}
        st = sb("st", [P, 2, HEAD])
        rn, uu = sb("rn", [P, HEAD]), sb("uu", [P, HEAD])
        yy = sb("yy", [P, NCH, HEAD])
        big = um = cs[:, 0:NSEQ * HEAD].rearrange("p (b v) -> p b v", b=NSEQ)
        vm = cse[:, 0:NSEQ * HEAD].rearrange("p (b v) -> p b v", b=NSEQ)
        r1, y1 = sb("r1", [P, HEAD]), sb("y1", [P, HEAD])
        so = sb("so", [P, NSEQ, HEAD])
        gm, gv = sb("gm", [P, NCH]), sb("gv", [P, NCH])
        ypad = pads["b"]
        oo = sb("oo", [P, T])
        ident = K.ident

        groups = [range(g * GRP, (g + 1) * GRP) for g in range(NCH // GRP)]
        plan = inverse_plan()
        inv = [f"{g}_{x[0]}" for g in range(len(groups)) for x in plan]
        chain = [f"{x}{c}" for c in range(NCH - 1) for x in "RUSY"]
        pe_s = Steps(sem("tensor"), ["r", "k", "v", "w", "a", "g", "ss", "bon"]
                     + [f"{x}{c}" for c in range(NCH) for x in "xt"] + inv + chain
                     + ["sR", "s8", "sY", "sU", "sV", "sS", "yT"])
        v_s = Steps(sem("vector"), ["sh_r", "sh_k", "ksq", "sh_v", "cse", "max", "rp", "b", "pq"]
                    + [f"{x}{c}" for c in range(NCH) for x in ("mx", "mt")]
                    + [y for g in range(len(groups))
                       for y in [f"il{g}"] + [f"{g}_{x[0]}" for x in plan if x[4] or x[5]]]
                    + [f"{x}{c}" for c in range(NCH - 1) for x in ("R", "U", "S")]
                    + ["sR", "s8", "sY", "sU", "sUm", "sV", "sS", "var", "ypad", "oa"])
        a_s = Steps(sem("scalar"), ["ev_r", "ev_k", "ev_v", "sg", "at", "gg", "rkk", "exp"]
                    + [f"tv{c}" for c in range(NCH)]
                    + [f"{g}_{x[0]}" for g in range(len(groups)) for x in plan if x[3]]
                    + [f"Y{c}" for c in range(NCH - 1)] + ["rstd"])
        p_s = Steps(sem("pool"), ["in_r", "in_k", "out_r", "in_v", "out_k", "out_v", "bp", "kp", "vp"])
        consts = sem("consts")
        lw = sem("lora_weights")
        wt = [sem("tile_" + x) for x in "rkv"]
        small = sem("small_weights")
        stored = sem("stored")
        shst = sem("shift_stored")
        lz = sem("lora_projected")
        lin = sem("lora_shift_in")
        lev = sem("lora_evacuated")
        lsh = sem("lora_shifted")
        ldn = sem("lora_done")
        lout = sem("lora_shift_out")
        padz = sem("pads_zeroed")
        Z = [K.ps[:, 0:2, 0:HT], K.ps[:, 2:4, 0:HT]]
        X = [K.ps[:, 4 + b, :] for b in range(4)]

        def views(z, n=P):
            s = z[0:n, 1 + TP:].rearrange("p (b l) -> p b l", b=NSEQ)
            return z[0:n, 1:1 + TP], z[0:n, 0:TP], s[:, :, 1:], s[:, :, 0:LSEQ]

        def evacuate(act, z, src, n=P):
            cur, _, scur, _ = views(z, n)
            act.copy(cur[:, 0:HT], src[0:n, 0, :])
            act.copy(cur[:, HT:TP], src[0:n, 1, 0:TP - HT])
            return act.copy(scur, src[0:n, 1, TP - HT:HT].rearrange("p (b l) -> p b l", b=NSEQ))

        def shift(dve, z, mu, out, n=P):
            cur, prev, scur, sprev = views(z, n)
            dve.tensor_tensor(dif[0:n, 0:TP], prev, cur, ALU.subtract)
            dve.tensor_tensor(dif[0:n, TP:T].rearrange("p (b l) -> p b l", b=NSEQ), sprev, scur, ALU.subtract)
            dve.drain()
            dve.scalar_tensor_tensor(out=out[0:n, 0:TP], in0=dif[0:n, 0:TP], scalar=mu, in1=cur,
                                     op0=ALU.mult, op1=ALU.add)
            last = dve.scalar_tensor_tensor(
                out=out[0:n, TP:T].rearrange("p (b l) -> p b l", b=NSEQ),
                in0=dif[0:n, TP:T].rearrange("p (b l) -> p b l", b=NSEQ), scalar=mu, in1=scur,
                op0=ALU.mult, op1=ALU.add)
            return last

        def last_rows(pool, z, t, n=P):
            s = z[0:n, 1 + TP:].rearrange("p (b l) -> p b l", b=NSEQ)
            pool.tensor_copy(shout[0:n, t, 0:1], z[0:n, TP:TP + 1])
            return pool.tensor_copy(shout[0:n, t, 1:1 + NSEQ], s[:, :, LSEQ])

        def first_rows(pool, z, t, n=P):
            s = z[0:n, 1 + TP:].rearrange("p (b l) -> p b l", b=NSEQ)
            return pool.tensor_copy(s[:, :, 0], shin[0:n, t, :])

        block = ctx.enter_context(nc.Block())

        @block.sync
        def _(sp):
            sp.dma_start(lora_w, a["w_lora"]).then_inc(lw, 16)
            for dst, src in ((par, "w_par"), (lmu, "lora_mu"), (shin, "shift_in"), (one0, "c_one0"),
                             (mask, "c_mask"), (moff, "c_moff"), (mlow, "c_mlow"), (mseq, "c_mseq"),
                             (blk, "c_blk"), (sel, "c_sel")):
                sp.dma_start(dst[:], a[src]).then_inc(consts, 16)
            sp.wait_ge(lz, 3)
            with sp.Fori(0, PAIRS) as i:
                for t, x in enumerate("rkv"):
                    sp.wait_ge(pe_s.sem, pe_s.of(i, x, 1))
                    sp.dma_start(ring[:, t, :, :], a["w_rkv"][i, t]).then_inc(wt[t], 16)
                sp.wait_ge(pe_s.sem, pe_s.of(i, "g", 1))
                sp.dma_start(low2[:, :], a["w_low2"][i]).then_inc(small, 16)
                sp.dma_start(low3[:, :], a["w_low3"][i]).then_inc(small, 16)
                sp.wait_ge(pe_s.sem, pe_s.of(i, "sS", 1))
                sp.dma_start(s0[:, :, :], a["wkv_in"][i]).then_inc(small, 16)

        @block.gpsimd
        def _(pool):
            p_s.ahead(pool)
            for x in "pqbkv":
                pool.memset(pads[x][:, :, :], 0.0)
            pool.memset(off[:, NCH - 1, :], 0.0)
            pool.memset(zx[:, :, 0:1], 0.0)
            pool.memset(shout[:, :, :], 0.0)
            pool.drain().then_inc(padz, 1)
            pool.wait_ge(consts, 160)
            for t, n in ((0, P), (1, P), (2, 32)):
                if t == 2:
                    pool.wait_ge(lsh, 1)
                first_rows(pool, zx[:, t % 2, :], PAIRS * 3 + t, n).then_inc(lin, 1)
                pool.drain()
                if t == 1:
                    pool.wait_ge(lev, 1)
                    last_rows(pool, zx[:, 0, :], PAIRS * 3, P).then_inc(lout, 1)
            for t, n in ((1, P), (2, 32)):
                pool.wait_ge(lev, t + 1)
                last_rows(pool, zx[:, t % 2, :], PAIRS * 3 + t, n).then_inc(lout, 1)
                pool.drain()
            with pool.Fori(0, PAIRS) as i:
                def rows_in(x, slot, t):
                    first_rows(pool, zx[:, slot, :], 3 * i + t).then_inc(p_s.step("in_" + x), 1)
                    pool.drain()

                def rows_out(x, slot, t):
                    pool.wait_ge(a_s.sem, a_s.of(i, "ev_" + x))
                    last_rows(pool, zx[:, slot, :], 3 * i + t).then_inc(p_s.step("out_" + x), 1)
                    pool.drain()

                pool.wait_ge(lsh, 3)
                pool.wait_ge(v_s.sem, v_s.of(i, "sh_v", 1))
                rows_in("r", 0, 0)
                rows_in("k", 1, 1)
                rows_out("r", 0, 0)
                pool.wait_ge(v_s.sem, v_s.of(i, "sh_r"))
                rows_in("v", 0, 2)
                rows_out("k", 1, 1)
                rows_out("v", 0, 2)

                def pad(x, p0, p1):
                    for h in range(2):
                        r = slice(HEAD * h, HEAD * h + HEAD)
                        o = pads[x][r, :, C * h:C * h + C]
                        u = p0[r, :].rearrange("p (c t) -> p c t", c=NCH)
                        if p1 is None:
                            last = pool.tensor_copy(o, u)
                        else:
                            last = pool.tensor_tensor(o, u, p1[r, :].rearrange("p (c t) -> p c t", c=NCH), ALU.mult)
                        if h == 0:
                            pool.drain()
                    return last

                pool.wait_ge(pe_s.sem, pe_s.of(i, "yT", 1))
                pool.wait_ge(a_s.sem, a_s.of(i, "exp"))
                pool.wait_ge(v_s.sem, v_s.of(i, "b"))
                pad("b", bb, cs).then_inc(p_s.step("bp"), 1)
                pool.drain()
                pad("k", kf, cs).then_inc(p_s.step("kp"), 1)
                pool.drain()
                pad("v", vs, None).then_inc(p_s.step("vp"), 1)
                pool.drain()

        @block.scalar
        def _(act):
            a_s.ahead(act)
            act.sem_inc(stored, 48)
            for t, n in ((0, P), (1, P), (2, 32)):
                act.wait_ge(lz, t + 1)
                act.wait_ge(padz, 1)
                if t == 2:
                    act.wait_ge(lsh, 1)
                    act.wait_ge(lout, 1)
                evacuate(act, zx[:, t % 2, :], Z[t % 2], n).then_inc(lev, 1)
            act.wait_ge(lsh, 3)
            act.activation(lo0[0:64, :], lo0[0:64, :], ACT.Tanh)
            act.activation(lo1[:, :], lo1[:, :], ACT.Sigmoid)
            act.activation(lo2[:, :], lo2[:, :], ACT.Sigmoid).then_inc(ldn, 1)
            with act.Fori(0, PAIRS) as i:
                for x, z, slot in (("r", 0, 0), ("k", 1, 1), ("v", 0, 0)):
                    act.wait_ge(pe_s.sem, pe_s.of(i, x))
                    if x == "v":
                        act.wait_ge(v_s.sem, v_s.of(i, "sh_r"))
                        act.wait_ge(p_s.sem, p_s.of(i, "out_r"))
                    else:
                        act.wait_ge(v_s.sem, v_s.of(i, "sh_v", 1))
                        act.wait_ge(p_s.sem, p_s.of(i, "out_v", 1))
                        act.wait_ge(lout, 3)
                    evacuate(act, zx[:, slot, :], Z[z]).then_inc(a_s.step("ev_" + x), 1)
                act.wait_ge(pe_s.sem, pe_s.of(i, "w"))
                act.wait_ge(v_s.sem, v_s.of(i, "oa", 1))
                act.activation(halves(sg[:, :]), Z[1], ACT.Sigmoid, bias=par[:, i, 3:4]).then_inc(a_s.step("sg"), 1)
                act.wait_ge(pe_s.sem, pe_s.of(i, "a"))
                act.activation(halves(at[:, :]), Z[0], ACT.Sigmoid, bias=par[:, i, 4:5]).then_inc(a_s.step("at"), 1)
                act.wait_ge(pe_s.sem, pe_s.of(i, "g"))
                act.copy(halves(gg[:, :]), Z[1]).then_inc(a_s.step("gg"), 1)
                act.wait_ge(v_s.sem, v_s.of(i, "max"))
                act.activation(rk[:, :], rk[:, :], ACT.Ln, scale=float(2 ** 30))
                act.drain()
                act.activation(rk[:, :], rk[:, :], ACT.Exp, scale=-0.5, bias=K.half30[:, 0:1]).then_inc(a_s.step("rkk"), 1)
                act.activation(winc[:, :], cs[:, :], ACT.Exp, scale=-DECAY)
                act.activation(cse[:, :], cse[:, :], ACT.Exp, scale=-DECAY)
                act.drain()
                act.activation(cs[:, :], cs[:, :], ACT.Exp, scale=DECAY).then_inc(a_s.step("exp"), 1)
                for c in range(NCH):
                    act.wait_ge(v_s.sem, v_s.of(i, f"mt{c}"))
                    act.copy(tok[:, c, :], X[2 + c % 2][:, P:P + 320]).then_inc(a_s.step(f"tv{c}"), 1)
                for g, cc in enumerate(groups):
                    for n, (name, _, _, to, _, _) in enumerate(plan):
                        if to:
                            act.wait_ge(pe_s.sem, pe_s.of(i, f"{g}_{name}"))
                            dst = zz[:, cc[0]:cc[-1] + 1, :] if to == "Z" else mats[to][:, :, :]
                            src = X[(g * len(plan) + n) % 4][:, 0:GRP * P].rearrange("p (a b) -> p a b", a=GRP)
                            act.copy(dst, src).then_inc(a_s.step(f"{g}_{name}"), 1)
                for c in range(NCH - 1):
                    act.wait_ge(pe_s.sem, pe_s.of(i, f"Y{c}"))
                    act.copy(yy[:, c, :], X[2][:, 0:HEAD]).then_inc(a_s.step(f"Y{c}"), 1)
                act.wait_ge(v_s.sem, v_s.of(i, "var"))
                act.activation(gv[:, :], gv[:, :], ACT.Ln)
                act.drain()
                act.activation(gv[:, :], gv[:, :], ACT.Exp, scale=-0.5).then_inc(a_s.step("rstd"), 1)
                act.wait_ge(v_s.sem, v_s.of(i, "oa"))
                act.dma_start(K.oa[i], oo[:, :]).then_inc(stored, 16)
                act.dma_start(a["wkv_out"][i, :, 0, :], st[:, 0, :]).then_inc(stored, 16)
                act.dma_start(a["wkv_out"][i, :, 1:1 + NSEQ, :], so[:, :, :]).then_inc(stored, 16)
            act.wait_ge(p_s.sem, p_s.of(PAIRS - 1, "out_v"))
            act.dma_start(a["shift_out"], shout[:, :, :]).then_inc(shst, 16)
            act.wait_ge(shst, 16)
            act.wait_ge(stored, 48 * PAIRS + 48)

        @block.tensor
        def _(pe):
            pe_s.ahead(pe)
            pe.wait_ge(lw, 16)
            for t, n in ((0, P), (1, P), (2, 32)):
                if t == 2:
                    pe.wait_ge(lev, 1)
                for c in range(DC):
                    for h in range(2):
                        last = pe.matmul(Z[t % 2][0:n, h, :], lora_w[:, c, P * t:P * t + n],
                                         K.hn[:, c, h * HT:(h + 1) * HT], start=(c == 0), stop=(c == DC - 1))
                last.then_inc(lz, 1)
            pe.wait_ge(lev, 3)
            pe.wait_ge(ldn, 1)
            pe.wait_ge(consts, 160)
            with pe.Fori(0, PAIRS) as i:
                for t, (x, z) in enumerate((("r", 0), ("k", 1), ("v", 0))):
                    pe.wait_ge(wt[t], 16 * i + 16)
                    if x == "r":
                        pe.wait_ge(v_s.sem, v_s.of(i, "oa", 1))
                    if x == "v":
                        pe.wait_ge(a_s.sem, a_s.of(i, "ev_r"))
                    project(pe, Z[z], ring[:, t, :, :], K.hn).then_inc(pe_s.step(x), 1)
                pe.wait_ge(small, 48 * i + 48)
                for x, z, ev in (("w", 1, "ev_k"), ("a", 0, "ev_v"), ("g", 1, "sg")):
                    pe.wait_ge(a_s.sem, a_s.of(i, ev))
                    for h in range(2):
                        tt = slice(h * HT, (h + 1) * HT)
                        if x == "w":
                            last = pe.matmul(Z[z][:, h, :], low2[0:64, 0:P], lo0[0:64, tt], start=True, stop=True)
                        elif x == "a":
                            last = pe.matmul(Z[z][:, h, :], low2[64:P, 0:P], lo0[64:P, tt], start=True, stop=True)
                        else:
                            pe.matmul(Z[z][:, h, :], low2[:, P:2 * P], lo1[:, tt], start=True, stop=False)
                            last = pe.matmul(Z[z][:, h, :], low3[:, :], lo2[:, tt], start=False, stop=True)
                    last.then_inc(pe_s.step(x), 1)
                for x, z, ev, src, after in (("ss", 0, "at", ksq, "ksq"), ("bon", 1, "gg", dif, "rp")):
                    pe.wait_ge(a_s.sem, a_s.of(i, ev))
                    pe.wait_ge(v_s.sem, v_s.of(i, after))
                    for h in range(2):
                        last = pe.matmul(Z[z][:, h, :], blk[:, :], src[:, h * HT:(h + 1) * HT], start=True, stop=True)
                    last.then_inc(pe_s.step(x), 1)
                pe.wait_ge(v_s.sem, v_s.of(i, "pq"))
                pe.wait_ge(p_s.sem, p_s.of(i, "vp"))
                for c in range(NCH):
                    pq = {x: pads[x][:, c, :] for x in "pqbkv"}
                    x = X[c % 2]
                    if c >= 2:
                        pe.wait_ge(v_s.sem, v_s.of(i, f"mx{c - 2}"))
                    for n, (l, r) in enumerate(("bp", "kp", "bq", "kq")):
                        last = pe.matmul(x[:, P * n:P * n + P], pq[l], pq[r], start=True, stop=True)
                    last.then_inc(pe_s.step(f"x{c}"), 1)
                    x = X[2 + c % 2]
                    if c >= 2:
                        pe.wait_ge(v_s.sem, v_s.of(i, f"mt{c - 2}"))
                        pe.wait_ge(a_s.sem, a_s.of(i, f"tv{c - 2}"))
                    pe.matmul(x[:, 0:P], pq["p"], pq["b"], start=True, stop=True)
                    pe.matmul(x[:, P:P + C], pq["v"], sel[:, :], start=True, stop=True)
                    pe.transpose(x[:, P + C:2 * P + C], pq["b"], ident[:, :])
                    pe.transpose(x[:, 2 * P + C:3 * P + C], pq["k"], ident[:, :])\
                        .then_inc(pe_s.step(f"t{c}"), 1)
                def out_of_bank(n):
                    g, (name, _, _, to, _, _) = n // len(plan), plan[n % len(plan)]
                    return ([f"{g}_{name}"], []) if to else ([], [f"{g}_{name}"])

                for g, cc in enumerate(groups):
                    for n, (name, l, r, _, _, _) in enumerate(plan):
                        at_bank = g * len(plan) + n
                        by_act, by_dve = out_of_bank(at_bank - 4) if at_bank >= 4 else ([], [])
                        for m in (l, r):
                            by = [k for k in range(n) if m in plan[k][3:6]]
                            if by and m == plan[by[-1]][3]:
                                by_act = by_act + [f"{g}_{plan[by[-1]][0]}"]
                            elif by:
                                by_dve = by_dve + [f"{g}_{plan[by[-1]][0]}"]
                        if n == 0:
                            by_dve = by_dve + [f"il{g}"]
                        if at_bank == 0:
                            by_act = by_act + [f"tv{NCH - 1}"]
                        if by_act:
                            pe.wait_ge(a_s.sem, a_s.last(i, by_act))
                        if by_dve:
                            pe.wait_ge(v_s.sem, v_s.last(i, by_dve))
                        for k, c in enumerate(cc):
                            given = {"f": xm[:, c, 0, :], "F": low[:, c, :], "IF": ilow[:, k, :], "o": off[:, c, :]}
                            ml, mr = (given[m] if m in given else mats[m][:, k, :] for m in (l, r))
                            last = pe.matmul(X[at_bank % 4][:, P * k:P * k + P], ml, mr, start=True, stop=True)
                        last.then_inc(pe_s.step(f"{g}_{name}"), 1)
                freed = [out_of_bank(len(groups) * len(plan) - 1 - n) for n in range(4)]
                pe.wait_ge(a_s.sem, a_s.last(i, sum((x for x, _ in freed), [])))
                pe.wait_ge(v_s.sem, v_s.last(i, sum((x for _, x in freed), [])))

                for c in range(NCH - 1):
                    s = st[:, c % 2, :]
                    v, b, k = tok[:, c, 0:C], tok[:, c, C:C + P], tok[:, c, C + P:C + 2 * P]
                    if c:
                        pe.wait_ge(v_s.sem, v_s.of(i, f"S{c - 1}"))
                        pe.matmul(X[0][:, 0:HEAD], pads["p"][:, c, :], s, start=True, stop=False)
                    pe.matmul(X[0][:, 0:HEAD], xm[:, c, 1, :], v, start=(c == 0), stop=True)\
                        .then_inc(pe_s.step(f"R{c}"), 1)
                    pe.wait_ge(v_s.sem, v_s.of(i, f"R{c}"))
                    pe.matmul(X[1][:, 0:HEAD], zz[:, c, :], rn[:, :], start=True, stop=True)\
                        .then_inc(pe_s.step(f"U{c}"), 1)
                    pe.wait_ge(v_s.sem, v_s.of(i, f"U{c}"))
                    if c:
                        pe.matmul(X[3][:, 0:HEAD], ident[:, :], s, start=True, stop=False)
                    pe.matmul(X[3][:, 0:HEAD], b, uu[:, :], start=(c == 0), stop=False)
                    pe.matmul(X[3][:, 0:HEAD], k, v, start=False, stop=True).then_inc(pe_s.step(f"S{c}"), 1)
                    if c:
                        pe.wait_ge(a_s.sem, a_s.of(i, f"Y{c - 1}"))
                        pe.matmul(X[2][:, 0:HEAD], pads["q"][:, c, :], s, start=True, stop=False)
                    pe.matmul(X[2][:, 0:HEAD], xm[:, c, 2, :], uu[:, :], start=(c == 0), stop=False)
                    pe.matmul(X[2][:, 0:HEAD], xm[:, c, 3, :], v, start=False, stop=True)\
                        .then_inc(pe_s.step(f"Y{c}"), 1)

                c = NCH - 1
                v, b, k = tok[:, c, 0:C], tok[:, c, C:C + P], tok[:, c, C + P:C + 2 * P]
                flat = s0[:, :, :].rearrange("p b v -> p (b v)")
                pe.matmul(X[0], pads["p"][:, c, :], flat, start=True, stop=True).then_inc(pe_s.step("sR"), 1)
                pe.matmul(X[1][:, 0:HEAD], xm[:, c, 1, :], v, start=True, stop=True).then_inc(pe_s.step("s8"), 1)
                pe.wait_ge(a_s.sem, a_s.of(i, f"Y{NCH - 2}"))
                pe.matmul(X[2], pads["q"][:, c, :], flat, start=True, stop=True).then_inc(pe_s.step("sY"), 1)
                pe.wait_ge(v_s.sem, v_s.of(i, "s8"))
                pe.matmul(X[3][:, 0:HEAD], zz[:, c, :], rn[:, :], start=True, stop=True)\
                    .then_inc(pe_s.step("sU"), 1)
                pe.wait_ge(v_s.sem, v_s.of(i, "sU"))
                pe.matmul(X[1][:, 0:HEAD], xm[:, c, 2, :], uu[:, :], start=True, stop=False)
                pe.matmul(X[1][:, 0:HEAD], xm[:, c, 3, :], v, start=False, stop=True)\
                    .then_inc(pe_s.step("sV"), 1)
                pe.wait_ge(v_s.sem, v_s.of(i, "sUm"))
                pe.matmul(X[0], ident[:, :], flat, start=True, stop=False)
                pe.matmul(X[0], b, cs[:, 0:NSEQ * HEAD], start=False, stop=False)
                pe.matmul(X[0], k, cse[:, 0:NSEQ * HEAD], start=False, stop=True)\
                    .then_inc(pe_s.step("sS"), 1)
                pe.wait_ge(v_s.sem, v_s.of(i, "ypad"))
                for c in range(NCH):
                    o = K.ps[:, c // 5, C * (c % 5):C * (c % 5) + C]
                    last = pe.matmul(o, ypad[:, c, :], sel[:, :], start=True, stop=True)
                last.then_inc(pe_s.step("yT"), 1)

        @block.vector
        def _(dve):
            v_s.ahead(dve)
            dve.wait_ge(consts, 160)
            for t, (n, out) in enumerate(((P, lo0), (P, lo1), (32, lo2))):
                dve.wait_ge(lev, t + 1)
                dve.wait_ge(lin, t + 1)
                shift(dve, zx[:, t % 2, :], lmu[0:n, t:t + 1], out, n).then_inc(lsh, 1)
                dve.drain()
            dve.wait_ge(padz, 1)
            with dve.Fori(0, PAIRS) as i:
                def mul_pads(x, p0, p1):
                    for h in range(2):
                        r = slice(HEAD * h, HEAD * h + HEAD)
                        last = dve.tensor_tensor(pads[x][r, :, C * h:C * h + C],
                                                 p0[r, :].rearrange("p (c t) -> p c t", c=NCH),
                                                 p1[r, :].rearrange("p (c t) -> p c t", c=NCH), ALU.mult)
                    return last

                def shifted(x, slot, mu, out):
                    dve.wait_ge(a_s.sem, a_s.of(i, "ev_" + x))
                    dve.wait_ge(p_s.sem, p_s.of(i, "in_" + x))
                    shift(dve, zx[:, slot, :], par[:, i, mu:mu + 1], out).then_inc(v_s.step("sh_" + x), 1)
                    dve.drain()

                shifted("r", 0, 0, rs)
                shifted("k", 1, 1, ks)
                dve.tensor_scalar(kk[:, :], ks[:, :], par[:, i, 5:6], None, ALU.mult)
                dve.drain()
                dve.tensor_tensor(ksq[:, :], kk[:, :], kk[:, :], ALU.mult).then_inc(v_s.step("ksq"), 1)
                dve.drain()
                shifted("v", 0, 2, vs)
                dve.wait_ge(a_s.sem, a_s.of(i, "sg"))
                dve.tensor_tensor_scan(cs[:, :], one0[:, :], sg[:, :], 0.0, ALU.mult, ALU.add)
                dve.drain()
                dve.tensor_tensor(cse[:, :], cs[:, :], sg[:, :], ALU.subtract).then_inc(v_s.step("cse"), 1)
                dve.drain()
                dve.wait_ge(pe_s.sem, pe_s.of(i, "ss"))
                dve.tensor_scalar(halves(rk[:, :]), Z[0], 1e-24, None, ALU.max).then_inc(v_s.step("max"), 1)
                dve.drain()
                dve.wait_ge(a_s.sem, a_s.of(i, "at"))
                dve.tensor_scalar(bb[:, :], at[:, :], 1.0, par[:, i, 6:7], ALU.subtract, ALU.mult)
                dve.drain()
                dve.scalar_tensor_tensor(out=kf[:, :], in0=bb[:, :], scalar=1.0, in1=ks[:, :],
                                         op0=ALU.add, op1=ALU.mult)
                dve.drain()
                dve.scalar_tensor_tensor(out=dif[:, :], in0=rs[:, :], scalar=par[:, i, 7:8], in1=kf[:, :],
                                         op0=ALU.mult, op1=ALU.mult).then_inc(v_s.step("rp"), 1)
                dve.drain()
                dve.wait_ge(a_s.sem, a_s.of(i, "rkk"))
                dve.tensor_tensor(kk[:, :], kk[:, :], rk[:, :], ALU.mult)
                dve.drain()
                dve.tensor_tensor(bb[:, :], kk[:, :], at[:, :], ALU.mult).then_inc(v_s.step("b"), 1)
                dve.drain()
                dve.wait_ge(a_s.sem, a_s.of(i, "exp"))
                mul_pads("p", kk, cse)
                mul_pads("q", rs, winc).then_inc(v_s.step("pq"), 1)
                dve.drain()
                for c in range(NCH):
                    kind = c // (NCH - 1)
                    dve.wait_ge(pe_s.sem, pe_s.of(i, f"x{c}"))
                    if kind == 0:
                        dve.tensor_tensor(off[:, c, :], X[c % 2][:, 0:P], moff[:, :], ALU.mult)
                    dve.tensor_tensor(xm[:, c, :, :], X[c % 2].rearrange("p (a b) -> p a b", a=4),
                                      mask[:, kind, :, :], ALU.mult).then_inc(v_s.step(f"mx{c}"), 1)
                    dve.drain()
                    dve.wait_ge(pe_s.sem, pe_s.of(i, f"t{c}"))
                    dve.tensor_tensor(low[:, c, :], X[2 + c % 2][:, 0:P], mlow[:, kind, :], ALU.mult)\
                        .then_inc(v_s.step(f"mt{c}"), 1)
                dve.drain()
                eye = ident[:, :].unsqueeze(1)
                for g, cc in enumerate(groups):
                    dve.scalar_tensor_tensor(out=ilow[:, :, :], in0=low[:, cc[0]:cc[-1] + 1, :], scalar=-1.0,
                                             in1=eye.broadcast_to([P, GRP, P]), op0=ALU.mult, op1=ALU.add)\
                        .then_inc(v_s.step(f"il{g}"), 1)
                    dve.drain()
                    for n, (name, _, _, to, plus, minus) in enumerate(plan):
                        if plus or minus:
                            src = X[(g * len(plan) + n) % 4][:, 0:GRP * P].rearrange("p (a b) -> p a b", a=GRP)
                            if to:
                                src = mats[to][:, :, :]
                                dve.wait_ge(a_s.sem, a_s.of(i, f"{g}_{name}"))
                            else:
                                dve.wait_ge(pe_s.sem, pe_s.of(i, f"{g}_{name}"))
                            dve.scalar_tensor_tensor(out=mats[plus or minus][:, :, :], in0=src,
                                                     scalar=1.0 if plus else -1.0,
                                                     in1=eye.broadcast_to([P, GRP, P]), op0=ALU.mult, op1=ALU.add)\
                                                         .then_inc(v_s.step(f"{g}_{name}"), 1)
                            dve.drain()
                dve.wait_ge(stored, 48 * i + 48)
                for c in range(NCH - 1):
                    dve.wait_ge(pe_s.sem, pe_s.of(i, f"R{c}"))
                    dve.tensor_scalar(rn[:, :], X[0][:, 0:HEAD], -1.0, None, ALU.mult).then_inc(v_s.step(f"R{c}"), 1)
                    dve.drain()
                    dve.wait_ge(pe_s.sem, pe_s.of(i, f"U{c}"))
                    dve.tensor_copy(uu[:, :], X[1][:, 0:HEAD]).then_inc(v_s.step(f"U{c}"), 1)
                    dve.drain()
                    dve.wait_ge(pe_s.sem, pe_s.of(i, f"S{c}"))
                    end = C * c + C - 1
                    dve.tensor_scalar(st[:, (c + 1) % 2, :], X[3][:, 0:HEAD], winc[:, end:end + 1], None, ALU.mult)\
                        .then_inc(v_s.step(f"S{c}"), 1)
                    dve.drain()
                seq = mseq[:, :].unsqueeze(2).broadcast_to([P, NSEQ, HEAD])

                def own_rows(bank, out):
                    dve.tensor_tensor(big[:, :, :], bank.rearrange("p (b v) -> p b v", b=NSEQ), seq, ALU.mult)
                    dve.drain()
                    return dve.tensor_reduce(out[:, :], big[:, :, :].rearrange("p b v -> p v b"), AX.X, ALU.add)

                dve.wait_ge(pe_s.sem, pe_s.of(i, "sR"))
                own_rows(X[0], r1).then_inc(v_s.step("sR"), 1)
                dve.drain()
                dve.wait_ge(pe_s.sem, pe_s.of(i, "s8"))
                dve.scalar_tensor_tensor(out=rn[:, :], in0=X[1][:, 0:HEAD], scalar=-1.0, in1=r1[:, :],
                                         op0=ALU.mult, op1=ALU.subtract).then_inc(v_s.step("s8"), 1)
                dve.drain()
                dve.wait_ge(pe_s.sem, pe_s.of(i, "sY"))
                own_rows(X[2], y1).then_inc(v_s.step("sY"), 1)
                dve.drain()
                dve.wait_ge(pe_s.sem, pe_s.of(i, "sU"))
                dve.tensor_copy(uu[:, :], X[3][:, 0:HEAD]).then_inc(v_s.step("sU"), 1)
                dve.drain()
                for dst, src in ((um, uu[:, :]), (vm, tok[:, NCH - 1, 0:C])):
                    last = dve.tensor_tensor(dst[:, :, :], src.unsqueeze(1).broadcast_to([P, NSEQ, HEAD]), seq, ALU.mult)
                last.then_inc(v_s.step("sUm"), 1)
                dve.drain()
                dve.wait_ge(pe_s.sem, pe_s.of(i, "sV"))
                dve.tensor_tensor(yy[:, NCH - 1, :], X[1][:, 0:HEAD], y1[:, :], ALU.add).then_inc(v_s.step("sV"), 1)
                dve.drain()
                dve.wait_ge(pe_s.sem, pe_s.of(i, "sS"))
                last_w = winc[:, TP + LSEQ - 1:T:LSEQ].unsqueeze(2).broadcast_to([P, NSEQ, HEAD])
                dve.tensor_tensor(so[:, :, :], X[0].rearrange("p (b v) -> p b v", b=NSEQ), last_w, ALU.mult)\
                    .then_inc(v_s.step("sS"), 1)
                dve.drain()
                dve.wait_ge(a_s.sem, a_s.of(i, f"Y{NCH - 2}"))
                dve.tensor_reduce(gm[:, :], yy[:, :, :], AX.X, ALU.add)
                dve.drain()
                dve.tensor_scalar(gm[:, :], gm[:, :], 1.0 / HEAD, None, ALU.mult)
                dve.drain()
                gmb = gm[:, :].unsqueeze(2).broadcast_to([P, NCH, HEAD])
                dve.tensor_tensor(yy[:, :, :], yy[:, :, :], gmb, ALU.subtract)
                dve.drain()
                y2 = dif[:, :].rearrange("p (c v) -> p c v", c=NCH)
                dve.tensor_tensor(y2, yy[:, :, :], yy[:, :, :], ALU.mult)
                dve.drain()
                dve.tensor_reduce(gv[:, :], y2, AX.X, ALU.add)
                dve.drain()
                dve.tensor_scalar(gv[:, :], gv[:, :], 1.0 / HEAD, GN_EPS, ALU.mult, ALU.add).then_inc(v_s.step("var"), 1)
                dve.drain()
                dve.wait_ge(a_s.sem, a_s.of(i, "rstd"))
                for h in range(2):
                    r = slice(HEAD * h, HEAD * h + HEAD)
                    last = dve.tensor_tensor(ypad[r, :, HEAD * h:HEAD * h + HEAD], yy[r, :, :],
                                             gv[r, :].unsqueeze(2).broadcast_to([HEAD, NCH, HEAD]), ALU.mult)
                last.then_inc(v_s.step("ypad"), 1)
                dve.drain()
                dve.tensor_tensor(halves(ksq[:, :]), Z[1], halves(vs[:, :]), ALU.mult)
                dve.wait_ge(pe_s.sem, pe_s.of(i, "yT"))
                for b, lo, hi in ((0, 0, 5 * C), (1, 5 * C, T)):
                    dve.tensor_scalar(kk[:, lo:hi], K.ps[:, b, 0:hi - lo], par[:, i, 8:9], par[:, i, 9:10],
                                      ALU.mult, ALU.add)
                dve.drain()
                dve.tensor_tensor(kk[:, :], kk[:, :], ksq[:, :], ALU.add)
                dve.drain()
                dve.tensor_tensor(oo[:, :], kk[:, :], gg[:, :], ALU.mult).then_inc(v_s.step("oa"), 1)
                dve.drain()


def ret_stage(nc, K, a):
    with ExitStack() as ctx:
        def sb(name, shape):
            return ctx.enter_context(nc.sbuf_tensor("ret_" + name, shape, F32))

        def sem(name):
            return ctx.enter_context(nc.semaphore("ret_" + name))

        w4 = sb("w4", [P, 4, DC, P])
        wv = sb("wv", [P, DC, VH])
        con = sb("con", [P, RET_CON])
        cos, sin, perm = sb("cos", [P, T]), sb("sin", [P, T]), sb("perm", [P, P])
        qr, kr, tmp = sb("qr", [P, T]), sb("kr", [P, T]), sb("tmp", [P, T])
        qt, kt, qd = sb("qt", [P, T]), sb("kt", [P, T]), sb("qd", [P, T])
        vt = sb("vt", [P, NRC + 1, VH])
        sm = sb("sm", [P, NRC + 1, RC])
        kd = sb("kd", [P, NRC, P])
        kds = sb("kds", [TS, NSEQ, P])
        rst = sb("rst", [P, 2, VH])
        r0, rout = sb("r0", [P, NSEQ, VH]), sb("rout", [P, NSEQ, VH])
        ot, o2, gate, ob = (sb(x, [P, 2, T]) for x in ("ot", "o2", "gate", "ob"))
        rstd = sb("rstd", [P, T])
        qdec, dm, dms = con[:, 0:T], con[:, T:T + RC], con[0:TS, T + RC:T + RC + TS]
        o = T + RC + TS
        kdec, gc, gs, kdecs = con[:, o:o + 1], con[:, o + 1:o + 2], con[:, o + 2:o + 3], con[0:TS, o + 3:o + 3 + NSEQ]
        NT = NRC + 1
        pe_s = Steps(sem("tensor"), ["q", "k"] + [f"v{c}" for c in range(NT)] + ["swq", "swk", "g0", "g1"]
                     + [f"s{c}" for c in range(NT)] + [x for c in range(NRC) for x in (f"o{c}", f"R{c}")]
                     + [f"o{NRC}"] + [f"RS{p}" for p in range(4)] + ["ss"])
        v_s = Steps(sem("vector"), ["q", "k"] + [f"s{c}" for c in range(NT)] + [f"R{c}" for c in range(NRC)]
                    + [f"RS{p}" for p in range(4)] + ["ms", "ob"])
        a_s = Steps(sem("scalar"), ["q", "k"] + [f"v{c}" for c in range(NT)] + ["g0", "g1"]
                    + [f"o{c}" for c in range(NT)] + ["sq", "rstd"])
        wts = [sem("w_" + x) for x in ("q", "k", "g0", "g1")]
        wvs, cons, consts, r0s, stored = sem("w_v"), sem("head_consts"), sem("consts"), sem("state_in"), sem("stored")
        Z = [K.ps[:, 0:2, 0:HT], K.ps[:, 2:4, 0:HT]]
        X = [K.ps[:, 4 + b, :] for b in range(4)]

        def chunk(c):
            return slice(RC * c, RC * c + (RC if c < NRC else TS))

        block = ctx.enter_context(nc.Block())

        @block.sync
        def _(sp):
            for dst, src in ((cos, "c_cos"), (sin, "c_sin"), (perm, "c_perm")):
                sp.dma_start(dst[:, :], a[src]).then_inc(consts, 16)
            with sp.Fori(0, HB) as i:
                for t, x in enumerate(("q", "k", "g0", "g1")):
                    if x == "g0":
                        sp.wait_ge(pe_s.sem, pe_s.of(i, f"v{NRC}", 1))
                        sp.dma_start(wv[:, :, :], a["w_v"][i]).then_inc(wvs, 16)
                    sp.wait_ge(pe_s.sem, pe_s.of(i, x, 1))
                    sp.dma_start(w4[:, t, :, :], a["w_qkg"][i, t]).then_inc(wts[t], 16)
                sp.wait_ge(v_s.sem, v_s.of(i, "ms", 1))
                sp.dma_start(con[:, :], a["c_ret"][i]).then_inc(cons, 16)
                sp.dma_start(r0[:, :, :], a["ret_in"][i]).then_inc(r0s, 16)

        @block.tensor
        def _(pe):
            pe_s.ahead(pe)
            pe.wait_ge(consts, 48)
            with pe.Fori(0, HB) as i:
                def matrix(x, z):
                    t = ("q", "k", "g0", "g1").index(x)
                    pe.wait_ge(wts[t], 16 * i + 16)
                    project(pe, Z[z], w4[:, t, :, :], K.hn).then_inc(pe_s.step(x), 1)

                pe.wait_ge(v_s.sem, v_s.of(i, "ms", 1))
                matrix("q", 0)
                matrix("k", 1)
                pe.wait_ge(wvs, 16 * i + 16)
                for c in range(NT):
                    if c >= 2:
                        pe.wait_ge(a_s.sem, a_s.of(i, f"v{c - 2}"))
                    n = RC if c < NRC else TS
                    for d in range(DC):
                        last = pe.matmul(X[c % 2][0:n, 0:VH], K.hn[:, d, chunk(c)], wv[:, d, :],
                                         start=(d == 0), stop=(d == DC - 1))
                    last.then_inc(pe_s.step(f"v{c}"), 1)
                for x, z, src in (("q", 0, qr), ("k", 1, kr)):
                    pe.wait_ge(a_s.sem, a_s.of(i, x))
                    for h in range(2):
                        last = pe.matmul(Z[z][:, h, :], perm[:, :], src[:, h * HT:(h + 1) * HT], start=True, stop=True)
                    last.then_inc(pe_s.step("sw" + x), 1)
                pe.wait_ge(v_s.sem, v_s.of(i, "q"))
                matrix("g0", 0)
                pe.wait_ge(v_s.sem, v_s.of(i, "k"))
                matrix("g1", 1)
                for c in range(NT):
                    if c >= 2:
                        pe.wait_ge(v_s.sem, v_s.of(i, f"s{c - 2}"))
                    n = RC if c < NRC else TS
                    pe.matmul(X[2 + c % 2][0:n, 0:n], kt[:, chunk(c)], qt[:, chunk(c)], start=True, stop=True)
                    pe.transpose(X[2 + c % 2][0:n, RC:RC + P], kt[:, chunk(c)], K.ident[:, :])\
                        .then_inc(pe_s.step(f"s{c}"), 1)
                for c in range(NRC):
                    pe.wait_ge(v_s.sem, v_s.of(i, f"R{c - 1}" if c else f"s{NRC}"))
                    pe.wait_ge(a_s.sem, a_s.of(i, f"o{c - 1}" if c else f"v{NRC}"))
                    for h in range(2):
                        y = X[0][:, RC * h:RC * h + RC]
                        last = pe.matmul(y, vt[:, c, P * h:P * h + P], sm[:, c, :], start=True, stop=(c == 0))
                        if c:
                            last = pe.matmul(y, rst[:, c % 2, P * h:P * h + P], qd[:, chunk(c)], start=False, stop=True)
                    last.then_inc(pe_s.step(f"o{c}"), 1)
                    pe.matmul(X[1][:, 0:VH], kd[:, c, :], vt[:, c, :], start=True, stop=True)\
                        .then_inc(pe_s.step(f"R{c}"), 1)
                pe.wait_ge(a_s.sem, a_s.of(i, f"o{NRC - 1}"))
                pe.wait_ge(r0s, 16 * i + 16)
                for h in range(2):
                    y = X[0][:, TS * h:TS * h + TS]
                    pe.matmul(y, vt[0:TS, NRC, P * h:P * h + P], sm[0:TS, NRC, 0:TS], start=True, stop=False)
                    for b in range(NSEQ):
                        q = slice(TP + LSEQ * b, TP + LSEQ * b + LSEQ)
                        last = pe.matmul(y[:, LSEQ * b:LSEQ * b + LSEQ], r0[:, b, P * h:P * h + P], qd[:, q],
                                         start=False, stop=(b == NSEQ - 1))
                last.then_inc(pe_s.step(f"o{NRC}"), 1)
                for p in range(4):
                    pe.wait_ge(v_s.sem, v_s.of(i, f"R{NRC - 1}" if p < 3 else "RS0"))
                    for b in (2 * p, 2 * p + 1):
                        last = pe.matmul(X[1 + p % 3][:, VH * (b % 2):VH * (b % 2) + VH], kds[:, b, :],
                                         vt[0:TS, NRC, :], start=True, stop=True)
                    last.then_inc(pe_s.step(f"RS{p}"), 1)
                pe.wait_ge(a_s.sem, a_s.of(i, "sq"))
                for h in range(2):
                    for k in range(2):
                        last = pe.matmul(Z[0][:, h, :], K.ones[:, :], o2[:, k, h * HT:(h + 1) * HT],
                                         start=(k == 0), stop=(k == 1))
                last.then_inc(pe_s.step("ss"), 1)

        @block.scalar
        def _(act):
            a_s.ahead(act)
            act.sem_inc(stored, 48)
            with act.Fori(0, HB) as i:
                act.wait_ge(pe_s.sem, pe_s.of(i, "q"))
                act.copy(halves(qr[:, :]), Z[0]).then_inc(a_s.step("q"), 1)
                act.wait_ge(pe_s.sem, pe_s.of(i, "k"))
                act.activation(halves(kr[:, :]), Z[1], ACT.Copy, scale=float(P) ** -0.5).then_inc(a_s.step("k"), 1)
                for c in range(NT):
                    n = RC if c < NRC else TS
                    act.wait_ge(pe_s.sem, pe_s.of(i, f"v{c}"))
                    act.copy(vt[0:n, c, :], X[c % 2][0:n, 0:VH]).then_inc(a_s.step(f"v{c}"), 1)
                for h in range(2):
                    act.wait_ge(pe_s.sem, pe_s.of(i, f"g{h}"))
                    if h == 0:
                        act.wait_ge(v_s.sem, v_s.of(i, "ob", 1))
                    act.activation(halves(gate[:, h, :]), Z[h], ACT.Silu).then_inc(a_s.step(f"g{h}"), 1)
                for c in range(NT):
                    n = RC if c < NRC else TS
                    act.wait_ge(pe_s.sem, pe_s.of(i, f"o{c}"))
                    act.copy(ot[:, :, chunk(c)], X[0][:, 0:2 * n].rearrange("p (h t) -> p h t", h=2))\
                        .then_inc(a_s.step(f"o{c}"), 1)
                act.drain()
                act.activation(o2[:, :, :], ot[:, :, :], ACT.Square).then_inc(a_s.step("sq"), 1)
                act.wait_ge(v_s.sem, v_s.of(i, "ms"))
                act.activation(rstd[:, :], rstd[:, :], ACT.Ln)
                act.drain()
                act.activation(rstd[:, :], rstd[:, :], ACT.Exp, scale=-0.5).then_inc(a_s.step("rstd"), 1)
                act.wait_ge(v_s.sem, v_s.of(i, "ob"))
                act.dma_start(K.ob[i], ob[:, :, :]).then_inc(stored, 16)
                act.dma_start(a["ret_out"][i, :, 0, :], rst[:, NRC % 2, :]).then_inc(stored, 16)
                act.dma_start(a["ret_out"][i, :, 1:1 + NSEQ, :], rout[:, :, :]).then_inc(stored, 16)
            act.wait_ge(stored, 48 * HB + 48)

        @block.vector
        def _(dve):
            v_s.ahead(dve)
            dve.wait_ge(consts, 48)
            with dve.Fori(0, HB) as i:
                dve.wait_ge(cons, 16 * i + 16)
                for x, z, raw, out in (("q", 0, qr, qt), ("k", 1, kr, kt)):
                    dve.wait_ge(pe_s.sem, pe_s.of(i, "sw" + x))
                    dve.tensor_tensor(halves(tmp[:, :]), Z[z], halves(sin[:, :]), ALU.mult)
                    dve.tensor_tensor(out[:, :], raw[:, :], cos[:, :], ALU.mult)
                    dve.drain()
                    last = dve.tensor_tensor(out[:, :], out[:, :], tmp[:, :], ALU.add)
                    if x == "k":
                        last = dve.tensor_tensor(qd[:, :], qt[:, :], qdec, ALU.mult)
                    last.then_inc(v_s.step(x), 1)
                    dve.drain()
                for c in range(NT):
                    n = RC if c < NRC else TS
                    x = X[2 + c % 2]
                    dve.wait_ge(pe_s.sem, pe_s.of(i, f"s{c}"))
                    dve.tensor_tensor(sm[0:n, c, 0:n], x[0:n, 0:n], dm if c < NRC else dms, ALU.mult)
                    if c < NRC:
                        last = dve.tensor_scalar(kd[:, c, :], x[:, RC:RC + P], kdec, None, ALU.mult)
                    else:
                        last = dve.tensor_tensor(kds[:, :, :], x[0:n, RC:RC + P].unsqueeze(1).broadcast_to([TS, NSEQ, P]),
                                                 kdecs.unsqueeze(2).broadcast_to([TS, NSEQ, P]), ALU.mult)
                    last.then_inc(v_s.step(f"s{c}"), 1)
                dve.drain()
                dve.wait_ge(stored, 48 * i + 48)
                for c in range(NRC):
                    dve.wait_ge(pe_s.sem, pe_s.of(i, f"R{c}"))
                    if c == 0:
                        last = dve.tensor_copy(rst[:, 1, :], X[1][:, 0:VH])
                    else:
                        last = dve.scalar_tensor_tensor(out=rst[:, (c + 1) % 2, :], in0=rst[:, c % 2, :], scalar=gc,
                                                        in1=X[1][:, 0:VH], op0=ALU.mult, op1=ALU.add)
                    last.then_inc(v_s.step(f"R{c}"), 1)
                    dve.drain()
                for p in range(4):
                    dve.wait_ge(pe_s.sem, pe_s.of(i, f"RS{p}"))
                    dve.scalar_tensor_tensor(out=rout[:, 2 * p:2 * p + 2, :], in0=r0[:, 2 * p:2 * p + 2, :], scalar=gs,
                                             in1=X[1 + p % 3].rearrange("p (b v) -> p b v", b=2),
                                             op0=ALU.mult, op1=ALU.add).then_inc(v_s.step(f"RS{p}"), 1)
                dve.wait_ge(pe_s.sem, pe_s.of(i, "ss"))
                dve.tensor_scalar(halves(rstd[:, :]), Z[0], 1.0 / VH, EPS, ALU.mult, ALU.add)\
                    .then_inc(v_s.step("ms"), 1)
                dve.tensor_tensor(ob[:, :, :], ot[:, :, :], gate[:, :, :], ALU.mult)
                dve.drain()
                dve.wait_ge(a_s.sem, a_s.of(i, "rstd"))
                dve.tensor_tensor(ob[:, :, :], ob[:, :, :], rstd[:, :].unsqueeze(1).broadcast_to([P, 2, T]), ALU.mult)\
                    .then_inc(v_s.step("ob"), 1)
                dve.drain()


def merge_stage(nc, K, a, m):
    with ExitStack() as ctx:
        def sb(name, shape):
            return ctx.enter_context(nc.sbuf_tensor("mrg_" + name, shape, F32))

        def sem(name):
            return ctx.enter_context(nc.semaphore("mrg_" + name))

        oa, ob = sb("oa", [P, PAIRS, T]), sb("ob", [P, HB * 2, T])
        KT = {"ga": DC, "gb": DC, "pa": PAIRS, "pb": 2 * HB}
        acts = {"ga": K.hn, "gb": K.hn, "pa": oa, "pb": ob}
        w = {x: sb("w_" + x, [P, k, P]) for x, k in KT.items()}
        sa, s2 = sb("sa", [P, T]), sb("s2", [P, T])
        banks = {x: K.ps[:, 2 * n:2 * n + 2, 0:HT] for n, x in enumerate(KT)}
        pe_s = Steps(sem("tensor"), list(KT))
        v_s = Steps(sem("vector"), ["a", "m"])
        a_s = Steps(sem("scalar"), ["ga", "gb"])
        wt = {x: sem("w_" + x) for x in KT}
        loaded = sem("loaded")
        block = ctx.enter_context(nc.Block())

        @block.sync
        def _(sp):
            with sp.Fori(0, DC) as i:
                for x in KT:
                    sp.wait_ge(pe_s.sem, pe_s.of(i, x, 1))
                    sp.dma_start(w[x][:, :, :], a["w_" + x][i]).then_inc(wt[x], 16)

        @block.gpsimd
        def _(pool):
            pool.dma_start(oa[:, :, :], K.oa.rearrange("i p t -> p i t")).then_inc(loaded, 16)
            pool.dma_start(ob[:, :, :].rearrange("p (i h) t -> p i h t", h=2),
                           K.ob.rearrange("i p h t -> p i h t")).then_inc(loaded, 16)

        @block.tensor
        def _(pe):
            pe_s.ahead(pe)
            with pe.Fori(0, DC) as i:
                for x in KT:
                    pe.wait_ge(wt[x], 16 * i + 16)
                    if x in ("ga", "gb"):
                        pe.wait_ge(a_s.sem, a_s.of(i, x, 1))
                    else:
                        pe.wait_ge(loaded, 32)
                        pe.wait_ge(v_s.sem, v_s.of(i, "a" if x == "pa" else "m", 1))
                    project(pe, banks[x], w[x], acts[x], KT[x]).then_inc(pe_s.step(x), 1)

        @block.scalar
        def _(act):
            a_s.ahead(act)
            with act.Fori(0, DC) as i:
                for x, s in (("ga", sa), ("gb", s2)):
                    act.wait_ge(pe_s.sem, pe_s.of(i, x))
                    act.wait_ge(v_s.sem, v_s.of(i, "m", 1))
                    act.activation(halves(s[:, :]), banks[x], ACT.Sigmoid).then_inc(a_s.step(x), 1)

        @block.vector
        def _(dve):
            v_s.ahead(dve)
            with dve.Fori(0, DC) as i:
                for x, s, step in (("pa", sa, "a"), ("pb", s2, None)):
                    dve.wait_ge(pe_s.sem, pe_s.of(i, x))
                    dve.wait_ge(a_s.sem, a_s.of(i, "g" + x[1]))
                    last = dve.tensor_tensor(halves(s[:, :]), halves(s[:, :]), banks[x], ALU.mult)
                    if step:
                        last.then_inc(v_s.step(step), 1)
                    dve.drain()
                dve.tensor_tensor(m[:, i, :], sa[:, :], s2[:, :], ALU.add).then_inc(v_s.step("m"), 1)
                dve.drain()


def out_stage(nc, K, a, m, x1):
    with ExitStack() as ctx:
        def sem(name):
            return ctx.enter_context(nc.semaphore("out_" + name))

        w = ctx.enter_context(nc.sbuf_tensor("out_w", [P, 2, DC, P], F32))
        pe_s, v_s = Steps(sem("tensor"), ["0", "1"]), Steps(sem("vector"), ["0", "1"])
        wt, loaded = [sem("w0"), sem("w1")], sem("loaded")
        block = ctx.enter_context(nc.Block())

        @block.sync
        def _(sp):
            with sp.Fori(0, DC // 2) as i:
                for u in range(2):
                    sp.wait_ge(pe_s.sem, pe_s.of(i, str(u), 1))
                    sp.dma_start(w[:, u, :, :], a["w_out"][2 * i + u]).then_inc(wt[u], 16)

        @block.scalar
        def _(act):
            act.dma_start(x1[:, :, :], a["x"]).then_inc(loaded, 16)

        @block.tensor
        def _(pe):
            pe_s.ahead(pe)
            with pe.Fori(0, DC // 2) as i:
                for u in range(2):
                    pe.wait_ge(wt[u], 16 * i + 16)
                    pe.wait_ge(v_s.sem, v_s.of(i, str(u), 1))
                    project(pe, K.ps[:, 2 * u:2 * u + 2, 0:HT], w[:, u, :, :], m).then_inc(pe_s.step(str(u)), 1)

        @block.vector
        def _(dve):
            v_s.ahead(dve)
            dve.wait_ge(loaded, 16)
            with dve.Fori(0, DC // 2) as i:
                for u in range(2):
                    dve.wait_ge(pe_s.sem, pe_s.of(i, str(u)))
                    x = halves(x1[:, 2 * i + u, :])
                    dve.tensor_tensor(x, x, K.ps[:, 2 * u:2 * u + 2, 0:HT], ALU.add).then_inc(v_s.step(str(u)), 1)


def route_stage(nc, K, a, top_v, top_i):
    with ExitStack() as ctx:
        def sb(name, shape, dt=F32):
            return ctx.enter_context(nc.sbuf_tensor("rt_" + name, shape, dt))

        def sem(name):
            return ctx.enter_context(nc.semaphore("rt_" + name))

        w = sb("w", [P, DC, P])
        wh, wl = sb("wh", [P, 2, DC, P], F32R), sb("wl", [P, 2, DC, P], F32R)
        keys = sb("keys", [P, 2 * PH, NK])
        qt = sb("qt", [P, 2, T])
        sc = sb("sc", [P, 2, NTT, NK])
        s2 = sb("s2", [P, NTT, NK])
        val, idx = sb("val", [P, NTT, TOPK]), sb("idx", [P, NTT, TOPK], U32)
        pe_s = Steps(sem("tensor"), ["q0", "q1", "s0", "s1"])
        a_s = Steps(sem("scalar"), ["w0", "w1", "q0", "q1", "s0", "s1"])
        v_s = Steps(sem("vector"), ["w0", "w1", "met0", "0", "met1", "1"])
        wt, loaded, zeroed = sem("w"), sem("keys_in"), sem("zeroed")
        block = ctx.enter_context(nc.Block())

        @block.sync
        def _(sp):
            sp.dma_start(keys[:, :, :], a["keys"]).then_inc(loaded, 16)
            with sp.Fori(0, PH) as i:
                for u in range(2):
                    sp.wait_ge(v_s.sem, v_s.of(i, "w1", 1) if u == 0 else v_s.of(i, "w0"))
                    sp.dma_start(w[:, :, :], a["w_q"][2 * i + u]).then_inc(wt, 16)

        @block.gpsimd
        def _(pool):
            pool.memset(sc[:, :, NTT - 1, :], 0.0).then_inc(zeroed, 1)

        @block.tensor
        def _(pe):
            pe_s.ahead(pe)
            pe.wait_ge(loaded, 16)
            with pe.Fori(0, PH) as i:
                for u in range(2):
                    pe.wait_ge(v_s.sem, v_s.of(i, f"w{u}"))
                    pe.wait_ge(a_s.sem, a_s.of(i, f"q{u}", 1))
                    project3(pe, K.ps[:, 2 * u:2 * u + 2, 0:HT], wh[:, u, :, :], wl[:, u, :, :], K.hh, K.hl).then_inc(pe_s.step(f"q{u}"), 1)
                for u in range(2):
                    pe.wait_ge(a_s.sem, a_s.last(i, [f"q{u}"]) if u else a_s.of(i, "q1"))
                    for n in range(NTT):
                        m = P if n < NTT - 1 else TS
                        last = pe.matmul(K.ps[0:m, 4 + 2 * u + n // 4, NK * (n % 4):NK * (n % 4) + NK],
                                         qt[:, u, P * n:P * n + m], keys[:, 2 * i + u, :], start=True, stop=True)
                    last.then_inc(pe_s.step(f"s{u}"), 1)

        @block.scalar
        def _(act):
            a_s.ahead(act)
            act.wait_ge(zeroed, 1)
            with act.Fori(0, PH) as i:
                for u in range(2):
                    act.wait_ge(wt, 32 * i + 16 * u + 16)
                    act.wait_ge(pe_s.sem, pe_s.of(i, f"q{u}", 1))
                    act.copy(wh[:, u, :, :], w[:, :, :]).then_inc(a_s.step(f"w{u}"), 1)
                for u in range(2):
                    act.wait_ge(pe_s.sem, pe_s.of(i, f"q{u}"))
                    act.copy(halves(qt[:, u, :]), K.ps[:, 2 * u:2 * u + 2, 0:HT]).then_inc(a_s.step(f"q{u}"), 1)
                for u in range(2):
                    act.wait_ge(pe_s.sem, pe_s.of(i, f"s{u}"))
                    act.wait_ge(v_s.sem, v_s.of(i, str(u), 1))
                    act.copy(sc[:, u, 0:4, :], K.ps[:, 4 + 2 * u, :].rearrange("p (n k) -> p n k", n=4))
                    act.copy(sc[0:TS, u, 4, :], K.ps[0:TS, 5 + 2 * u, 0:NK]).then_inc(a_s.step(f"s{u}"), 1)

        @block.vector
        def _(dve):
            v_s.ahead(dve)
            with dve.Fori(0, PH) as i:
                for u in range(2):
                    dve.wait_ge(a_s.sem, a_s.of(i, f"w{u}"))
                    dve.tensor_tensor(wl[:, u, :, :], w[:, :, :], wh[:, u, :, :].bitcast(F32), ALU.subtract)\
                        .then_inc(v_s.step(f"w{u}"), 1)
                for u in range(2):
                    dve.wait_ge(a_s.sem, a_s.of(i, f"s{u}"))
                    dve.sem_inc(v_s.step(f"met{u}"), 1)
                    for n in range(NTT):
                        dve.max(val[:, n, 0:8], sc[:, u, n, :])
                    dve.drain()
                    for n in range(NTT):
                        dve.max_index(idx[:, n, 0:8], val[:, n, 0:8], sc[:, u, n, :])
                        dve.match_replace(s2[:, n, :], val[:, n, 0:8], sc[:, u, n, :], LEAST)
                    dve.drain()
                    for n in range(NTT):
                        dve.max(val[:, n, 8:16], s2[:, n, :])
                    dve.drain()
                    for n in range(NTT):
                        dve.max_index(idx[:, n, 8:16], val[:, n, 8:16], s2[:, n, :])
                    dve.drain()
                    dve.tensor_copy(top_v[:, :, 2 * i + u, :], val[:, :, :])
                    dve.tensor_copy(top_i[:, :, 2 * i + u, :], idx[:, :, :]).then_inc(v_s.step(str(u)), 1)
                    dve.drain()


def pick_stage(nc, K, a, top_v, top_i, slots):
    with ExitStack() as ctx:
        def sb(name, shape, dt=F32):
            return ctx.enter_context(nc.sbuf_tensor("pk_" + name, shape, dt))

        def sem(name):
            return ctx.enter_context(nc.semaphore("pk_" + name))

        cand, cand2, eq = (sb(x, [P, PH, TOPK * TOPK]) for x in ("cand", "cand2", "eq"))
        flat, pos = sb("flat", [P, PH, TOPK], U32), sb("pos", [P, 2, PH, TOPK], U32)
        posf, best = sb("posf", [P, 2, PH, TOPK]), sb("best", [P, PH, TOPK])
        ids = sb("ids", [P, 3, PH, TOPK])
        total = sb("total", [P, PH])
        iota = sb("iota", [P, TOPK])
        pe_s, a_s = Steps(sem("tensor"), ["t"]), Steps(sem("scalar"), ["e", "t"])
        v_s = Steps(sem("vector"), ["d", "ids"])
        loaded = sem("iota_in")
        block = ctx.enter_context(nc.Block())

        @block.sync
        def _(sp):
            sp.dma_start(iota[:, :], a["c_iota"][:, 0:TOPK]).then_inc(loaded, 16)

        @block.vector
        def _(dve):
            v_s.ahead(dve)
            dve.wait_ge(loaded, 16)
            with dve.Fori(0, NTT) as i:
                dve.wait_ge(pe_s.sem, pe_s.of(i, "t", 1))
                dve.tensor_tensor(cand[:, :, :].rearrange("p h (x y) -> p h x y", x=TOPK),
                                  top_v[:, i, 0:2 * PH:2, :].unsqueeze(3).broadcast_to([P, PH, TOPK, TOPK]),
                                  top_v[:, i, 1:2 * PH:2, :].unsqueeze(2).broadcast_to([P, PH, TOPK, TOPK]), ALU.add)
                dve.drain()
                for h in range(PH):
                    dve.max(best[:, h, 0:8], cand[:, h, :])
                dve.drain()
                for h in range(PH):
                    dve.max_index(flat[:, h, 0:8], best[:, h, 0:8], cand[:, h, :])
                    dve.match_replace(cand2[:, h, :], best[:, h, 0:8], cand[:, h, :], LEAST)
                dve.drain()
                for h in range(PH):
                    dve.max(best[:, h, 8:16], cand2[:, h, :])
                dve.drain()
                for h in range(PH):
                    dve.max_index(flat[:, h, 8:16], best[:, h, 8:16], cand2[:, h, :])
                gate = ids[:, 2, :, :]
                dve.tensor_tensor(gate, best[:, :, :], best[:, :, 0:1].broadcast_to([P, PH, TOPK]), ALU.subtract)\
                    .then_inc(v_s.step("d"), 1)
                dve.drain()
                dve.tensor_scalar(pos[:, 0, :, :], flat[:, :, :], 4, None, ALU.logical_shift_right)
                dve.tensor_scalar(pos[:, 1, :, :], flat[:, :, :], 15, None, ALU.bitwise_and)
                dve.drain()
                dve.tensor_copy(posf[:, :, :, :], pos[:, :, :, :])
                dve.drain()
                for s in range(2):
                    e = eq[:, :, :].rearrange("p h (x y) -> p h x y", x=TOPK)
                    dve.tensor_tensor(e, posf[:, s, :, :].unsqueeze(3).broadcast_to([P, PH, TOPK, TOPK]),
                                      iota[:, :].unsqueeze(1).unsqueeze(1).broadcast_to([P, PH, TOPK, TOPK]),
                                      ALU.is_equal)
                    dve.drain()
                    dve.tensor_tensor(e, e, top_i[:, i, s:2 * PH:2, :].unsqueeze(2)
                                      .broadcast_to([P, PH, TOPK, TOPK]), ALU.mult)
                    dve.drain()
                    dve.tensor_reduce(ids[:, s, :, :], e, AX.X, ALU.add)
                    dve.drain()
                dve.wait_ge(a_s.sem, a_s.of(i, "e"))
                dve.tensor_reduce(total[:, :], gate, AX.X, ALU.add)
                dve.drain()
                dve.reciprocal(total[:, :], total[:, :])
                dve.drain()
                dve.tensor_tensor(gate, gate, total[:, :].unsqueeze(2).broadcast_to([P, PH, TOPK]), ALU.mult)\
                    .then_inc(v_s.step("ids"), 1)
                dve.drain()

        @block.scalar
        def _(act):
            a_s.ahead(act)
            with act.Fori(0, NTT) as i:
                act.wait_ge(v_s.sem, v_s.of(i, "d"))
                act.activation(ids[:, 2, :, :], ids[:, 2, :, :], ACT.Exp).then_inc(a_s.step("e"), 1)
                act.wait_ge(pe_s.sem, pe_s.of(i, "t"))
                act.copy(slots[:, :, bass.ds(P * i, P)], K.ps[:, 0, 0:3 * P].rearrange("p (s t) -> p s t", s=3))\
                    .then_inc(a_s.step("t"), 1)

        @block.tensor
        def _(pe):
            pe_s.ahead(pe)
            with pe.Fori(0, NTT) as i:
                pe.wait_ge(v_s.sem, v_s.of(i, "ids"))
                pe.wait_ge(a_s.sem, a_s.of(i, "t", 1))
                for s in range(3):
                    last = pe.transpose(K.ps[:, 0, P * s:P * s + P], ids[:, s, :, :].rearrange("p h k -> p (h k)"),
                                        K.ident[:, :])
                last.then_inc(pe_s.step("t"), 1)


def gates_stage(nc, K, a, slots):
    with ExitStack() as ctx:
        def sb(name, shape):
            return ctx.enter_context(nc.sbuf_tensor("gt_" + name, shape, F32))

        def sem(name):
            return ctx.enter_context(nc.semaphore("gt_" + name))

        iota = sb("iota", [P, P])
        rows, cols = sb("rows", [P, 16, P]), sb("cols", [P, 16, P])
        stage = sb("stage", [P, 2, ROWS, TC])
        Q = ["0", "1", "2", "3"]
        pe_s, a_s = Steps(sem("tensor"), Q), Steps(sem("scalar"), Q)
        v_s = Steps(sem("vector"), Q)
        loaded, stored = sem("iota_in"), [sem("stored0"), sem("stored1")]
        PER = TC // 16
        NST = T // TC // 2
        block = ctx.enter_context(nc.Block())

        @block.sync
        def _(sp):
            sp.dma_start(iota[:, :], a["c_iota"]).then_inc(loaded, 16)
            for b in range(2):
                sp.sem_inc(stored[b], 16)
            with sp.Fori(0, NST) as s:
                for b in range(2):
                    sp.wait_ge(a_s.sem, a_s.of((2 * s + b) * PER + PER - 1, "3"))
                    sp.dma_start(K.gates[:, 2 * s + b, :, :], stage[:, b, :, :]).then_inc(stored[b], 16)
            for b in range(2):
                sp.wait_ge(stored[b], 16 * NST + 16)

        def turns(eng, body):
            with eng.Fori(0, NST) as s:
                for b in range(2):
                    with eng.Fori(0, PER) as q:
                        body((2 * s + b) * PER + q, s, b, q)

        @block.vector
        def _(dve):
            v_s.ahead(dve)
            dve.wait_ge(loaded, 16)

            def body(i, s, b, q):
                for g in range(4):
                    dve.wait_ge(pe_s.sem, pe_s.of(i, Q[g], 1))
                    for t in range(4 * g, 4 * g + 4):
                        at = bass.ds(16 * i + t, 1)
                        dve.tensor_scalar(cols[:, t, :], iota[:, :], slots[:, 1, at], None, ALU.is_equal)
                        last = dve.tensor_scalar(rows[:, t, :], iota[:, :], slots[:, 0, at], slots[:, 2, at],
                                                 ALU.is_equal, ALU.mult)
                    last.then_inc(v_s.step(Q[g]), 1)
            turns(dve, body)

        @block.tensor
        def _(pe):
            pe_s.ahead(pe)

            def body(i, s, b, q):
                for g in range(4):
                    pe.wait_ge(v_s.sem, v_s.of(i, Q[g]))
                    pe.wait_ge(a_s.sem, a_s.of(i, Q[g], 1))
                    for t in range(4):
                        last = pe.matmul(K.ps[:, g, P * t:P * t + P], cols[:, 4 * g + t, :], rows[:, 4 * g + t, :],
                                         start=True, stop=True)
                    last.then_inc(pe_s.step(Q[g]), 1)
            turns(pe, body)

        @block.scalar
        def _(act):
            a_s.ahead(act)

            def body(i, s, b, q):
                act.wait_ge(stored[b], 16 * s + 16)
                for g in range(4):
                    act.wait_ge(pe_s.sem, pe_s.of(i, Q[g]))
                    act.copy(stage[:, b, :, bass.ds(16 * q + 4 * g, 4)].rearrange("p i t -> p t i"),
                             K.ps[:, g, :].rearrange("p (t i) -> p t i", t=4)).then_inc(a_s.step(Q[g]), 1)
            turns(act, body)


def experts_stage(nc, K, a, x1):
    R = 2
    with ExitStack() as ctx:
        def sb(name, shape, dt=F32):
            return ctx.enter_context(nc.sbuf_tensor("ex_" + name, shape, dt))

        def sem(name):
            return ctx.enter_context(nc.semaphore("ex_" + name))

        u, uh, ul = sb("u", [P, DC, P]), sb("uh", [P, R, DC, P], F32R), sb("ul", [P, R, DC, P], F32R)
        v, vh, vl = sb("v", [P, DC, P]), sb("vh", [P, R, DC, P], F32R), sb("vl", [P, R, DC, P], F32R)
        g, h = sb("g", [P, T]), sb("h", [P, T])
        hh, hl = sb("hh", [P, R, T], F32R), sb("hl", [P, R, T], F32R)
        V = [f"V{d}" for d in range(DC)]
        pe_s = Steps(sem("tensor"), ["U0", "U1"] + V)
        a_s = Steps(sem("scalar"), ["u1", "v0", "gelu0", "h0", "v1", "gelu1", "h1", "u0"])
        v_s = Steps(sem("vector"), ["u1", "v0", "gate0", "h0", "v1", "gate1", "h1"] + V[:9] + ["u0"] + V[9:])
        us, vs, gs = sem("u_in"), sem("v_in"), sem("gates_in")
        Z = [K.ps[:, 2 * n:2 * n + 2, 0:HT] for n in range(4)]
        N = ROWS // R
        block = ctx.enter_context(nc.Block())

        def by_stage(g):
            return g[:, :].rearrange("p (s t) -> p s t", t=TC)

        def every_turn(eng, body):
            with eng.Fori(0, N - 1) as i:
                body(i, False)
            body(N - 1, True)

        @block.sync
        def _(sp):
            sp.dma_start(u[:, :, :], a["peer_u"][0]).then_inc(us, 16)

            def body(i, last):
                sp.wait_ge(v_s.sem, v_s.of(i, "u0", 1))
                sp.dma_start(u[:, :, :], a["peer_u"][R * i + 1]).then_inc(us, 16)
                sp.wait_ge(v_s.sem, v_s.of(i, "v1", 1))
                sp.dma_start(v[:, :, :], a["peer_v"][R * i]).then_inc(vs, 16)
                sp.wait_ge(v_s.sem, v_s.of(i, "gate1", 1))
                sp.dma_start(by_stage(g), K.gates[:, :, R * i, :]).then_inc(gs, 16)
                if not last:
                    sp.wait_ge(v_s.sem, v_s.of(i, "u1"))
                    sp.dma_start(u[:, :, :], a["peer_u"][R * i + 2]).then_inc(us, 16)
                sp.wait_ge(v_s.sem, v_s.of(i, "v0"))
                sp.dma_start(v[:, :, :], a["peer_v"][R * i + 1]).then_inc(vs, 16)
                sp.wait_ge(v_s.sem, v_s.of(i, "gate0"))
                sp.dma_start(by_stage(g), K.gates[:, :, R * i + 1, :]).then_inc(gs, 16)
            every_turn(sp, body)

        @block.tensor
        def _(pe):
            pe_s.ahead(pe)

            def body(i, last):
                for r in range(R):
                    pe.wait_ge(v_s.sem, v_s.of(i, "u0", 1) if r == 0 else v_s.of(i, "u1"))
                    pe.wait_ge(a_s.sem, a_s.of(i, f"gelu{r}", 1))
                    project3(pe, Z[r], uh[:, r, :, :], ul[:, r, :, :], K.hh, K.hl).then_inc(pe_s.step(f"U{r}"), 1)
                for d in range(DC):
                    pe.wait_ge(v_s.sem, v_s.of(i, V[d - 2]) if d >= 2 else v_s.of(i, "v1"))
                    z = Z[2 + d % 2]
                    for r in range(R):
                        if d == 0 and r == 1:
                            pe.wait_ge(v_s.sem, v_s.of(i, "h1"))
                        for n in range(2):
                            t = slice(n * HT, (n + 1) * HT)
                            pe.matmul(z[:, n, :], vh[:, r, d, :], hh[:, r, t], start=(r == 0), stop=False)
                            pe.matmul(z[:, n, :], vh[:, r, d, :], hl[:, r, t], start=False, stop=False)
                        for n in range(2):
                            t = slice(n * HT, (n + 1) * HT)
                            done = pe.matmul(z[:, n, :], vl[:, r, d, :], hh[:, r, t], start=False, stop=(r == R - 1))
                    done.then_inc(pe_s.step(V[d]), 1)
            every_turn(pe, body)

        @block.scalar
        def _(act):
            a_s.ahead(act)
            act.wait_ge(us, 16)
            act.copy(uh[:, 0, :, :], u[:, :, :]).then_inc(us, 1)

            def body(i, last):
                def row(r):
                    act.wait_ge(pe_s.sem, pe_s.of(i, f"U{r}"))
                    act.wait_ge(v_s.sem, v_s.of(i, "h1", 1) if r == 0 else v_s.of(i, "h0"))
                    act.activation(halves(h[:, :]), Z[r], ACT.Gelu).then_inc(a_s.step(f"gelu{r}"), 1)
                    act.wait_ge(v_s.sem, v_s.of(i, f"gate{r}"))
                    act.copy(hh[:, r, :], h[:, :]).then_inc(a_s.step(f"h{r}"), 1)

                act.wait_ge(pe_s.sem, pe_s.of(i, V[-1], 1))
                act.wait_ge(us, 32 * i + 33)
                act.copy(uh[:, 1, :, :], u[:, :, :]).then_inc(a_s.step("u1"), 1)
                act.wait_ge(vs, 32 * i + 16)
                act.copy(vh[:, 0, :, :], v[:, :, :]).then_inc(a_s.step("v0"), 1)
                row(0)
                act.wait_ge(vs, 32 * i + 32)
                act.copy(vh[:, 1, :, :], v[:, :, :]).then_inc(a_s.step("v1"), 1)
                row(1)
                if not last:
                    act.wait_ge(us, 32 * i + 49)
                    act.copy(uh[:, 0, :, :], u[:, :, :]).then_inc(a_s.step("u0"), 1)
            every_turn(act, body)

        @block.vector
        def _(dve):
            dve.wait_ge(us, 17)
            dve.tensor_tensor(ul[:, 0, :, :], u[:, :, :], uh[:, 0, :, :].bitcast(F32), ALU.subtract)
            dve.drain()
            v_s.ahead(dve)

            def body(i, last):
                def low(name, out, src, high):
                    dve.wait_ge(a_s.sem, a_s.of(i, name))
                    dve.tensor_tensor(out, src[:], high.bitcast(F32), ALU.subtract).then_inc(v_s.step(name), 1)

                def row(r):
                    dve.wait_ge(a_s.sem, a_s.of(i, f"gelu{r}"))
                    dve.wait_ge(gs, 32 * i + 16 * r + 16)
                    dve.tensor_tensor(h[:, :], h[:, :], g[:, :], ALU.mult).then_inc(v_s.step(f"gate{r}"), 1)
                    low(f"h{r}", hl[:, r, :], h, hh[:, r, :])

                low("u1", ul[:, 1, :, :], u, uh[:, 1, :, :])
                low("v0", vl[:, 0, :, :], v, vh[:, 0, :, :])
                row(0)
                low("v1", vl[:, 1, :, :], v, vh[:, 1, :, :])
                row(1)
                for d in range(DC):
                    if d in (3, 5, 7, 9) and not last:
                        q = slice(2 * (d - 3), 2 * (d - 3) + 4)
                        if d == 3:
                            dve.wait_ge(a_s.sem, a_s.of(i, "u0"))
                        low_u = dve.tensor_tensor(ul[:, 0, q, :], u[:, q, :], uh[:, 0, q, :].bitcast(F32), ALU.subtract)
                    if d == 9:
                        if last:
                            dve.drain().then_inc(v_s.step("u0"), 1)
                        else:
                            low_u.then_inc(v_s.step("u0"), 1)
                    x = halves(x1[:, d, :])
                    dve.wait_ge(pe_s.sem, pe_s.of(i, V[d]))
                    dve.tensor_tensor(x, x, Z[2 + d % 2], ALU.add).then_inc(v_s.step(V[d]), 1)
            every_turn(dve, body)


class Kit:
    pass


def constants():
    t = np.arange(C)
    h2, t2 = np.repeat([0, 1], C), np.tile(t, 2)
    same = h2[:, None] == h2[None, :]
    i, s = t2[:, None], t2[None, :]
    out = {}
    mask = np.zeros((P, 2, 4, P))
    b16, b8 = i // 16 == s // 16, i // LSEQ == s // LSEQ
    mask[:, 0, 0] = same & b16 & (i < s)
    mask[:, 0, 1] = same & (i < s)
    mask[:, 0, 2] = mask[:, 0, 3] = same & (i <= s)
    mask[:, 1, 0] = mask[:, 1, 1] = same & b8 & (i < s)
    mask[:, 1, 2] = mask[:, 1, 3] = same & b8 & (i <= s)
    out["c_mask"] = mask
    out["c_moff"] = same & ~b16 & (i < s)
    out["c_mlow"] = np.stack([same & b16 & (i > s), same & b8 & (i > s)], 1)
    out["c_mseq"] = t2[:, None] // LSEQ == np.arange(NSEQ)[None, :]
    one0 = np.ones((P, T))
    one0[:, 0:TP:C] = 0
    one0[:, TP::LSEQ] = 0
    out["c_one0"] = one0
    f = np.arange(P)
    out["c_blk"] = f[:, None] // HEAD == f[None, :] // HEAD
    out["c_sel"] = f[:, None] % C == np.arange(C)[None, :]
    out["c_ident"] = np.eye(P)
    out["c_half30"] = np.full((P, 1), 15 * np.log(2.0))
    pos = np.concatenate([np.arange(TP), PAST + np.tile(np.arange(LSEQ), NSEQ)]).astype(np.float32)
    inv = np.power(np.float32(10000.0), -np.linspace(0.0, 1.0, P // 2, dtype=np.float32)).astype(np.float32)
    ang = (inv[:, None] * pos[None, :]).astype(np.float32).astype(np.float64)
    out["c_cos"] = np.concatenate([np.cos(ang), np.cos(ang)])
    out["c_sin"] = np.concatenate([-np.sin(ang), np.sin(ang)])
    out["c_perm"] = f[:, None] == (f[None, :] + P // 2) % P
    ret = np.zeros((HB, P, RET_CON))
    for h in range(HB):
        lg = float(np.log(np.float32(1.0 - 2.0 ** (-5.0 - h))))
        i = np.arange(RC)
        ts = np.arange(TS)
        d = i[None, :] - i[:, None]
        ds = ts[None, :] - ts[:, None]
        own = ts[None, :] // LSEQ == ts[:, None] // LSEQ
        ret[h, :, 0:TP] = np.exp(lg * (np.arange(TP) % RC + 1.0))
        ret[h, :, TP:T] = np.exp(lg * (ts % LSEQ + 1.0))
        ret[h, :, T:T + RC] = np.where(d >= 0, np.exp(lg * np.maximum(d, 0)), 0)
        ret[h, :TS, T + RC:T + RC + TS] = np.where((ds >= 0) & own, np.exp(lg * np.maximum(ds, 0)), 0)
        o = T + RC + TS
        ret[h, :, o] = np.exp(lg * (RC - 1.0 - i))
        ret[h, :, o + 1] = np.exp(lg * RC)
        ret[h, :, o + 2] = np.exp(lg * LSEQ)
        ret[h, :TS, o + 3:] = np.exp(lg * (LSEQ - 1.0 - ts % LSEQ))[:, None] * (ts[:, None] // LSEQ == np.arange(NSEQ))
    out["c_ret"] = ret
    return {k: np.ascontiguousarray(v, dtype=np.float32) for k, v in out.items()}


def columns(w):
    k, n = w.shape
    return np.ascontiguousarray(w.reshape(k // P, P, n // P, P).transpose(2, 1, 0, 3))


def features(v):
    return np.ascontiguousarray(v.reshape(-1, P).T)


def lay_out(i):
    A = {k: np.asarray(v) for k, v in i.items()}
    out = constants()
    x = np.concatenate([A["x_prompt"].reshape(TP, D), A["x_sample"].reshape(TS, D)])
    out["x"] = np.ascontiguousarray(x.T.reshape(DC, P, T).transpose(1, 0, 2))
    w = A["w_in"][0]
    out["w_rkv"] = np.ascontiguousarray(columns(w[:, :3072]).reshape(3, PAIRS, P, DC, P).transpose(1, 0, 2, 3, 4))
    out["w_lora"] = np.ascontiguousarray(w[:, 3072:3360].reshape(DC, P, LORA).transpose(1, 0, 2))
    out["w_low2"] = np.ascontiguousarray(np.concatenate(
        [np.concatenate([A["w_w2"][0], A["w_a2"][0]]).reshape(P, PAIRS, P), A["w_g2"][0][:P].reshape(P, PAIRS, P)], 2)
        .transpose(1, 0, 2))
    out["w_low3"] = np.ascontiguousarray(A["w_g2"][0][P:].reshape(32, PAIRS, P).transpose(1, 0, 2))
    mu = A["mu_shift"][0]
    out["w_par"] = np.ascontiguousarray(np.stack(
        [features(mu[0:1024]), features(mu[1024:2048]), features(mu[2048:3072])]
        + [features(A[n][0]) for n in ("w0", "a0", "k_k", "k_a", "r_k", "lnx_w", "lnx_b")], 2))

    def with_lora(rows):
        n = rows.shape[0]
        r = rows[:, :3072].reshape(n, 3, PAIRS, P).transpose(3, 2, 1, 0).reshape(P, 3 * PAIRS, n)
        l = np.zeros((P, 3, n), np.float32)
        l[:, 0], l[:, 1], l[:32, 2] = rows[:, 3072:3200].T, rows[:, 3200:3328].T, rows[:, 3328:].T
        return np.ascontiguousarray(np.concatenate([r, l], 1))

    out["lora_mu"] = np.ascontiguousarray(with_lora(mu[None])[:, 3 * PAIRS:, 0])
    out["shift_in"] = with_lora(A["state_shift"][0])
    out["wkv_in"] = np.ascontiguousarray(A["state_wkv"][0].reshape(NSEQ, PAIRS, 2, HEAD, HEAD)
                                         .transpose(1, 2, 4, 0, 3).reshape(PAIRS, P, NSEQ, HEAD))
    out["g_norm1"] = features(A["norm1"][0])
    out["g_norm2"] = features(A["norm2"][0])
    out["g_normf"] = features(A["norm_f"])
    q0, k0, v0, g0, m0 = 3360, 3360 + 1024, 3360 + 2048, 3360 + 4096, 3360 + 6144
    gate = columns(w[:, g0:m0]).reshape(HB, 2, P, DC, P)
    out["w_qkg"] = np.ascontiguousarray(np.concatenate(
        [columns(w[:, q0:k0])[:, None], columns(w[:, k0:v0])[:, None], gate], 1))
    out["w_v"] = np.ascontiguousarray(w[:, v0:g0].reshape(DC, P, HB, VH).transpose(2, 1, 0, 3))
    out["ret_in"] = np.ascontiguousarray(A["state_ret"][0].transpose(1, 2, 0, 3))
    out["w_ga"], out["w_gb"] = columns(w[:, m0:m0 + D]), columns(w[:, m0 + D:])
    out["w_pa"], out["w_pb"], out["w_out"] = (columns(A[n][0]) for n in ("w_pa", "w_pb", "w_out"))
    out["c_iota"] = np.ascontiguousarray(np.broadcast_to(np.arange(P, dtype=np.float32), (P, P)))
    out["w_q"] = columns(A["peer_wq"][0])
    out["keys"] = np.ascontiguousarray(A["peer_keys"][0].transpose(3, 0, 1, 2).reshape(P, 2 * PH, NK))
    out["peer_u"] = np.ascontiguousarray(A["peer_u"][0].reshape(ROWS, P, DC, P).transpose(0, 3, 2, 1))
    out["peer_v"] = np.ascontiguousarray(A["peer_v"][0].reshape(ROWS, P, DC, P))
    return out


OUTS = {"y": (P, DC, T), "ret_out": (HB, P, 1 + NSEQ, VH), "shift_out": (P, 3 * PAIRS + 3, 1 + NSEQ), "wkv_out": (PAIRS, P, 1 + NSEQ, HEAD)}


def build(nc, a):
    K = Kit()
    with ExitStack() as ctx:
        K.ps = ctx.enter_context(nc.psum_tensor("ps", [P, 8, 512], F32))
        K.ones = ctx.enter_context(nc.sbuf_tensor("ones", [P, P], F32))
        K.ident = ctx.enter_context(nc.sbuf_tensor("ident", [P, P], F32))
        K.half30 = ctx.enter_context(nc.sbuf_tensor("half30", [P, 1], F32))
        K.hn = ctx.enter_context(nc.sbuf_tensor("hn", [P, DC, T], F32))
        K.oa = nc.dram_tensor("oa", (PAIRS, P, T), F32, kind="Internal").ap()
        K.ob = nc.dram_tensor("ob", (HB, P, 2, T), F32, kind="Internal").ap()
        g1 = ctx.enter_context(nc.sbuf_tensor("g1", [P, DC], F32))
        s_c = ctx.enter_context(nc.semaphore("constants"))
        s_1 = ctx.enter_context(nc.semaphore("ones_made"))
        with nc.Block() as block:
            @block.sync
            def _(sp):
                for dst, src in ((K.ident, "c_ident"), (K.half30, "c_half30"), (g1, "g_norm1")):
                    sp.dma_start(dst[:, :], a[src]).then_inc(s_c, 16)
                sp.wait_ge(s_c, 48)

            @block.gpsimd
            def _(pool):
                pool.memset(K.ones[:, :], 1.0).then_inc(s_1, 1)
                pool.wait_ge(s_1, 1)
        with nc.sbuf_tensor("x1a", [P, DC, T], F32) as xt:
            norm_stage(nc, K, "n1", xt, K.hn, g1, load=a["x"])
        rwkv_stage(nc, K, a)
        ret_stage(nc, K, a)
        x1 = K.hn
        g2 = ctx.enter_context(nc.sbuf_tensor("g2", [P, 2, DC], F32))
        with nc.sbuf_tensor("m", [P, DC, T], F32) as m:
            merge_stage(nc, K, a, m)
            out_stage(nc, K, a, m, x1)
        s_g = ctx.enter_context(nc.semaphore("gains"))
        with nc.Block() as block:
            @block.sync
            def _(sp):
                for n, src in enumerate(("g_norm2", "g_normf")):
                    sp.dma_start(g2[:, n, :], a[src]).then_inc(s_g, 16)
                sp.wait_ge(s_g, 32)
        K.gates = nc.dram_tensor("gates", (P, T // TC, ROWS, TC), F32, kind="Internal").ap()
        with (nc.sbuf_tensor("hn_high", [P, DC, T], F32R) as K.hh,
              nc.sbuf_tensor("hn_low", [P, DC, T], F32R) as K.hl):
            with nc.sbuf_tensor("hn2", [P, DC, T], F32) as hn2:
                norm_stage(nc, K, "n2", x1, hn2, g2[:, 0, :], parts=(K.hh, K.hl))
            with nc.sbuf_tensor("slots", [P, 3, NTT * P], F32) as slots:
                with (nc.sbuf_tensor("top_v", [P, NTT, 2 * PH, TOPK], F32) as top_v,
                      nc.sbuf_tensor("top_i", [P, NTT, 2 * PH, TOPK], F32) as top_i):
                    route_stage(nc, K, a, top_v, top_i)
                    pick_stage(nc, K, a, top_v, top_i, slots)
                gates_stage(nc, K, a, slots)
            experts_stage(nc, K, a, x1)
        with nc.sbuf_tensor("y_sb", [P, DC, T], F32) as y:
            norm_stage(nc, K, "nf", x1, y, g2[:, 1, :], store=a["y"])


def kernel(**inputs):
    import concourse.bacc as bacc
    from concourse.bass_utils import run_bass_kernel_spmd

    nc = bacc.Bacc("TRN2", target_bir_lowering=False, num_devices=1)
    arrays = lay_out(inputs)
    a = {n: nc.dram_tensor(n, v.shape, F32, kind="ExternalInput").ap() for n, v in arrays.items()}
    a.update({n: nc.dram_tensor(n, s, F32, kind="ExternalOutput").ap() for n, s in OUTS.items()})
    build(nc, a)
    got = run_bass_kernel_spmd(nc, [arrays], core_ids=[0]).results[0]
    y = np.ascontiguousarray(got["y"].transpose(2, 1, 0).reshape(T, D))
    sh = got["shift_out"]
    rkv = sh[:, :3 * PAIRS].reshape(P, PAIRS, 3, 1 + NSEQ).transpose(3, 2, 1, 0).reshape(1 + NSEQ, 3 * PAIRS * P)
    lora = [sh[:n, 3 * PAIRS + t].T for t, n in enumerate((P, P, 32))]
    shift = np.ascontiguousarray(np.concatenate([rkv] + lora, 1))
    wkv = np.ascontiguousarray(got["wkv_out"].reshape(PAIRS, 2, HEAD, 1 + NSEQ, HEAD).transpose(3, 0, 1, 4, 2)
                               .reshape(1 + NSEQ, 2 * PAIRS, HEAD, HEAD))
    ret = np.ascontiguousarray(got["ret_out"].transpose(2, 0, 1, 3))
    return (y[:TP].reshape(1, TP, D), y[TP:].reshape(NSEQ, LSEQ, D), shift[None, :1], wkv[None, :1], ret[None, :1],
            shift[None, 1:], wkv[None, 1:], ret[None, 1:])
```

```python
from contextlib import ExitStack
import numpy as np
import concourse.bass as bass
from concourse import mybir

F32 = mybir.dt.float32
F32R = mybir.dt.float32r
U32 = mybir.dt.uint32
ALU = mybir.AluOpType
ACT = mybir.ActivationFunctionType
AX = mybir.AxisListType

P = 128
D = 2048
DC = D // P
TP = 512
NSEQ, LSEQ = 8, 8
TS = NSEQ * LSEQ
T = TP + TS
HT = T // 2
HEAD = 64
PAIRS = 8
C = 64
NCH = T // C
GRP = 3
PAST = 4096
PH = 8
NK = 128
TOPK = 16
NTT = -(-T // P)
LEAST = -3.0e38
TC = 48
LORA = 288
HB = 8
RC = 128
NRC = TP // RC
VH = 256
ROWS = 128
RET_CON = T + RC + TS + 3 + NSEQ
DECAY = float(np.exp(-0.5))
EPS = 1e-6
GN_EPS = 64e-5


class Steps:

    def __init__(self, sem, names):
        self.sem, self.names, self.n = sem, {x: k + 1 for k, x in enumerate(names)}, len(names)
        self.told = 0

    def ahead(self, eng):
        eng.sem_inc(self.sem, self.n)

    def of(self, i, name, back=0):
        return (i + (1 - back)) * self.n + self.names[name]

    def last(self, i, names):
        return (i + 1) * self.n + max(self.names[x] for x in names)

    def step(self, name):
        assert self.names[name] == self.told % self.n + 1, (name, self.told)
        self.told += 1
        return self.sem


def halves(ap):
    return ap.rearrange("p (a b) -> p a b", a=2)


def project(pe, out, weight, act, k=DC):
    for c in range(k):
        for h in range(2):
            last = pe.matmul(out[:, h, :], weight[:, c, :], act[:, c, h * HT:(h + 1) * HT],
                             start=(c == 0), stop=(c == k - 1))
    return last


def project3(pe, out, wh, wl, ah, al, k=DC):
    for c in range(k):
        for h in range(2):
            t = slice(h * HT, (h + 1) * HT)
            pe.matmul(out[:, h, :], wh[:, c, :], ah[:, c, t], start=(c == 0), stop=False)
            pe.matmul(out[:, h, :], wh[:, c, :], al[:, c, t], start=False, stop=False)
        for h in range(2):
            t = slice(h * HT, (h + 1) * HT)
            last = pe.matmul(out[:, h, :], wl[:, c, :], ah[:, c, t], start=False, stop=(c == k - 1))
    return last


def norm_stage(nc, K, tag, src, dst, gain, load=None, store=None, parts=None):
    with ExitStack() as ctx:
        ld = ctx.enter_context(nc.semaphore(tag + "_loaded"))
        sq = ctx.enter_context(nc.semaphore(tag + "_squared"))
        ss = ctx.enter_context(nc.semaphore(tag + "_summed"))
        ms = ctx.enter_context(nc.semaphore(tag + "_mean"))
        rs = ctx.enter_context(nc.semaphore(tag + "_rstd"))
        dn = ctx.enter_context(nc.semaphore(tag + "_normed"))
        st = ctx.enter_context(nc.semaphore(tag + "_stored"))
        hi = ctx.enter_context(nc.semaphore(tag + "_high"))
        rstd = ctx.enter_context(nc.sbuf_tensor(tag + "_r", [P, T], F32))
        pz = K.ps[:, 0:2, 0:HT]
        block = ctx.enter_context(nc.Block())

        @block.sync
        def _(sp):
            if load is not None:
                for q in range(4):
                    sp.dma_start(src[:, 4 * q:4 * q + 4, :], load[:, 4 * q:4 * q + 4, :]).then_inc(ld, 16)
            if store is not None:
                for q in range(4):
                    sp.wait_ge(dn, 4 * q + 4)
                    sp.dma_start(store[:, 4 * q:4 * q + 4, :], dst[:, 4 * q:4 * q + 4, :]).then_inc(st, 16)
                sp.wait_ge(st, 64)

        @block.scalar
        def _(act):
            for c in range(DC):
                if load is not None:
                    act.wait_ge(ld, 64)
                act.activation(dst[:, c, :], src[:, c, :], ACT.Square).then_inc(sq, 1)
            act.wait_ge(ms, 1)
            act.activation(rstd[:, :], rstd[:, :], ACT.Ln)
            act.drain()
            act.activation(rstd[:, :], rstd[:, :], ACT.Exp, scale=-0.5).then_inc(rs, 1)
            for c in range(DC if parts else 0):
                act.wait_ge(dn, c + 1)
                act.copy(parts[0][:, c, :], dst[:, c, :]).then_inc(hi, 1)

        @block.tensor
        def _(pe):
            for c in range(DC):
                pe.wait_ge(sq, c + 1)
                for h in range(2):
                    last = pe.matmul(pz[:, h, :], K.ones[:, :], dst[:, c, h * HT:(h + 1) * HT],
                                     start=(c == 0), stop=(c == DC - 1))
            last.then_inc(ss, 1)

        @block.vector
        def _(dve):
            dve.wait_ge(ss, 1)
            dve.tensor_scalar(halves(rstd[:, :]), pz, 1.0 / D, EPS, ALU.mult, ALU.add).then_inc(ms, 1)
            dve.wait_ge(rs, 1)
            for c in range(DC):
                dve.scalar_tensor_tensor(out=dst[:, c, :], in0=src[:, c, :], scalar=gain[:, c:c + 1],
                                         in1=rstd[:, :], op0=ALU.mult, op1=ALU.mult).then_inc(dn, 1)
            for c in range(DC if parts else 0):
                dve.wait_ge(hi, c + 1)
                dve.tensor_tensor(parts[1][:, c, :], dst[:, c, :], parts[0][:, c, :].bitcast(F32), ALU.subtract)


def inverse_plan():
    return [
        ("f2", "F", "f", "A", "G", None),
        ("F2", "f", "F", "B", None, None),
        ("f4", "B", "A", "E", None, None),
        ("F4", "A", "B", "H", "J", None),
        ("D1", "G", "IF", "L", None, None),
        ("f8", "H", "E", None, "A", None),
        ("D2", "J", "A", "B", None, None),
        ("D", "L", "B", "G", None, None),
        ("DT", "B", "L", "E", None, None),
        ("e", "E", "o", "H", None, None),
        ("eT", "o", "E", "A", None, "J"),
        ("e2", "H", "A", None, "L", None),
        ("h", "L", "G", "B", None, None),
        ("Z", "J", "B", "Z", None, None),
    ]


def rwkv_stage(nc, K, a):
    with ExitStack() as ctx:
        def sb(name, shape):
            return ctx.enter_context(nc.sbuf_tensor("rwkv_" + name, shape, F32))

        def sem(name):
            return ctx.enter_context(nc.semaphore("rwkv_" + name))

        ring = sb("weights", [P, 3, DC, P])
        lora_w = ring[:, :, :, :].rearrange("p a b c -> p (a b c)")[:, 0:DC * LORA]\
            .rearrange("p (c n) -> p c n", c=DC)
        low2 = sb("low2", [P, 2 * P])
        low3 = sb("low3", [32, P])
        s0 = sb("s0", [P, NSEQ, HEAD])
        par = sb("par", [P, PAIRS, 10])
        lmu = sb("lmu", [P, 3])
        shin = sb("shin", [P, PAIRS * 3 + 3, NSEQ])
        shout = sb("shout", [P, PAIRS * 3 + 3, 1 + NSEQ])
        one0 = sb("one0", [P, T])
        mask = sb("mask", [P, 2, 4, P])
        moff = sb("moff", [P, P])
        mlow = sb("mlow", [P, 2, P])
        mseq = sb("mseq", [P, NSEQ])
        blk = sb("blk", [P, P])
        sel = sb("sel", [P, C])
        zx = sb("zx", [P, 3, 1 + TP + NSEQ * (LSEQ + 1)])
        dif = sb("dif", [P, T])
        rs, ks, vs = sb("rs", [P, T]), sb("ks", [P, T]), sb("vs", [P, T])
        lo0, lo1, lo2 = sb("lo0", [P, T]), sb("lo1", [P, T]), sb("lo2", [32, T])
        kk, ksq, cs, cse = sb("kk", [P, T]), sb("ksq", [P, T]), sb("cs", [P, T]), sb("cse", [P, T])
        sg, at, winc, gg = sb("sg", [P, T]), sb("at", [P, T]), sb("winc", [P, T]), sb("gg", [P, T])
        kf, bb, rk = sb("kf", [P, T]), sb("bb", [P, T]), sg
        pads = {x: sb("pad_" + x, [P, NCH, P]) for x in "pqbkv"}
        xm = sb("xm", [P, NCH, 4, P])
        off = sb("off", [P, NCH, P])
        low = sb("low", [P, NCH, P])
        ilow = sb("ilow", [P, GRP, P])
        tok = sb("tok", [P, NCH, 320])
        zz = sb("zz", [P, NCH, P])
        mats = {x: sb("m" + x, [P, GRP, P]) for x in "ABEGHJL"}
        st = sb("st", [P, 2, HEAD])
        rn, uu = sb("rn", [P, HEAD]), sb("uu", [P, HEAD])
        yy = sb("yy", [P, NCH, HEAD])
        big = um = cs[:, 0:NSEQ * HEAD].rearrange("p (b v) -> p b v", b=NSEQ)
        vm = cse[:, 0:NSEQ * HEAD].rearrange("p (b v) -> p b v", b=NSEQ)
        r1, y1 = sb("r1", [P, HEAD]), sb("y1", [P, HEAD])
        so = sb("so", [P, NSEQ, HEAD])
        gm, gv = sb("gm", [P, NCH]), sb("gv", [P, NCH])
        ypad = pads["b"]
        oo = sb("oo", [P, T])
        ident = K.ident

        groups = [range(g * GRP, (g + 1) * GRP) for g in range(NCH // GRP)]
        plan = inverse_plan()
        inv = [f"{g}_{x[0]}" for g in range(len(groups)) for x in plan]
        chain = [f"{x}{c}" for c in range(NCH - 1) for x in "RUSY"]
        pe_s = Steps(sem("tensor"), ["w", "a", "g", "ss", "bon"]
                     + [f"{x}{c}" for c in range(NCH) for x in "xt"] + inv + chain
                     + ["sR", "s8", "sY", "sU", "sV", "sS", "yT"])
        v_s = Steps(sem("vector"), ["sh_r", "sh_k", "ksq", "sh_v", "cse", "max", "rp", "b", "pq"]
                    + [f"{x}{c}" for c in range(NCH) for x in ("mx", "mt")]
                    + [y for g in range(len(groups))
                       for y in [f"il{g}"] + [f"{g}_{x[0]}" for x in plan if x[4] or x[5]]]
                    + [f"{x}{c}" for c in range(NCH - 1) for x in ("R", "U", "S")]
                    + ["sR", "s8", "sY", "sU", "sUm", "sV", "sS", "var", "ypad", "oa"])
        a_s = Steps(sem("scalar"), ["sg", "at", "gg", "rkk", "exp"]
                    + [f"tv{c}" for c in range(NCH)]
                    + [f"{g}_{x[0]}" for g in range(len(groups)) for x in plan if x[3]]
                    + [f"Y{c}" for c in range(NCH - 1)] + ["rstd"])
        p_s = Steps(sem("pool"), ["bp", "kp", "vp"])
        made, copied = Steps(sem("made"), "rkv"), Steps(sem("copied"), "rkv")
        rows_in, rows_out = Steps(sem("rows_in"), "rkv"), Steps(sem("rows_out"), "rkv")
        POINTS = len(groups) * len(plan)
        pieces = [64 * (n + 1) // POINTS for n in range(POINTS)]
        pieces += [64 + 32 * (n + 1) // (4 * NCH - 8) for n in range(4 * NCH - 8)] + [96] * 4
        consts = sem("consts")
        lw = sem("lora_weights")
        wt = [sem("tile_" + x) for x in "rkv"]
        small = sem("small_weights")
        stored = sem("stored")
        shst = sem("shift_stored")
        lz = sem("lora_projected")
        lin = sem("lora_shift_in")
        lev = sem("lora_evacuated")
        lsh = sem("lora_shifted")
        ldn = sem("lora_done")
        lout = sem("lora_shift_out")
        padz = sem("pads_zeroed")
        Z = [K.ps[:, 0:2, 0:HT], K.ps[:, 2:4, 0:HT]]
        X = [K.ps[:, 4 + b, :] for b in range(4)]

        def views(z, n=P):
            s = z[0:n, 1 + TP:].rearrange("p (b l) -> p b l", b=NSEQ)
            return z[0:n, 1:1 + TP], z[0:n, 0:TP], s[:, :, 1:], s[:, :, 0:LSEQ]

        def evacuate(act, z, src, n=P):
            cur, _, scur, _ = views(z, n)
            act.copy(cur[:, 0:HT], src[0:n, 0, :])
            act.copy(cur[:, HT:TP], src[0:n, 1, 0:TP - HT])
            return act.copy(scur, src[0:n, 1, TP - HT:HT].rearrange("p (b l) -> p b l", b=NSEQ))

        def shift(dve, z, mu, out, n=P):
            cur, prev, scur, sprev = views(z, n)
            dve.tensor_tensor(dif[0:n, 0:TP], prev, cur, ALU.subtract)
            dve.tensor_tensor(dif[0:n, TP:T].rearrange("p (b l) -> p b l", b=NSEQ), sprev, scur, ALU.subtract)
            dve.drain()
            dve.scalar_tensor_tensor(out=out[0:n, 0:TP], in0=dif[0:n, 0:TP], scalar=mu, in1=cur,
                                     op0=ALU.mult, op1=ALU.add)
            last = dve.scalar_tensor_tensor(
                out=out[0:n, TP:T].rearrange("p (b l) -> p b l", b=NSEQ),
                in0=dif[0:n, TP:T].rearrange("p (b l) -> p b l", b=NSEQ), scalar=mu, in1=scur,
                op0=ALU.mult, op1=ALU.add)
            return last

        def every_pair(eng, body):
            with eng.Fori(0, PAIRS - 1) as i:
                body(i, False)
            body(PAIRS - 1, True)

        def last_rows(pool, z, t, n=P):
            s = z[0:n, 1 + TP:].rearrange("p (b l) -> p b l", b=NSEQ)
            pool.tensor_copy(shout[0:n, t, 0:1], z[0:n, TP:TP + 1])
            return pool.tensor_copy(shout[0:n, t, 1:1 + NSEQ], s[:, :, LSEQ])

        def first_rows(pool, z, t, n=P):
            s = z[0:n, 1 + TP:].rearrange("p (b l) -> p b l", b=NSEQ)
            return pool.tensor_copy(s[:, :, 0], shin[0:n, t, :])

        block = ctx.enter_context(nc.Block())

        @block.sync
        def _(sp):
            sp.dma_start(lora_w, a["w_lora"]).then_inc(lw, 16)
            for dst, src in ((par, "w_par"), (lmu, "lora_mu"), (shin, "shift_in"), (one0, "c_one0"),
                             (mask, "c_mask"), (moff, "c_moff"), (mlow, "c_mlow"), (mseq, "c_mseq"),
                             (blk, "c_blk"), (sel, "c_sel")):
                sp.dma_start(dst[:], a[src]).then_inc(consts, 16)
            sp.wait_ge(lz, 3)
            with sp.Fori(0, PAIRS) as i:
                for t, x in enumerate("rkv"):
                    sp.wait_ge(made.sem, made.of(i, x, 1))
                    sp.dma_start(ring[:, t, :, :], a["w_rkv"][i, t]).then_inc(wt[t], 16)
                sp.wait_ge(pe_s.sem, pe_s.of(i, "g", 1))
                sp.dma_start(low2[:, :], a["w_low2"][i]).then_inc(small, 16)
                sp.dma_start(low3[:, :], a["w_low3"][i]).then_inc(small, 16)
                sp.wait_ge(pe_s.sem, pe_s.of(i, "sS", 1))
                sp.dma_start(s0[:, :, :], a["wkv_in"][i]).then_inc(small, 16)

        @block.gpsimd
        def _(pool):
            p_s.ahead(pool)
            rows_in.ahead(pool)
            rows_out.ahead(pool)
            for x in "pqbkv":
                pool.memset(pads[x][:, :, :], 0.0)
            pool.memset(off[:, NCH - 1, :], 0.0)
            pool.memset(zx[:, :, 0:1], 0.0)
            pool.memset(shout[:, :, :], 0.0)
            pool.drain().then_inc(padz, 1)
            pool.wait_ge(consts, 160)
            for t, n in ((0, P), (1, P), (2, 32)):
                if t == 2:
                    pool.wait_ge(lsh, 1)
                first_rows(pool, zx[:, t % 2, :], PAIRS * 3 + t, n).then_inc(lin, 1)
                pool.drain()
                if t == 1:
                    pool.wait_ge(lev, 1)
                    last_rows(pool, zx[:, 0, :], PAIRS * 3, P).then_inc(lout, 1)
            for t, n in ((1, P), (2, 32)):
                pool.wait_ge(lev, t + 1)
                last_rows(pool, zx[:, t % 2, :], PAIRS * 3 + t, n).then_inc(lout, 1)
                pool.drain()

            def rows(i):
                for t, x in enumerate("rkv"):
                    pool.wait_ge(v_s.sem, v_s.of(i, "sh_" + x, 1))
                    first_rows(pool, zx[:, t, :], 3 * i + t).then_inc(rows_in.step(x), 1)
                    pool.drain()
                for t, x in enumerate("rkv"):
                    pool.wait_ge(copied.sem, copied.of(i, x))
                    last_rows(pool, zx[:, t, :], 3 * i + t).then_inc(rows_out.step(x), 1)
                    pool.drain()

            pool.wait_ge(lsh, 3)
            rows(0)

            def body(i, last):
                def pad(x, p0, p1):
                    for h in range(2):
                        r = slice(HEAD * h, HEAD * h + HEAD)
                        o = pads[x][r, :, C * h:C * h + C]
                        u = p0[r, :].rearrange("p (c t) -> p c t", c=NCH)
                        if p1 is None:
                            last = pool.tensor_copy(o, u)
                        else:
                            last = pool.tensor_tensor(o, u, p1[r, :].rearrange("p (c t) -> p c t", c=NCH), ALU.mult)
                        if h == 0:
                            pool.drain()
                    return last

                pool.wait_ge(pe_s.sem, pe_s.of(i, "yT", 1))
                pool.wait_ge(a_s.sem, a_s.of(i, "exp"))
                pool.wait_ge(v_s.sem, v_s.of(i, "b"))
                pad("b", bb, cs).then_inc(p_s.step("bp"), 1)
                pool.drain()
                pad("k", kf, cs).then_inc(p_s.step("kp"), 1)
                pool.drain()
                pad("v", vs, None).then_inc(p_s.step("vp"), 1)
                pool.drain()
                if not last:
                    rows(i + 1)
            every_pair(pool, body)

        @block.scalar
        def _(act):
            a_s.ahead(act)
            copied.ahead(act)
            act.sem_inc(stored, 48)
            for t, n in ((0, P), (1, P), (2, 32)):
                act.wait_ge(lz, t + 1)
                act.wait_ge(padz, 1)
                if t == 2:
                    act.wait_ge(lsh, 1)
                    act.wait_ge(lout, 1)
                evacuate(act, zx[:, t % 2, :], Z[t % 2], n).then_inc(lev, 1)
            act.wait_ge(lsh, 3)
            act.activation(lo0[0:64, :], lo0[0:64, :], ACT.Tanh)
            act.activation(lo1[:, :], lo1[:, :], ACT.Sigmoid)
            act.activation(lo2[:, :], lo2[:, :], ACT.Sigmoid).then_inc(ldn, 1)

            def copy_out(i, x):
                act.wait_ge(made.sem, made.of(i, x))
                act.wait_ge(v_s.sem, v_s.of(i, "sh_" + x, 1))
                act.wait_ge(rows_out.sem, rows_out.of(i, x, 1))
                evacuate(act, zx[:, "rkv".index(x), :], Z[0]).then_inc(copied.step(x), 1)

            act.wait_ge(lout, 3)
            for x in "rkv":
                copy_out(0, x)

            def body(i, last):
                act.wait_ge(pe_s.sem, pe_s.of(i, "w"))
                act.wait_ge(v_s.sem, v_s.of(i, "oa", 1))
                act.activation(halves(sg[:, :]), Z[1], ACT.Sigmoid, bias=par[:, i, 3:4]).then_inc(a_s.step("sg"), 1)
                act.wait_ge(pe_s.sem, pe_s.of(i, "a"))
                act.activation(halves(at[:, :]), Z[0], ACT.Sigmoid, bias=par[:, i, 4:5]).then_inc(a_s.step("at"), 1)
                act.wait_ge(pe_s.sem, pe_s.of(i, "g"))
                act.copy(halves(gg[:, :]), Z[1]).then_inc(a_s.step("gg"), 1)
                act.wait_ge(v_s.sem, v_s.of(i, "max"))
                act.activation(rk[:, :], rk[:, :], ACT.Ln, scale=float(2 ** 30))
                act.drain()
                act.activation(rk[:, :], rk[:, :], ACT.Exp, scale=-0.5, bias=K.half30[:, 0:1]).then_inc(a_s.step("rkk"), 1)
                act.activation(winc[:, :], cs[:, :], ACT.Exp, scale=-DECAY)
                act.activation(cse[:, :], cse[:, :], ACT.Exp, scale=-DECAY)
                act.drain()
                act.activation(cs[:, :], cs[:, :], ACT.Exp, scale=DECAY).then_inc(a_s.step("exp"), 1)
                for c in range(NCH):
                    act.wait_ge(v_s.sem, v_s.of(i, f"mt{c}"))
                    act.copy(tok[:, c, :], X[2 + c % 2][:, P:P + 320]).then_inc(a_s.step(f"tv{c}"), 1)
                for g, cc in enumerate(groups):
                    for n, (name, _, _, to, _, _) in enumerate(plan):
                        if to:
                            act.wait_ge(pe_s.sem, pe_s.of(i, f"{g}_{name}"))
                            dst = zz[:, cc[0]:cc[-1] + 1, :] if to == "Z" else mats[to][:, :, :]
                            src = X[(g * len(plan) + n) % 4][:, 0:GRP * P].rearrange("p (a b) -> p a b", a=GRP)
                            act.copy(dst, src).then_inc(a_s.step(f"{g}_{name}"), 1)
                        point = g * len(plan) + n
                        if not last and (pieces[point - 1] if point else 0) < 32 <= pieces[point]:
                            copy_out(i + 1, "r")
                if not last:
                    copy_out(i + 1, "k")
                for c in range(NCH - 1):
                    act.wait_ge(pe_s.sem, pe_s.of(i, f"Y{c}"))
                    act.copy(yy[:, c, :], X[2][:, 0:HEAD]).then_inc(a_s.step(f"Y{c}"), 1)
                if not last:
                    copy_out(i + 1, "v")
                act.wait_ge(v_s.sem, v_s.of(i, "var"))
                act.activation(gv[:, :], gv[:, :], ACT.Ln)
                act.drain()
                act.activation(gv[:, :], gv[:, :], ACT.Exp, scale=-0.5).then_inc(a_s.step("rstd"), 1)
                act.wait_ge(v_s.sem, v_s.of(i, "oa"))
                act.dma_start(K.oa[i], oo[:, :]).then_inc(stored, 16)
                act.dma_start(a["wkv_out"][i, :, 0, :], st[:, 0, :]).then_inc(stored, 16)
                act.dma_start(a["wkv_out"][i, :, 1:1 + NSEQ, :], so[:, :, :]).then_inc(stored, 16)
            every_pair(act, body)
            act.wait_ge(rows_out.sem, rows_out.of(PAIRS - 1, "v"))
            act.dma_start(a["shift_out"], shout[:, :, :]).then_inc(shst, 16)
            act.wait_ge(shst, 16)
            act.wait_ge(stored, 48 * PAIRS + 48)

        @block.tensor
        def _(pe):
            pe_s.ahead(pe)
            made.ahead(pe)
            pe.wait_ge(lw, 16)
            for t, n in ((0, P), (1, P), (2, 32)):
                if t == 2:
                    pe.wait_ge(lev, 1)
                for c in range(DC):
                    for h in range(2):
                        last = pe.matmul(Z[t % 2][0:n, h, :], lora_w[:, c, P * t:P * t + n],
                                         K.hn[:, c, h * HT:(h + 1) * HT], start=(c == 0), stop=(c == DC - 1))
                last.then_inc(lz, 1)
            pe.wait_ge(lev, 3)
            pe.wait_ge(ldn, 1)
            pe.wait_ge(consts, 160)

            def project_pieces(i, lo, hi):
                for m in range(lo, hi):
                    t, c, h = m // 32, m % 32 // 2, m % 2
                    if m % 32 == 0:
                        pe.wait_ge(wt[t], 16 * i + 16)
                        if t:
                            pe.wait_ge(copied.sem, copied.of(i, "rkv"[t - 1]))
                    last = pe.matmul(Z[0][:, h, :], ring[:, t, c, :], K.hn[:, c, h * HT:(h + 1) * HT],
                                     start=(c == 0), stop=(c == DC - 1))
                    if m % 32 == 31:
                        last.then_inc(made.step("rkv"[t]), 1)

            project_pieces(0, 0, 96)

            def body(i, last_pair):
                pe.wait_ge(small, 48 * i + 48)
                pe.wait_ge(v_s.sem, v_s.of(i, "oa", 1))
                pe.wait_ge(copied.sem, copied.of(i, "v"))
                for x, z in (("w", 1), ("a", 0), ("g", 1)):
                    if x == "g":
                        pe.wait_ge(a_s.sem, a_s.of(i, "sg"))
                    for h in range(2):
                        tt = slice(h * HT, (h + 1) * HT)
                        if x == "w":
                            last = pe.matmul(Z[z][:, h, :], low2[0:64, 0:P], lo0[0:64, tt], start=True, stop=True)
                        elif x == "a":
                            last = pe.matmul(Z[z][:, h, :], low2[64:P, 0:P], lo0[64:P, tt], start=True, stop=True)
                        else:
                            pe.matmul(Z[z][:, h, :], low2[:, P:2 * P], lo1[:, tt], start=True, stop=False)
                            last = pe.matmul(Z[z][:, h, :], low3[:, :], lo2[:, tt], start=False, stop=True)
                    last.then_inc(pe_s.step(x), 1)
                for x, z, ev, src, after in (("ss", 0, "at", ksq, "ksq"), ("bon", 1, "gg", dif, "rp")):
                    pe.wait_ge(a_s.sem, a_s.of(i, ev))
                    pe.wait_ge(v_s.sem, v_s.of(i, after))
                    for h in range(2):
                        last = pe.matmul(Z[z][:, h, :], blk[:, :], src[:, h * HT:(h + 1) * HT], start=True, stop=True)
                    last.then_inc(pe_s.step(x), 1)
                pe.wait_ge(v_s.sem, v_s.of(i, "pq"))
                pe.wait_ge(p_s.sem, p_s.of(i, "vp"))
                for c in range(NCH):
                    pq = {x: pads[x][:, c, :] for x in "pqbkv"}
                    x = X[c % 2]
                    if c >= 2:
                        pe.wait_ge(v_s.sem, v_s.of(i, f"mx{c - 2}"))
                    for n, (l, r) in enumerate(("bp", "kp", "bq", "kq")):
                        last = pe.matmul(x[:, P * n:P * n + P], pq[l], pq[r], start=True, stop=True)
                    last.then_inc(pe_s.step(f"x{c}"), 1)
                    x = X[2 + c % 2]
                    if c >= 2:
                        pe.wait_ge(v_s.sem, v_s.of(i, f"mt{c - 2}"))
                        pe.wait_ge(a_s.sem, a_s.of(i, f"tv{c - 2}"))
                    pe.matmul(x[:, 0:P], pq["p"], pq["b"], start=True, stop=True)
                    pe.matmul(x[:, P:P + C], pq["v"], sel[:, :], start=True, stop=True)
                    pe.transpose(x[:, P + C:2 * P + C], pq["b"], ident[:, :])
                    pe.transpose(x[:, 2 * P + C:3 * P + C], pq["k"], ident[:, :])\
                        .then_inc(pe_s.step(f"t{c}"), 1)
                def out_of_bank(n):
                    g, (name, _, _, to, _, _) = n // len(plan), plan[n % len(plan)]
                    return ([f"{g}_{name}"], []) if to else ([], [f"{g}_{name}"])

                for g, cc in enumerate(groups):
                    for n, (name, l, r, _, _, _) in enumerate(plan):
                        at_bank = g * len(plan) + n
                        by_act, by_dve = out_of_bank(at_bank - 4) if at_bank >= 4 else ([], [])
                        for m in (l, r):
                            by = [k for k in range(n) if m in plan[k][3:6]]
                            if by and m == plan[by[-1]][3]:
                                by_act = by_act + [f"{g}_{plan[by[-1]][0]}"]
                            elif by:
                                by_dve = by_dve + [f"{g}_{plan[by[-1]][0]}"]
                        if n == 0:
                            by_dve = by_dve + [f"il{g}"]
                        if at_bank == 0:
                            by_act = by_act + [f"tv{NCH - 1}"]
                        if by_act:
                            pe.wait_ge(a_s.sem, a_s.last(i, by_act))
                        if by_dve:
                            pe.wait_ge(v_s.sem, v_s.last(i, by_dve))
                        for k, c in enumerate(cc):
                            given = {"f": xm[:, c, 0, :], "F": low[:, c, :], "IF": ilow[:, k, :], "o": off[:, c, :]}
                            ml, mr = (given[m] if m in given else mats[m][:, k, :] for m in (l, r))
                            last = pe.matmul(X[at_bank % 4][:, P * k:P * k + P], ml, mr, start=True, stop=True)
                        last.then_inc(pe_s.step(f"{g}_{name}"), 1)
                        if at_bank == 0:
                            pe.wait_ge(v_s.sem, v_s.of(i, "max"))
                        if not last_pair:
                            project_pieces(i + 1, pieces[at_bank - 1] if at_bank else 0, pieces[at_bank])
                freed = [out_of_bank(len(groups) * len(plan) - 1 - n) for n in range(4)]
                pe.wait_ge(a_s.sem, a_s.last(i, sum((x for x, _ in freed), [])))
                pe.wait_ge(v_s.sem, v_s.last(i, sum((x for _, x in freed), [])))

                def between(n):
                    if not last_pair:
                        project_pieces(i + 1, pieces[POINTS + n - 1], pieces[POINTS + n])

                for c in range(NCH - 1):
                    s = st[:, c % 2, :]
                    v, b, k = tok[:, c, 0:C], tok[:, c, C:C + P], tok[:, c, C + P:C + 2 * P]
                    if c:
                        pe.wait_ge(v_s.sem, v_s.of(i, f"S{c - 1}"))
                        pe.matmul(X[0][:, 0:HEAD], pads["p"][:, c, :], s, start=True, stop=False)
                    pe.matmul(X[0][:, 0:HEAD], xm[:, c, 1, :], v, start=(c == 0), stop=True)\
                        .then_inc(pe_s.step(f"R{c}"), 1)
                    between(4 * c)
                    pe.wait_ge(v_s.sem, v_s.of(i, f"R{c}"))
                    pe.matmul(X[1][:, 0:HEAD], zz[:, c, :], rn[:, :], start=True, stop=True)\
                        .then_inc(pe_s.step(f"U{c}"), 1)
                    between(4 * c + 1)
                    pe.wait_ge(v_s.sem, v_s.of(i, f"U{c}"))
                    if c:
                        pe.matmul(X[3][:, 0:HEAD], ident[:, :], s, start=True, stop=False)
                    pe.matmul(X[3][:, 0:HEAD], b, uu[:, :], start=(c == 0), stop=False)
                    pe.matmul(X[3][:, 0:HEAD], k, v, start=False, stop=True).then_inc(pe_s.step(f"S{c}"), 1)
                    between(4 * c + 2)
                    if c:
                        pe.wait_ge(a_s.sem, a_s.of(i, f"Y{c - 1}"))
                        pe.matmul(X[2][:, 0:HEAD], pads["q"][:, c, :], s, start=True, stop=False)
                    pe.matmul(X[2][:, 0:HEAD], xm[:, c, 2, :], uu[:, :], start=(c == 0), stop=False)
                    pe.matmul(X[2][:, 0:HEAD], xm[:, c, 3, :], v, start=False, stop=True)\
                        .then_inc(pe_s.step(f"Y{c}"), 1)
                    between(4 * c + 3)

                c = NCH - 1
                v, b, k = tok[:, c, 0:C], tok[:, c, C:C + P], tok[:, c, C + P:C + 2 * P]
                flat = s0[:, :, :].rearrange("p b v -> p (b v)")
                pe.matmul(X[0], pads["p"][:, c, :], flat, start=True, stop=True).then_inc(pe_s.step("sR"), 1)
                pe.matmul(X[1][:, 0:HEAD], xm[:, c, 1, :], v, start=True, stop=True).then_inc(pe_s.step("s8"), 1)
                pe.wait_ge(a_s.sem, a_s.of(i, f"Y{NCH - 2}"))
                pe.matmul(X[2], pads["q"][:, c, :], flat, start=True, stop=True).then_inc(pe_s.step("sY"), 1)
                pe.wait_ge(v_s.sem, v_s.of(i, "s8"))
                pe.matmul(X[3][:, 0:HEAD], zz[:, c, :], rn[:, :], start=True, stop=True)\
                    .then_inc(pe_s.step("sU"), 1)
                pe.wait_ge(v_s.sem, v_s.of(i, "sU"))
                pe.matmul(X[1][:, 0:HEAD], xm[:, c, 2, :], uu[:, :], start=True, stop=False)
                pe.matmul(X[1][:, 0:HEAD], xm[:, c, 3, :], v, start=False, stop=True)\
                    .then_inc(pe_s.step("sV"), 1)
                pe.wait_ge(v_s.sem, v_s.of(i, "sUm"))
                pe.matmul(X[0], ident[:, :], flat, start=True, stop=False)
                pe.matmul(X[0], b, cs[:, 0:NSEQ * HEAD], start=False, stop=False)
                pe.matmul(X[0], k, cse[:, 0:NSEQ * HEAD], start=False, stop=True)\
                    .then_inc(pe_s.step("sS"), 1)
                pe.wait_ge(v_s.sem, v_s.of(i, "ypad"))
                if not last_pair:
                    pe.wait_ge(copied.sem, copied.of(i + 1, "v"))
                for c in range(NCH):
                    o = K.ps[:, c // 5, C * (c % 5):C * (c % 5) + C]
                    last = pe.matmul(o, ypad[:, c, :], sel[:, :], start=True, stop=True)
                last.then_inc(pe_s.step("yT"), 1)
            every_pair(pe, body)

        @block.vector
        def _(dve):
            v_s.ahead(dve)
            dve.wait_ge(consts, 160)
            for t, (n, out) in enumerate(((P, lo0), (P, lo1), (32, lo2))):
                dve.wait_ge(lev, t + 1)
                dve.wait_ge(lin, t + 1)
                shift(dve, zx[:, t % 2, :], lmu[0:n, t:t + 1], out, n).then_inc(lsh, 1)
                dve.drain()
            dve.wait_ge(padz, 1)

            def body(i, last_pair):
                def mul_pads(x, p0, p1):
                    for h in range(2):
                        r = slice(HEAD * h, HEAD * h + HEAD)
                        last = dve.tensor_tensor(pads[x][r, :, C * h:C * h + C],
                                                 p0[r, :].rearrange("p (c t) -> p c t", c=NCH),
                                                 p1[r, :].rearrange("p (c t) -> p c t", c=NCH), ALU.mult)
                    return last

                def shifted(x, slot, mu, out):
                    dve.wait_ge(copied.sem, copied.of(i, x))
                    dve.wait_ge(rows_in.sem, rows_in.of(i, x))
                    shift(dve, zx[:, slot, :], par[:, i, mu:mu + 1], out).then_inc(v_s.step("sh_" + x), 1)
                    dve.drain()

                shifted("r", 0, 0, rs)
                shifted("k", 1, 1, ks)
                dve.tensor_scalar(kk[:, :], ks[:, :], par[:, i, 5:6], None, ALU.mult)
                dve.drain()
                dve.tensor_tensor(ksq[:, :], kk[:, :], kk[:, :], ALU.mult).then_inc(v_s.step("ksq"), 1)
                dve.drain()
                shifted("v", 2, 2, vs)
                dve.wait_ge(a_s.sem, a_s.of(i, "sg"))
                dve.tensor_tensor_scan(cs[:, :], one0[:, :], sg[:, :], 0.0, ALU.mult, ALU.add)
                dve.drain()
                dve.tensor_tensor(cse[:, :], cs[:, :], sg[:, :], ALU.subtract).then_inc(v_s.step("cse"), 1)
                dve.drain()
                dve.wait_ge(pe_s.sem, pe_s.of(i, "ss"))
                dve.tensor_scalar(halves(rk[:, :]), Z[0], 1e-24, None, ALU.max).then_inc(v_s.step("max"), 1)
                dve.drain()
                dve.wait_ge(a_s.sem, a_s.of(i, "at"))
                dve.tensor_scalar(bb[:, :], at[:, :], 1.0, par[:, i, 6:7], ALU.subtract, ALU.mult)
                dve.drain()
                dve.scalar_tensor_tensor(out=kf[:, :], in0=bb[:, :], scalar=1.0, in1=ks[:, :],
                                         op0=ALU.add, op1=ALU.mult)
                dve.drain()
                dve.scalar_tensor_tensor(out=dif[:, :], in0=rs[:, :], scalar=par[:, i, 7:8], in1=kf[:, :],
                                         op0=ALU.mult, op1=ALU.mult).then_inc(v_s.step("rp"), 1)
                dve.drain()
                dve.wait_ge(a_s.sem, a_s.of(i, "rkk"))
                dve.tensor_tensor(kk[:, :], kk[:, :], rk[:, :], ALU.mult)
                dve.drain()
                dve.tensor_tensor(bb[:, :], kk[:, :], at[:, :], ALU.mult).then_inc(v_s.step("b"), 1)
                dve.drain()
                dve.wait_ge(a_s.sem, a_s.of(i, "exp"))
                mul_pads("p", kk, cse)
                mul_pads("q", rs, winc).then_inc(v_s.step("pq"), 1)
                dve.drain()
                for c in range(NCH):
                    kind = c // (NCH - 1)
                    dve.wait_ge(pe_s.sem, pe_s.of(i, f"x{c}"))
                    if kind == 0:
                        dve.tensor_tensor(off[:, c, :], X[c % 2][:, 0:P], moff[:, :], ALU.mult)
                    dve.tensor_tensor(xm[:, c, :, :], X[c % 2].rearrange("p (a b) -> p a b", a=4),
                                      mask[:, kind, :, :], ALU.mult).then_inc(v_s.step(f"mx{c}"), 1)
                    dve.drain()
                    dve.wait_ge(pe_s.sem, pe_s.of(i, f"t{c}"))
                    dve.tensor_tensor(low[:, c, :], X[2 + c % 2][:, 0:P], mlow[:, kind, :], ALU.mult)\
                        .then_inc(v_s.step(f"mt{c}"), 1)
                dve.drain()
                eye = ident[:, :].unsqueeze(1)
                for g, cc in enumerate(groups):
                    dve.scalar_tensor_tensor(out=ilow[:, :, :], in0=low[:, cc[0]:cc[-1] + 1, :], scalar=-1.0,
                                             in1=eye.broadcast_to([P, GRP, P]), op0=ALU.mult, op1=ALU.add)\
                        .then_inc(v_s.step(f"il{g}"), 1)
                    dve.drain()
                    for n, (name, _, _, to, plus, minus) in enumerate(plan):
                        if plus or minus:
                            src = X[(g * len(plan) + n) % 4][:, 0:GRP * P].rearrange("p (a b) -> p a b", a=GRP)
                            if to:
                                src = mats[to][:, :, :]
                                dve.wait_ge(a_s.sem, a_s.of(i, f"{g}_{name}"))
                            else:
                                dve.wait_ge(pe_s.sem, pe_s.of(i, f"{g}_{name}"))
                            dve.scalar_tensor_tensor(out=mats[plus or minus][:, :, :], in0=src,
                                                     scalar=1.0 if plus else -1.0,
                                                     in1=eye.broadcast_to([P, GRP, P]), op0=ALU.mult, op1=ALU.add)\
                                                         .then_inc(v_s.step(f"{g}_{name}"), 1)
                            dve.drain()
                dve.wait_ge(stored, 48 * i + 48)
                for c in range(NCH - 1):
                    dve.wait_ge(pe_s.sem, pe_s.of(i, f"R{c}"))
                    dve.tensor_scalar(rn[:, :], X[0][:, 0:HEAD], -1.0, None, ALU.mult).then_inc(v_s.step(f"R{c}"), 1)
                    dve.drain()
                    dve.wait_ge(pe_s.sem, pe_s.of(i, f"U{c}"))
                    dve.tensor_copy(uu[:, :], X[1][:, 0:HEAD]).then_inc(v_s.step(f"U{c}"), 1)
                    dve.drain()
                    dve.wait_ge(pe_s.sem, pe_s.of(i, f"S{c}"))
                    end = C * c + C - 1
                    dve.tensor_scalar(st[:, (c + 1) % 2, :], X[3][:, 0:HEAD], winc[:, end:end + 1], None, ALU.mult)\
                        .then_inc(v_s.step(f"S{c}"), 1)
                    dve.drain()
                seq = mseq[:, :].unsqueeze(2).broadcast_to([P, NSEQ, HEAD])

                def own_rows(bank, out):
                    dve.tensor_tensor(big[:, :, :], bank.rearrange("p (b v) -> p b v", b=NSEQ), seq, ALU.mult)
                    dve.drain()
                    return dve.tensor_reduce(out[:, :], big[:, :, :].rearrange("p b v -> p v b"), AX.X, ALU.add)

                dve.wait_ge(pe_s.sem, pe_s.of(i, "sR"))
                own_rows(X[0], r1).then_inc(v_s.step("sR"), 1)
                dve.drain()
                dve.wait_ge(pe_s.sem, pe_s.of(i, "s8"))
                dve.scalar_tensor_tensor(out=rn[:, :], in0=X[1][:, 0:HEAD], scalar=-1.0, in1=r1[:, :],
                                         op0=ALU.mult, op1=ALU.subtract).then_inc(v_s.step("s8"), 1)
                dve.drain()
                dve.wait_ge(pe_s.sem, pe_s.of(i, "sY"))
                own_rows(X[2], y1).then_inc(v_s.step("sY"), 1)
                dve.drain()
                dve.wait_ge(pe_s.sem, pe_s.of(i, "sU"))
                dve.tensor_copy(uu[:, :], X[3][:, 0:HEAD]).then_inc(v_s.step("sU"), 1)
                dve.drain()
                for dst, src in ((um, uu[:, :]), (vm, tok[:, NCH - 1, 0:C])):
                    last = dve.tensor_tensor(dst[:, :, :], src.unsqueeze(1).broadcast_to([P, NSEQ, HEAD]), seq, ALU.mult)
                last.then_inc(v_s.step("sUm"), 1)
                dve.drain()
                dve.wait_ge(pe_s.sem, pe_s.of(i, "sV"))
                dve.tensor_tensor(yy[:, NCH - 1, :], X[1][:, 0:HEAD], y1[:, :], ALU.add).then_inc(v_s.step("sV"), 1)
                dve.drain()
                dve.wait_ge(pe_s.sem, pe_s.of(i, "sS"))
                last_w = winc[:, TP + LSEQ - 1:T:LSEQ].unsqueeze(2).broadcast_to([P, NSEQ, HEAD])
                dve.tensor_tensor(so[:, :, :], X[0].rearrange("p (b v) -> p b v", b=NSEQ), last_w, ALU.mult)\
                    .then_inc(v_s.step("sS"), 1)
                dve.drain()
                dve.wait_ge(a_s.sem, a_s.of(i, f"Y{NCH - 2}"))
                dve.tensor_reduce(gm[:, :], yy[:, :, :], AX.X, ALU.add)
                dve.drain()
                dve.tensor_scalar(gm[:, :], gm[:, :], 1.0 / HEAD, None, ALU.mult)
                dve.drain()
                gmb = gm[:, :].unsqueeze(2).broadcast_to([P, NCH, HEAD])
                dve.tensor_tensor(yy[:, :, :], yy[:, :, :], gmb, ALU.subtract)
                dve.drain()
                y2 = dif[:, :].rearrange("p (c v) -> p c v", c=NCH)
                dve.tensor_tensor(y2, yy[:, :, :], yy[:, :, :], ALU.mult)
                dve.drain()
                dve.tensor_reduce(gv[:, :], y2, AX.X, ALU.add)
                dve.drain()
                dve.tensor_scalar(gv[:, :], gv[:, :], 1.0 / HEAD, GN_EPS, ALU.mult, ALU.add).then_inc(v_s.step("var"), 1)
                dve.drain()
                dve.wait_ge(a_s.sem, a_s.of(i, "rstd"))
                for h in range(2):
                    r = slice(HEAD * h, HEAD * h + HEAD)
                    last = dve.tensor_tensor(ypad[r, :, HEAD * h:HEAD * h + HEAD], yy[r, :, :],
                                             gv[r, :].unsqueeze(2).broadcast_to([HEAD, NCH, HEAD]), ALU.mult)
                last.then_inc(v_s.step("ypad"), 1)
                dve.drain()
                dve.tensor_tensor(halves(ksq[:, :]), Z[1], halves(vs[:, :]), ALU.mult)
                dve.wait_ge(pe_s.sem, pe_s.of(i, "yT"))
                for b, lo, hi in ((0, 0, 5 * C), (1, 5 * C, T)):
                    dve.tensor_scalar(kk[:, lo:hi], K.ps[:, b, 0:hi - lo], par[:, i, 8:9], par[:, i, 9:10],
                                      ALU.mult, ALU.add)
                dve.drain()
                dve.tensor_tensor(kk[:, :], kk[:, :], ksq[:, :], ALU.add)
                dve.drain()
                dve.tensor_tensor(oo[:, :], kk[:, :], gg[:, :], ALU.mult).then_inc(v_s.step("oa"), 1)
                dve.drain()
            every_pair(dve, body)


def ret_stage(nc, K, a):
    with ExitStack() as ctx:
        def sb(name, shape):
            return ctx.enter_context(nc.sbuf_tensor("ret_" + name, shape, F32))

        def sem(name):
            return ctx.enter_context(nc.semaphore("ret_" + name))

        w4 = sb("w4", [P, 4, DC, P])
        wv = sb("wv", [P, DC, VH])
        con = sb("con", [P, RET_CON])
        cos, sin, perm = sb("cos", [P, T]), sb("sin", [P, T]), sb("perm", [P, P])
        qr, kr, tmp = sb("qr", [P, T]), sb("kr", [P, T]), sb("tmp", [P, T])
        qt, kt, qd = sb("qt", [P, T]), sb("kt", [P, T]), sb("qd", [P, T])
        vt = sb("vt", [P, NRC + 1, VH])
        sm = sb("sm", [P, NRC + 1, RC])
        kd = sb("kd", [P, NRC, P])
        kds = sb("kds", [TS, NSEQ, P])
        rst = sb("rst", [P, 2, VH])
        r0, rout = sb("r0", [P, NSEQ, VH]), sb("rout", [P, NSEQ, VH])
        ot, o2, gate, ob = (sb(x, [P, 2, T]) for x in ("ot", "o2", "gate", "ob"))
        rstd = sb("rstd", [P, T])
        qdec, dm, dms = con[:, 0:T], con[:, T:T + RC], con[0:TS, T + RC:T + RC + TS]
        o = T + RC + TS
        kdec, gc, gs, kdecs = con[:, o:o + 1], con[:, o + 1:o + 2], con[:, o + 2:o + 3], con[0:TS, o + 3:o + 3 + NSEQ]
        NT = NRC + 1
        pe_s = Steps(sem("tensor"), ["q", "k"] + [f"v{c}" for c in range(NT)] + ["swq", "swk", "g0", "g1"]
                     + [f"s{c}" for c in range(NT)] + [x for c in range(NRC) for x in (f"o{c}", f"R{c}")]
                     + [f"o{NRC}"] + [f"RS{p}" for p in range(4)] + ["ss"])
        v_s = Steps(sem("vector"), ["q", "k"] + [f"s{c}" for c in range(NT)] + [f"R{c}" for c in range(NRC)]
                    + [f"RS{p}" for p in range(4)] + ["ms", "ob"])
        a_s = Steps(sem("scalar"), ["q", "k"] + [f"v{c}" for c in range(NT)] + ["g0", "g1"]
                    + [f"o{c}" for c in range(NT)] + ["sq", "rstd"])
        wts = [sem("w_" + x) for x in ("q", "k", "g0", "g1")]
        wvs, cons, consts, r0s, stored = sem("w_v"), sem("head_consts"), sem("consts"), sem("state_in"), sem("stored")
        Z = [K.ps[:, 0:2, 0:HT], K.ps[:, 2:4, 0:HT]]
        X = [K.ps[:, 4 + b, :] for b in range(4)]

        def chunk(c):
            return slice(RC * c, RC * c + (RC if c < NRC else TS))

        block = ctx.enter_context(nc.Block())

        @block.sync
        def _(sp):
            for dst, src in ((cos, "c_cos"), (sin, "c_sin"), (perm, "c_perm")):
                sp.dma_start(dst[:, :], a[src]).then_inc(consts, 16)
            with sp.Fori(0, HB) as i:
                for t, x in enumerate(("q", "k", "g0", "g1")):
                    if x == "g0":
                        sp.wait_ge(pe_s.sem, pe_s.of(i, f"v{NRC}", 1))
                        sp.dma_start(wv[:, :, :], a["w_v"][i]).then_inc(wvs, 16)
                    sp.wait_ge(pe_s.sem, pe_s.of(i, x, 1))
                    sp.dma_start(w4[:, t, :, :], a["w_qkg"][i, t]).then_inc(wts[t], 16)
                sp.wait_ge(v_s.sem, v_s.of(i, "ms", 1))
                sp.dma_start(con[:, :], a["c_ret"][i]).then_inc(cons, 16)
                sp.dma_start(r0[:, :, :], a["ret_in"][i]).then_inc(r0s, 16)

        @block.tensor
        def _(pe):
            pe_s.ahead(pe)
            pe.wait_ge(consts, 48)
            with pe.Fori(0, HB) as i:
                def matrix(x, z):
                    t = ("q", "k", "g0", "g1").index(x)
                    pe.wait_ge(wts[t], 16 * i + 16)
                    project(pe, Z[z], w4[:, t, :, :], K.hn).then_inc(pe_s.step(x), 1)

                pe.wait_ge(v_s.sem, v_s.of(i, "ms", 1))
                matrix("q", 0)
                matrix("k", 1)
                pe.wait_ge(wvs, 16 * i + 16)
                for c in range(NT):
                    if c >= 2:
                        pe.wait_ge(a_s.sem, a_s.of(i, f"v{c - 2}"))
                    n = RC if c < NRC else TS
                    for d in range(DC):
                        last = pe.matmul(X[c % 2][0:n, 0:VH], K.hn[:, d, chunk(c)], wv[:, d, :],
                                         start=(d == 0), stop=(d == DC - 1))
                    last.then_inc(pe_s.step(f"v{c}"), 1)
                for x, z, src in (("q", 0, qr), ("k", 1, kr)):
                    pe.wait_ge(a_s.sem, a_s.of(i, x))
                    for h in range(2):
                        last = pe.matmul(Z[z][:, h, :], perm[:, :], src[:, h * HT:(h + 1) * HT], start=True, stop=True)
                    last.then_inc(pe_s.step("sw" + x), 1)
                pe.wait_ge(v_s.sem, v_s.of(i, "q"))
                matrix("g0", 0)
                pe.wait_ge(v_s.sem, v_s.of(i, "k"))
                matrix("g1", 1)
                for c in range(NT):
                    if c >= 2:
                        pe.wait_ge(v_s.sem, v_s.of(i, f"s{c - 2}"))
                    n = RC if c < NRC else TS
                    pe.matmul(X[2 + c % 2][0:n, 0:n], kt[:, chunk(c)], qt[:, chunk(c)], start=True, stop=True)
                    pe.transpose(X[2 + c % 2][0:n, RC:RC + P], kt[:, chunk(c)], K.ident[:, :])\
                        .then_inc(pe_s.step(f"s{c}"), 1)
                for c in range(NRC):
                    pe.wait_ge(v_s.sem, v_s.of(i, f"R{c - 1}" if c else f"s{NRC}"))
                    pe.wait_ge(a_s.sem, a_s.of(i, f"o{c - 1}" if c else f"v{NRC}"))
                    for h in range(2):
                        y = X[0][:, RC * h:RC * h + RC]
                        last = pe.matmul(y, vt[:, c, P * h:P * h + P], sm[:, c, :], start=True, stop=(c == 0))
                        if c:
                            last = pe.matmul(y, rst[:, c % 2, P * h:P * h + P], qd[:, chunk(c)], start=False, stop=True)
                    last.then_inc(pe_s.step(f"o{c}"), 1)
                    pe.matmul(X[1][:, 0:VH], kd[:, c, :], vt[:, c, :], start=True, stop=True)\
                        .then_inc(pe_s.step(f"R{c}"), 1)
                pe.wait_ge(a_s.sem, a_s.of(i, f"o{NRC - 1}"))
                pe.wait_ge(r0s, 16 * i + 16)
                for h in range(2):
                    y = X[0][:, TS * h:TS * h + TS]
                    pe.matmul(y, vt[0:TS, NRC, P * h:P * h + P], sm[0:TS, NRC, 0:TS], start=True, stop=False)
                    for b in range(NSEQ):
                        q = slice(TP + LSEQ * b, TP + LSEQ * b + LSEQ)
                        last = pe.matmul(y[:, LSEQ * b:LSEQ * b + LSEQ], r0[:, b, P * h:P * h + P], qd[:, q],
                                         start=False, stop=(b == NSEQ - 1))
                last.then_inc(pe_s.step(f"o{NRC}"), 1)
                for p in range(4):
                    pe.wait_ge(v_s.sem, v_s.of(i, f"R{NRC - 1}" if p < 3 else "RS0"))
                    for b in (2 * p, 2 * p + 1):
                        last = pe.matmul(X[1 + p % 3][:, VH * (b % 2):VH * (b % 2) + VH], kds[:, b, :],
                                         vt[0:TS, NRC, :], start=True, stop=True)
                    last.then_inc(pe_s.step(f"RS{p}"), 1)
                pe.wait_ge(a_s.sem, a_s.of(i, "sq"))
                for h in range(2):
                    for k in range(2):
                        last = pe.matmul(Z[0][:, h, :], K.ones[:, :], o2[:, k, h * HT:(h + 1) * HT],
                                         start=(k == 0), stop=(k == 1))
                last.then_inc(pe_s.step("ss"), 1)

        @block.scalar
        def _(act):
            a_s.ahead(act)
            act.sem_inc(stored, 48)
            with act.Fori(0, HB) as i:
                act.wait_ge(pe_s.sem, pe_s.of(i, "q"))
                act.copy(halves(qr[:, :]), Z[0]).then_inc(a_s.step("q"), 1)
                act.wait_ge(pe_s.sem, pe_s.of(i, "k"))
                act.activation(halves(kr[:, :]), Z[1], ACT.Copy, scale=float(P) ** -0.5).then_inc(a_s.step("k"), 1)
                for c in range(NT):
                    n = RC if c < NRC else TS
                    act.wait_ge(pe_s.sem, pe_s.of(i, f"v{c}"))
                    act.copy(vt[0:n, c, :], X[c % 2][0:n, 0:VH]).then_inc(a_s.step(f"v{c}"), 1)
                for h in range(2):
                    act.wait_ge(pe_s.sem, pe_s.of(i, f"g{h}"))
                    if h == 0:
                        act.wait_ge(v_s.sem, v_s.of(i, "ob", 1))
                    act.activation(halves(gate[:, h, :]), Z[h], ACT.Silu).then_inc(a_s.step(f"g{h}"), 1)
                for c in range(NT):
                    n = RC if c < NRC else TS
                    act.wait_ge(pe_s.sem, pe_s.of(i, f"o{c}"))
                    act.copy(ot[:, :, chunk(c)], X[0][:, 0:2 * n].rearrange("p (h t) -> p h t", h=2))\
                        .then_inc(a_s.step(f"o{c}"), 1)
                act.drain()
                act.activation(o2[:, :, :], ot[:, :, :], ACT.Square).then_inc(a_s.step("sq"), 1)
                act.wait_ge(v_s.sem, v_s.of(i, "ms"))
                act.activation(rstd[:, :], rstd[:, :], ACT.Ln)
                act.drain()
                act.activation(rstd[:, :], rstd[:, :], ACT.Exp, scale=-0.5).then_inc(a_s.step("rstd"), 1)
                act.wait_ge(v_s.sem, v_s.of(i, "ob"))
                act.dma_start(K.ob[i], ob[:, :, :]).then_inc(stored, 16)
                act.dma_start(a["ret_out"][i, :, 0, :], rst[:, NRC % 2, :]).then_inc(stored, 16)
                act.dma_start(a["ret_out"][i, :, 1:1 + NSEQ, :], rout[:, :, :]).then_inc(stored, 16)
            act.wait_ge(stored, 48 * HB + 48)

        @block.vector
        def _(dve):
            v_s.ahead(dve)
            dve.wait_ge(consts, 48)
            with dve.Fori(0, HB) as i:
                dve.wait_ge(cons, 16 * i + 16)
                for x, z, raw, out in (("q", 0, qr, qt), ("k", 1, kr, kt)):
                    dve.wait_ge(pe_s.sem, pe_s.of(i, "sw" + x))
                    dve.tensor_tensor(halves(tmp[:, :]), Z[z], halves(sin[:, :]), ALU.mult)
                    dve.tensor_tensor(out[:, :], raw[:, :], cos[:, :], ALU.mult)
                    dve.drain()
                    last = dve.tensor_tensor(out[:, :], out[:, :], tmp[:, :], ALU.add)
                    if x == "k":
                        last = dve.tensor_tensor(qd[:, :], qt[:, :], qdec, ALU.mult)
                    last.then_inc(v_s.step(x), 1)
                    dve.drain()
                for c in range(NT):
                    n = RC if c < NRC else TS
                    x = X[2 + c % 2]
                    dve.wait_ge(pe_s.sem, pe_s.of(i, f"s{c}"))
                    dve.tensor_tensor(sm[0:n, c, 0:n], x[0:n, 0:n], dm if c < NRC else dms, ALU.mult)
                    if c < NRC:
                        last = dve.tensor_scalar(kd[:, c, :], x[:, RC:RC + P], kdec, None, ALU.mult)
                    else:
                        last = dve.tensor_tensor(kds[:, :, :], x[0:n, RC:RC + P].unsqueeze(1).broadcast_to([TS, NSEQ, P]),
                                                 kdecs.unsqueeze(2).broadcast_to([TS, NSEQ, P]), ALU.mult)
                    last.then_inc(v_s.step(f"s{c}"), 1)
                dve.drain()
                dve.wait_ge(stored, 48 * i + 48)
                for c in range(NRC):
                    dve.wait_ge(pe_s.sem, pe_s.of(i, f"R{c}"))
                    if c == 0:
                        last = dve.tensor_copy(rst[:, 1, :], X[1][:, 0:VH])
                    else:
                        last = dve.scalar_tensor_tensor(out=rst[:, (c + 1) % 2, :], in0=rst[:, c % 2, :], scalar=gc,
                                                        in1=X[1][:, 0:VH], op0=ALU.mult, op1=ALU.add)
                    last.then_inc(v_s.step(f"R{c}"), 1)
                    dve.drain()
                for p in range(4):
                    dve.wait_ge(pe_s.sem, pe_s.of(i, f"RS{p}"))
                    dve.scalar_tensor_tensor(out=rout[:, 2 * p:2 * p + 2, :], in0=r0[:, 2 * p:2 * p + 2, :], scalar=gs,
                                             in1=X[1 + p % 3].rearrange("p (b v) -> p b v", b=2),
                                             op0=ALU.mult, op1=ALU.add).then_inc(v_s.step(f"RS{p}"), 1)
                dve.wait_ge(pe_s.sem, pe_s.of(i, "ss"))
                dve.tensor_scalar(halves(rstd[:, :]), Z[0], 1.0 / VH, EPS, ALU.mult, ALU.add)\
                    .then_inc(v_s.step("ms"), 1)
                dve.tensor_tensor(ob[:, :, :], ot[:, :, :], gate[:, :, :], ALU.mult)
                dve.drain()
                dve.wait_ge(a_s.sem, a_s.of(i, "rstd"))
                dve.tensor_tensor(ob[:, :, :], ob[:, :, :], rstd[:, :].unsqueeze(1).broadcast_to([P, 2, T]), ALU.mult)\
                    .then_inc(v_s.step("ob"), 1)
                dve.drain()


def merge_stage(nc, K, a, m):
    with ExitStack() as ctx:
        def sb(name, shape):
            return ctx.enter_context(nc.sbuf_tensor("mrg_" + name, shape, F32))

        def sem(name):
            return ctx.enter_context(nc.semaphore("mrg_" + name))

        oa, ob = sb("oa", [P, PAIRS, T]), sb("ob", [P, HB * 2, T])
        KT = {"ga": DC, "gb": DC, "pa": PAIRS, "pb": 2 * HB}
        acts = {"ga": K.hn, "gb": K.hn, "pa": oa, "pb": ob}
        w = {x: sb("w_" + x, [P, k, P]) for x, k in KT.items()}
        sa, s2 = sb("sa", [P, T]), sb("s2", [P, T])
        banks = {x: K.ps[:, 2 * n:2 * n + 2, 0:HT] for n, x in enumerate(KT)}
        pe_s = Steps(sem("tensor"), list(KT))
        v_s = Steps(sem("vector"), ["a", "m"])
        a_s = Steps(sem("scalar"), ["ga", "gb"])
        wt = {x: sem("w_" + x) for x in KT}
        loaded = sem("loaded")
        block = ctx.enter_context(nc.Block())

        @block.sync
        def _(sp):
            with sp.Fori(0, DC) as i:
                for x in KT:
                    sp.wait_ge(pe_s.sem, pe_s.of(i, x, 1))
                    sp.dma_start(w[x][:, :, :], a["w_" + x][i]).then_inc(wt[x], 16)

        @block.gpsimd
        def _(pool):
            pool.dma_start(oa[:, :, :], K.oa.rearrange("i p t -> p i t")).then_inc(loaded, 16)
            pool.dma_start(ob[:, :, :].rearrange("p (i h) t -> p i h t", h=2),
                           K.ob.rearrange("i p h t -> p i h t")).then_inc(loaded, 16)

        @block.tensor
        def _(pe):
            pe_s.ahead(pe)
            with pe.Fori(0, DC) as i:
                for x in KT:
                    pe.wait_ge(wt[x], 16 * i + 16)
                    if x in ("ga", "gb"):
                        pe.wait_ge(a_s.sem, a_s.of(i, x, 1))
                    else:
                        pe.wait_ge(loaded, 32)
                        pe.wait_ge(v_s.sem, v_s.of(i, "a" if x == "pa" else "m", 1))
                    project(pe, banks[x], w[x], acts[x], KT[x]).then_inc(pe_s.step(x), 1)

        @block.scalar
        def _(act):
            a_s.ahead(act)
            with act.Fori(0, DC) as i:
                for x, s in (("ga", sa), ("gb", s2)):
                    act.wait_ge(pe_s.sem, pe_s.of(i, x))
                    act.wait_ge(v_s.sem, v_s.of(i, "m", 1))
                    act.activation(halves(s[:, :]), banks[x], ACT.Sigmoid).then_inc(a_s.step(x), 1)

        @block.vector
        def _(dve):
            v_s.ahead(dve)
            with dve.Fori(0, DC) as i:
                for x, s, step in (("pa", sa, "a"), ("pb", s2, None)):
                    dve.wait_ge(pe_s.sem, pe_s.of(i, x))
                    dve.wait_ge(a_s.sem, a_s.of(i, "g" + x[1]))
                    last = dve.tensor_tensor(halves(s[:, :]), halves(s[:, :]), banks[x], ALU.mult)
                    if step:
                        last.then_inc(v_s.step(step), 1)
                    dve.drain()
                dve.tensor_tensor(m[:, i, :], sa[:, :], s2[:, :], ALU.add).then_inc(v_s.step("m"), 1)
                dve.drain()


def out_stage(nc, K, a, m, x1):
    with ExitStack() as ctx:
        def sem(name):
            return ctx.enter_context(nc.semaphore("out_" + name))

        w = ctx.enter_context(nc.sbuf_tensor("out_w", [P, 2, DC, P], F32))
        pe_s, v_s = Steps(sem("tensor"), ["0", "1"]), Steps(sem("vector"), ["0", "1"])
        wt, loaded = [sem("w0"), sem("w1")], sem("loaded")
        block = ctx.enter_context(nc.Block())

        @block.sync
        def _(sp):
            with sp.Fori(0, DC // 2) as i:
                for u in range(2):
                    sp.wait_ge(pe_s.sem, pe_s.of(i, str(u), 1))
                    sp.dma_start(w[:, u, :, :], a["w_out"][2 * i + u]).then_inc(wt[u], 16)

        @block.scalar
        def _(act):
            act.dma_start(x1[:, :, :], a["x"]).then_inc(loaded, 16)

        @block.tensor
        def _(pe):
            pe_s.ahead(pe)
            with pe.Fori(0, DC // 2) as i:
                for u in range(2):
                    pe.wait_ge(wt[u], 16 * i + 16)
                    pe.wait_ge(v_s.sem, v_s.of(i, str(u), 1))
                    project(pe, K.ps[:, 2 * u:2 * u + 2, 0:HT], w[:, u, :, :], m).then_inc(pe_s.step(str(u)), 1)

        @block.vector
        def _(dve):
            v_s.ahead(dve)
            dve.wait_ge(loaded, 16)
            with dve.Fori(0, DC // 2) as i:
                for u in range(2):
                    dve.wait_ge(pe_s.sem, pe_s.of(i, str(u)))
                    x = halves(x1[:, 2 * i + u, :])
                    dve.tensor_tensor(x, x, K.ps[:, 2 * u:2 * u + 2, 0:HT], ALU.add).then_inc(v_s.step(str(u)), 1)


def route_stage(nc, K, a, top_v, top_i):
    with ExitStack() as ctx:
        def sb(name, shape, dt=F32):
            return ctx.enter_context(nc.sbuf_tensor("rt_" + name, shape, dt))

        def sem(name):
            return ctx.enter_context(nc.semaphore("rt_" + name))

        w = sb("w", [P, DC, P])
        wh, wl = sb("wh", [P, 2, DC, P], F32R), sb("wl", [P, 2, DC, P], F32R)
        keys = sb("keys", [P, 2 * PH, NK])
        qt = sb("qt", [P, 2, T])
        sc = sb("sc", [P, 2, NTT, NK])
        s2 = sb("s2", [P, NTT, NK])
        val, idx = sb("val", [P, NTT, TOPK]), sb("idx", [P, NTT, TOPK], U32)
        pe_s = Steps(sem("tensor"), ["q0", "q1", "s0", "s1"])
        a_s = Steps(sem("scalar"), ["q0", "w0", "q1", "w1", "s0", "s1"])
        v_s = Steps(sem("vector"), ["w0", "w1", "met0", "0", "met1", "1"])
        wt, loaded, zeroed, first = sem("w"), sem("keys_in"), sem("zeroed"), sem("first_parts")
        block = ctx.enter_context(nc.Block())

        @block.sync
        def _(sp):
            sp.dma_start(keys[:, :, :], a["keys"]).then_inc(loaded, 16)
            sp.dma_start(w[:, :, :], a["w_q"][0]).then_inc(wt, 16)
            sp.wait_ge(first, 2)
            sp.dma_start(w[:, :, :], a["w_q"][1]).then_inc(wt, 16)
            with sp.Fori(0, PH - 1) as i:
                for u in range(2):
                    sp.wait_ge(v_s.sem, v_s.of(i, "w1", 1) if u == 0 else v_s.of(i, "w0"))
                    sp.dma_start(w[:, :, :], a["w_q"][2 * i + 2 + u]).then_inc(wt, 16)

        def every_turn(eng, body):
            with eng.Fori(0, PH - 1) as i:
                body(i, False)
            body(PH - 1, True)

        @block.gpsimd
        def _(pool):
            pool.memset(sc[:, :, NTT - 1, :], 0.0).then_inc(zeroed, 1)

        @block.tensor
        def _(pe):
            pe_s.ahead(pe)
            pe.wait_ge(loaded, 16)
            with pe.Fori(0, PH) as i:
                for u in range(2):
                    pe.wait_ge(v_s.sem, v_s.of(i, f"w{u}", 1))
                    pe.wait_ge(a_s.sem, a_s.of(i, f"q{u}", 1))
                    project3(pe, K.ps[:, 2 * u:2 * u + 2, 0:HT], wh[:, u, :, :], wl[:, u, :, :], K.hh, K.hl)\
                        .then_inc(pe_s.step(f"q{u}"), 1)
                for u in range(2):
                    pe.wait_ge(a_s.sem, a_s.last(i, [f"q{u}"]) if u else a_s.of(i, "q1"))
                    for n in range(NTT):
                        m = P if n < NTT - 1 else TS
                        last = pe.matmul(K.ps[0:m, 4 + 2 * u + n // 4, NK * (n % 4):NK * (n % 4) + NK],
                                         qt[:, u, P * n:P * n + m], keys[:, 2 * i + u, :], start=True, stop=True)
                    last.then_inc(pe_s.step(f"s{u}"), 1)

        @block.scalar
        def _(act):
            a_s.ahead(act)
            act.wait_ge(zeroed, 1)
            act.wait_ge(wt, 16)
            act.copy(wh[:, 0, :, :], w[:, :, :]).then_inc(first, 1)
            act.wait_ge(wt, 32)
            act.copy(wh[:, 1, :, :], w[:, :, :]).then_inc(first, 1)

            def body(i, last):
                for u in range(2):
                    act.wait_ge(pe_s.sem, pe_s.of(i, f"q{u}"))
                    act.copy(halves(qt[:, u, :]), K.ps[:, 2 * u:2 * u + 2, 0:HT]).then_inc(a_s.step(f"q{u}"), 1)
                    if last:
                        act.drain().then_inc(a_s.step(f"w{u}"), 1)
                    else:
                        act.wait_ge(wt, 32 * i + 16 * u + 48)
                        act.copy(wh[:, u, :, :], w[:, :, :]).then_inc(a_s.step(f"w{u}"), 1)
                for u in range(2):
                    act.wait_ge(pe_s.sem, pe_s.of(i, f"s{u}"))
                    act.wait_ge(v_s.sem, v_s.of(i, str(u), 1))
                    act.copy(sc[:, u, 0:4, :], K.ps[:, 4 + 2 * u, :].rearrange("p (n k) -> p n k", n=4))
                    act.copy(sc[0:TS, u, 4, :], K.ps[0:TS, 5 + 2 * u, 0:NK]).then_inc(a_s.step(f"s{u}"), 1)
            every_turn(act, body)

        @block.vector
        def _(dve):
            dve.wait_ge(first, 1)
            dve.tensor_tensor(wl[:, 0, :, :], w[:, :, :], wh[:, 0, :, :].bitcast(F32), ALU.subtract).then_inc(first, 1)
            dve.wait_ge(first, 3)
            dve.tensor_tensor(wl[:, 1, :, :], w[:, :, :], wh[:, 1, :, :].bitcast(F32), ALU.subtract)
            dve.drain()
            v_s.ahead(dve)

            def body(i, last):
                for u in range(2):
                    if last:
                        dve.drain().then_inc(v_s.step(f"w{u}"), 1)
                    else:
                        dve.wait_ge(a_s.sem, a_s.of(i, f"w{u}"))
                        dve.tensor_tensor(wl[:, u, :, :], w[:, :, :], wh[:, u, :, :].bitcast(F32), ALU.subtract)\
                            .then_inc(v_s.step(f"w{u}"), 1)
                for u in range(2):
                    dve.drain()
                    dve.wait_ge(a_s.sem, a_s.of(i, f"s{u}"))
                    dve.sem_inc(v_s.step(f"met{u}"), 1)
                    for n in range(NTT):
                        dve.max(val[:, n, 0:8], sc[:, u, n, :])
                    dve.drain()
                    for n in range(NTT):
                        dve.max_index(idx[:, n, 0:8], val[:, n, 0:8], sc[:, u, n, :])
                        dve.match_replace(s2[:, n, :], val[:, n, 0:8], sc[:, u, n, :], LEAST)
                    dve.drain()
                    for n in range(NTT):
                        dve.max(val[:, n, 8:16], s2[:, n, :])
                    dve.drain()
                    for n in range(NTT):
                        dve.max_index(idx[:, n, 8:16], val[:, n, 8:16], s2[:, n, :])
                    dve.drain()
                    dve.tensor_copy(top_v[:, :, 2 * i + u, :], val[:, :, :])
                    dve.tensor_copy(top_i[:, :, 2 * i + u, :], idx[:, :, :]).then_inc(v_s.step(str(u)), 1)
                    dve.drain()
            every_turn(dve, body)


def pick_stage(nc, K, a, top_v, top_i, slots):
    with ExitStack() as ctx:
        def sb(name, shape, dt=F32):
            return ctx.enter_context(nc.sbuf_tensor("pk_" + name, shape, dt))

        def sem(name):
            return ctx.enter_context(nc.semaphore("pk_" + name))

        cand, cand2, eq = (sb(x, [P, PH, TOPK * TOPK]) for x in ("cand", "cand2", "eq"))
        flat, pos = sb("flat", [P, PH, TOPK], U32), sb("pos", [P, 2, PH, TOPK], U32)
        posf, best = sb("posf", [P, 2, PH, TOPK]), sb("best", [P, PH, TOPK])
        ids = sb("ids", [P, 3, PH, TOPK])
        total = sb("total", [P, PH])
        iota = sb("iota", [P, TOPK])
        pe_s, a_s = Steps(sem("tensor"), ["t"]), Steps(sem("scalar"), ["e", "t"])
        v_s = Steps(sem("vector"), ["d", "ids"])
        loaded = sem("iota_in")
        block = ctx.enter_context(nc.Block())

        @block.sync
        def _(sp):
            sp.dma_start(iota[:, :], a["c_iota"][:, 0:TOPK]).then_inc(loaded, 16)

        @block.vector
        def _(dve):
            v_s.ahead(dve)
            dve.wait_ge(loaded, 16)
            with dve.Fori(0, NTT) as i:
                dve.wait_ge(pe_s.sem, pe_s.of(i, "t", 1))
                dve.tensor_tensor(cand[:, :, :].rearrange("p h (x y) -> p h x y", x=TOPK),
                                  top_v[:, i, 0:2 * PH:2, :].unsqueeze(3).broadcast_to([P, PH, TOPK, TOPK]),
                                  top_v[:, i, 1:2 * PH:2, :].unsqueeze(2).broadcast_to([P, PH, TOPK, TOPK]), ALU.add)
                dve.drain()
                for h in range(PH):
                    dve.max(best[:, h, 0:8], cand[:, h, :])
                dve.drain()
                for h in range(PH):
                    dve.max_index(flat[:, h, 0:8], best[:, h, 0:8], cand[:, h, :])
                    dve.match_replace(cand2[:, h, :], best[:, h, 0:8], cand[:, h, :], LEAST)
                dve.drain()
                for h in range(PH):
                    dve.max(best[:, h, 8:16], cand2[:, h, :])
                dve.drain()
                for h in range(PH):
                    dve.max_index(flat[:, h, 8:16], best[:, h, 8:16], cand2[:, h, :])
                gate = ids[:, 2, :, :]
                dve.tensor_tensor(gate, best[:, :, :], best[:, :, 0:1].broadcast_to([P, PH, TOPK]), ALU.subtract)\
                    .then_inc(v_s.step("d"), 1)
                dve.drain()
                dve.tensor_scalar(pos[:, 0, :, :], flat[:, :, :], 4, None, ALU.logical_shift_right)
                dve.tensor_scalar(pos[:, 1, :, :], flat[:, :, :], 15, None, ALU.bitwise_and)
                dve.drain()
                dve.tensor_copy(posf[:, :, :, :], pos[:, :, :, :])
                dve.drain()
                for s in range(2):
                    e = eq[:, :, :].rearrange("p h (x y) -> p h x y", x=TOPK)
                    dve.tensor_tensor(e, posf[:, s, :, :].unsqueeze(3).broadcast_to([P, PH, TOPK, TOPK]),
                                      iota[:, :].unsqueeze(1).unsqueeze(1).broadcast_to([P, PH, TOPK, TOPK]),
                                      ALU.is_equal)
                    dve.drain()
                    dve.tensor_tensor(e, e, top_i[:, i, s:2 * PH:2, :].unsqueeze(2)
                                      .broadcast_to([P, PH, TOPK, TOPK]), ALU.mult)
                    dve.drain()
                    dve.tensor_reduce(ids[:, s, :, :], e, AX.X, ALU.add)
                    dve.drain()
                dve.wait_ge(a_s.sem, a_s.of(i, "e"))
                dve.tensor_reduce(total[:, :], gate, AX.X, ALU.add)
                dve.drain()
                dve.reciprocal(total[:, :], total[:, :])
                dve.drain()
                dve.tensor_tensor(gate, gate, total[:, :].unsqueeze(2).broadcast_to([P, PH, TOPK]), ALU.mult)\
                    .then_inc(v_s.step("ids"), 1)
                dve.drain()

        @block.scalar
        def _(act):
            a_s.ahead(act)
            with act.Fori(0, NTT) as i:
                act.wait_ge(v_s.sem, v_s.of(i, "d"))
                act.activation(ids[:, 2, :, :], ids[:, 2, :, :], ACT.Exp).then_inc(a_s.step("e"), 1)
                act.wait_ge(pe_s.sem, pe_s.of(i, "t"))
                act.copy(slots[:, :, bass.ds(P * i, P)], K.ps[:, 0, 0:3 * P].rearrange("p (s t) -> p s t", s=3))\
                    .then_inc(a_s.step("t"), 1)

        @block.tensor
        def _(pe):
            pe_s.ahead(pe)
            with pe.Fori(0, NTT) as i:
                pe.wait_ge(v_s.sem, v_s.of(i, "ids"))
                pe.wait_ge(a_s.sem, a_s.of(i, "t", 1))
                for s in range(3):
                    last = pe.transpose(K.ps[:, 0, P * s:P * s + P], ids[:, s, :, :].rearrange("p h k -> p (h k)"),
                                        K.ident[:, :])
                last.then_inc(pe_s.step("t"), 1)


def gates_stage(nc, K, a, slots):
    with ExitStack() as ctx:
        def sb(name, shape):
            return ctx.enter_context(nc.sbuf_tensor("gt_" + name, shape, F32))

        def sem(name):
            return ctx.enter_context(nc.semaphore("gt_" + name))

        iota = sb("iota", [P, P])
        hot = sb("hot", [P, 2, 16, P])
        rows = sb("rows", [P, 16, P])
        stage = sb("stage", [P, 2, ROWS, TC])
        Q = ["0", "1", "2", "3"]
        pe_s, a_s = Steps(sem("tensor"), Q), Steps(sem("scalar"), Q)
        v_s, p_s = Steps(sem("vector"), Q), Steps(sem("pool"), Q)
        loaded, stored = sem("iota_in"), [sem("stored0"), sem("stored1")]
        PER = TC // 16
        NST = T // TC // 2
        block = ctx.enter_context(nc.Block())

        @block.sync
        def _(sp):
            sp.dma_start(iota[:, :], a["c_iota"]).then_inc(loaded, 16)
            for b in range(2):
                sp.sem_inc(stored[b], 16)
            with sp.Fori(0, NST) as s:
                for b in range(2):
                    sp.wait_ge(a_s.sem, a_s.of((2 * s + b) * PER + PER - 1, "3"))
                    sp.dma_start(K.gates[:, 2 * s + b, :, :], stage[:, b, :, :]).then_inc(stored[b], 16)
            for b in range(2):
                sp.wait_ge(stored[b], 16 * NST + 16)

        def turns(eng, body):
            with eng.Fori(0, NST) as s:
                for b in range(2):
                    with eng.Fori(0, PER) as q:
                        body((2 * s + b) * PER + q, s, b, q)

        @block.vector
        def _(dve):
            v_s.ahead(dve)
            dve.wait_ge(loaded, 16)

            def body(i, s, b, q):
                for g in range(4):
                    t = slice(4 * g, 4 * g + 4)
                    dve.wait_ge(pe_s.sem, pe_s.of(i, Q[g], 1))
                    dve.tensor_tensor(hot[:, :, t, :], iota[:, :].unsqueeze(1).unsqueeze(1).broadcast_to([P, 2, 4, P]),
                                      slots[:, 0:2, bass.ds(16 * i + 4 * g, 4)].unsqueeze(3)
                                      .broadcast_to([P, 2, 4, P]), ALU.is_equal).then_inc(v_s.step(Q[g]), 1)
            turns(dve, body)

        @block.gpsimd
        def _(pool):
            p_s.ahead(pool)

            def body(i, s, b, q):
                for g in range(4):
                    t = slice(4 * g, 4 * g + 4)
                    pool.wait_ge(v_s.sem, v_s.of(i, Q[g]))
                    pool.tensor_tensor(rows[:, t, :], hot[:, 0, t, :], slots[:, 2, bass.ds(16 * i + 4 * g, 4)]
                                       .unsqueeze(2).broadcast_to([P, 4, P]), ALU.mult).then_inc(p_s.step(Q[g]), 1)
            turns(pool, body)

        @block.tensor
        def _(pe):
            pe_s.ahead(pe)

            def body(i, s, b, q):
                for g in range(4):
                    pe.wait_ge(p_s.sem, p_s.of(i, Q[g]))
                    pe.wait_ge(a_s.sem, a_s.of(i, Q[g], 1))
                    for t in range(4):
                        last = pe.matmul(K.ps[:, g, P * t:P * t + P], hot[:, 1, 4 * g + t, :], rows[:, 4 * g + t, :],
                                         start=True, stop=True)
                    last.then_inc(pe_s.step(Q[g]), 1)
            turns(pe, body)

        @block.scalar
        def _(act):
            a_s.ahead(act)

            def body(i, s, b, q):
                act.wait_ge(stored[b], 16 * s + 16)
                for g in range(4):
                    act.wait_ge(pe_s.sem, pe_s.of(i, Q[g]))
                    act.copy(stage[:, b, :, bass.ds(16 * q + 4 * g, 4)].rearrange("p i t -> p t i"),
                             K.ps[:, g, :].rearrange("p (t i) -> p t i", t=4)).then_inc(a_s.step(Q[g]), 1)
            turns(act, body)


def experts_stage(nc, K, a, x1):
    R = 2
    with ExitStack() as ctx:
        def sb(name, shape, dt=F32):
            return ctx.enter_context(nc.sbuf_tensor("ex_" + name, shape, dt))

        def sem(name):
            return ctx.enter_context(nc.semaphore("ex_" + name))

        u, uh, ul = sb("u", [P, DC, P]), sb("uh", [P, R, DC, P], F32R), sb("ul", [P, R, DC, P], F32R)
        v, vh, vl = sb("v", [P, DC, P]), sb("vh", [P, R, DC, P], F32R), sb("vl", [P, R, DC, P], F32R)
        g, h = sb("g", [P, R, T]), sb("h", [P, R, T])
        hh, hl = sb("hh", [P, R, T], F32R), sb("hl", [P, R, T], F32R)
        V = [f"V{d}" for d in range(DC)]
        pe_s = Steps(sem("tensor"), ["U1", "U0"] + V)
        a_s = Steps(sem("scalar"), ["v0", "u0", "gelu1", "h1", "v1", "u1", "gelu0", "h0"])
        v_s = Steps(sem("vector"), ["v0", "u0", "gate1", "h1", "v1", "u1", "gate0"] + V + ["h0"])
        us, vs, gs = sem("u_in"), sem("v_in"), [sem("gates_in0"), sem("gates_in1")]
        first = sem("first")
        Z = [K.ps[:, 2 * n:2 * n + 2, 0:HT] for n in range(4)]
        N = ROWS // R
        block = ctx.enter_context(nc.Block())

        def by_stage(r):
            return g[:, r, :].rearrange("p (s t) -> p s t", t=TC)

        def every_turn(eng, body):
            with eng.Fori(0, N - 1) as i:
                body(i, False)
            body(N - 1, True)

        @block.sync
        def _(sp):
            sp.dma_start(u[:, :, :], a["peer_u"][0]).then_inc(us, 16)
            sp.dma_start(by_stage(0), K.gates[:, :, 0, :]).then_inc(gs[0], 16)
            sp.wait_ge(first, 2)
            sp.dma_start(u[:, :, :], a["peer_u"][1]).then_inc(us, 16)

            def body(i, last):
                sp.wait_ge(v_s.sem, v_s.of(i, "v1", 1))
                sp.dma_start(v[:, :, :], a["peer_v"][R * i]).then_inc(vs, 16)
                sp.wait_ge(v_s.sem, v_s.of(i, "gate1", 1))
                sp.dma_start(by_stage(1), K.gates[:, :, R * i + 1, :]).then_inc(gs[1], 16)
                if not last:
                    sp.wait_ge(v_s.sem, v_s.of(i, "u1", 1))
                    sp.dma_start(u[:, :, :], a["peer_u"][R * i + 2]).then_inc(us, 16)
                sp.wait_ge(v_s.sem, v_s.of(i, "v0"))
                sp.dma_start(v[:, :, :], a["peer_v"][R * i + 1]).then_inc(vs, 16)
                if not last:
                    sp.wait_ge(v_s.sem, v_s.of(i, "u0"))
                    sp.dma_start(u[:, :, :], a["peer_u"][R * i + 3]).then_inc(us, 16)
                    sp.wait_ge(v_s.sem, v_s.of(i, "gate0", 1))
                    sp.dma_start(by_stage(0), K.gates[:, :, R * i + 2, :]).then_inc(gs[0], 16)
            every_turn(sp, body)

        @block.tensor
        def _(pe):
            pe_s.ahead(pe)
            pe.wait_ge(first, 2)
            project3(pe, Z[0], uh[:, 0, :, :], ul[:, 0, :, :], K.hh, K.hl).then_inc(first, 1)

            def body(i, last):
                pe.wait_ge(v_s.sem, v_s.of(i, "u1", 1))
                pe.wait_ge(a_s.sem, a_s.of(i, "gelu1", 1))
                project3(pe, Z[1], uh[:, 1, :, :], ul[:, 1, :, :], K.hh, K.hl).then_inc(pe_s.step("U1"), 1)
                if last:
                    pe.drain().then_inc(pe_s.step("U0"), 1)
                else:
                    pe.wait_ge(v_s.sem, v_s.of(i, "u0"))
                    pe.wait_ge(a_s.sem, a_s.of(i, "gelu0", 1))
                    project3(pe, Z[0], uh[:, 0, :, :], ul[:, 0, :, :], K.hh, K.hl).then_inc(pe_s.step("U0"), 1)
                for d in range(DC):
                    pe.wait_ge(v_s.sem, v_s.of(i, V[d - 2]) if d >= 2 else v_s.of(i, "v1"))
                    z = Z[2 + d % 2]
                    for r in range(R):
                        for n in range(2):
                            t = slice(n * HT, (n + 1) * HT)
                            pe.matmul(z[:, n, :], vh[:, r, d, :], hh[:, r, t], start=(r == 0), stop=False)
                            pe.matmul(z[:, n, :], vh[:, r, d, :], hl[:, r, t], start=False, stop=False)
                        for n in range(2):
                            t = slice(n * HT, (n + 1) * HT)
                            done = pe.matmul(z[:, n, :], vl[:, r, d, :], hh[:, r, t], start=False, stop=(r == R - 1))
                    done.then_inc(pe_s.step(V[d]), 1)
            every_turn(pe, body)

        @block.scalar
        def _(act):
            a_s.ahead(act)
            act.wait_ge(us, 16)
            act.copy(uh[:, 0, :, :], u[:, :, :]).then_inc(first, 1)
            act.wait_ge(us, 32)
            act.copy(uh[:, 1, :, :], u[:, :, :]).then_inc(us, 1)
            act.wait_ge(first, 3)
            act.activation(halves(h[:, 0, :]), Z[0], ACT.Gelu).then_inc(first, 1)
            act.wait_ge(first, 5)
            act.copy(hh[:, 0, :], h[:, 0, :]).then_inc(first, 1)

            def body(i, last):
                act.wait_ge(pe_s.sem, pe_s.of(i, V[-1], 1))
                act.wait_ge(vs, 32 * i + 16)
                act.copy(vh[:, 0, :, :], v[:, :, :]).then_inc(a_s.step("v0"), 1)
                if last:
                    act.drain().then_inc(a_s.step("u0"), 1)
                else:
                    act.wait_ge(us, 32 * i + 49)
                    act.copy(uh[:, 0, :, :], u[:, :, :]).then_inc(a_s.step("u0"), 1)
                act.wait_ge(pe_s.sem, pe_s.of(i, "U1"))
                act.activation(halves(h[:, 1, :]), Z[1], ACT.Gelu).then_inc(a_s.step("gelu1"), 1)
                act.wait_ge(v_s.sem, v_s.of(i, "gate1"))
                act.copy(hh[:, 1, :], h[:, 1, :]).then_inc(a_s.step("h1"), 1)
                act.wait_ge(vs, 32 * i + 32)
                act.copy(vh[:, 1, :, :], v[:, :, :]).then_inc(a_s.step("v1"), 1)
                if last:
                    return
                act.wait_ge(us, 32 * i + 65)
                act.copy(uh[:, 1, :, :], u[:, :, :]).then_inc(a_s.step("u1"), 1)
                act.wait_ge(pe_s.sem, pe_s.of(i, "U0"))
                act.activation(halves(h[:, 0, :]), Z[0], ACT.Gelu).then_inc(a_s.step("gelu0"), 1)
                act.wait_ge(v_s.sem, v_s.of(i, "gate0"))
                act.wait_ge(pe_s.sem, pe_s.of(i, V[-1]))
                act.copy(hh[:, 0, :], h[:, 0, :]).then_inc(a_s.step("h0"), 1)
            every_turn(act, body)

        @block.vector
        def _(dve):
            dve.wait_ge(first, 1)
            dve.tensor_tensor(ul[:, 0, :, :], u[:, :, :], uh[:, 0, :, :].bitcast(F32), ALU.subtract).then_inc(first, 1)
            dve.wait_ge(us, 33)
            dve.tensor_tensor(ul[:, 1, :, :], u[:, :, :], uh[:, 1, :, :].bitcast(F32), ALU.subtract)
            dve.wait_ge(first, 4)
            dve.wait_ge(gs[0], 16)
            dve.tensor_tensor(h[:, 0, :], h[:, 0, :], g[:, 0, :], ALU.mult).then_inc(first, 1)
            dve.wait_ge(first, 6)
            dve.tensor_tensor(hl[:, 0, :], h[:, 0, :], hh[:, 0, :].bitcast(F32), ALU.subtract)
            dve.drain()
            v_s.ahead(dve)

            def body(i, last):
                def low(name, out, src, high):
                    dve.wait_ge(a_s.sem, a_s.of(i, name))
                    dve.tensor_tensor(out, src, high.bitcast(F32), ALU.subtract).then_inc(v_s.step(name), 1)

                def gated(r, turns):
                    dve.wait_ge(a_s.sem, a_s.of(i, f"gelu{r}"))
                    dve.wait_ge(gs[r], 16 * turns + 16)
                    dve.tensor_tensor(h[:, r, :], h[:, r, :], g[:, r, :], ALU.mult).then_inc(v_s.step(f"gate{r}"), 1)

                low("v0", vl[:, 0, :, :], v[:, :, :], vh[:, 0, :, :])
                if last:
                    dve.drain().then_inc(v_s.step("u0"), 1)
                else:
                    low("u0", ul[:, 0, :, :], u[:, :, :], uh[:, 0, :, :])
                gated(1, i)
                low("h1", hl[:, 1, :], h[:, 1, :], hh[:, 1, :])
                low("v1", vl[:, 1, :, :], v[:, :, :], vh[:, 1, :, :])
                if last:
                    dve.drain().then_inc(v_s.step("u1"), 1)
                    dve.drain().then_inc(v_s.step("gate0"), 1)
                else:
                    low("u1", ul[:, 1, :, :], u[:, :, :], uh[:, 1, :, :])
                    gated(0, i + 1)
                for d in range(DC):
                    x = halves(x1[:, d, :])
                    dve.wait_ge(pe_s.sem, pe_s.of(i, V[d]))
                    dve.tensor_tensor(x, x, Z[2 + d % 2], ALU.add).then_inc(v_s.step(V[d]), 1)
                if not last:
                    low("h0", hl[:, 0, :], h[:, 0, :], hh[:, 0, :])
            every_turn(dve, body)


class Kit:
    pass


def constants():
    t = np.arange(C)
    h2, t2 = np.repeat([0, 1], C), np.tile(t, 2)
    same = h2[:, None] == h2[None, :]
    i, s = t2[:, None], t2[None, :]
    out = {}
    mask = np.zeros((P, 2, 4, P))
    b16, b8 = i // 16 == s // 16, i // LSEQ == s // LSEQ
    mask[:, 0, 0] = same & b16 & (i < s)
    mask[:, 0, 1] = same & (i < s)
    mask[:, 0, 2] = mask[:, 0, 3] = same & (i <= s)
    mask[:, 1, 0] = mask[:, 1, 1] = same & b8 & (i < s)
    mask[:, 1, 2] = mask[:, 1, 3] = same & b8 & (i <= s)
    out["c_mask"] = mask
    out["c_moff"] = same & ~b16 & (i < s)
    out["c_mlow"] = np.stack([same & b16 & (i > s), same & b8 & (i > s)], 1)
    out["c_mseq"] = t2[:, None] // LSEQ == np.arange(NSEQ)[None, :]
    one0 = np.ones((P, T))
    one0[:, 0:TP:C] = 0
    one0[:, TP::LSEQ] = 0
    out["c_one0"] = one0
    f = np.arange(P)
    out["c_blk"] = f[:, None] // HEAD == f[None, :] // HEAD
    out["c_sel"] = f[:, None] % C == np.arange(C)[None, :]
    out["c_ident"] = np.eye(P)
    out["c_half30"] = np.full((P, 1), 15 * np.log(2.0))
    pos = np.concatenate([np.arange(TP), PAST + np.tile(np.arange(LSEQ), NSEQ)]).astype(np.float32)
    inv = np.power(np.float32(10000.0), -np.linspace(0.0, 1.0, P // 2, dtype=np.float32)).astype(np.float32)
    ang = (inv[:, None] * pos[None, :]).astype(np.float32).astype(np.float64)
    out["c_cos"] = np.concatenate([np.cos(ang), np.cos(ang)])
    out["c_sin"] = np.concatenate([-np.sin(ang), np.sin(ang)])
    out["c_perm"] = f[:, None] == (f[None, :] + P // 2) % P
    ret = np.zeros((HB, P, RET_CON))
    for h in range(HB):
        lg = float(np.log(np.float32(1.0 - 2.0 ** (-5.0 - h))))
        i = np.arange(RC)
        ts = np.arange(TS)
        d = i[None, :] - i[:, None]
        ds = ts[None, :] - ts[:, None]
        own = ts[None, :] // LSEQ == ts[:, None] // LSEQ
        ret[h, :, 0:TP] = np.exp(lg * (np.arange(TP) % RC + 1.0))
        ret[h, :, TP:T] = np.exp(lg * (ts % LSEQ + 1.0))
        ret[h, :, T:T + RC] = np.where(d >= 0, np.exp(lg * np.maximum(d, 0)), 0)
        ret[h, :TS, T + RC:T + RC + TS] = np.where((ds >= 0) & own, np.exp(lg * np.maximum(ds, 0)), 0)
        o = T + RC + TS
        ret[h, :, o] = np.exp(lg * (RC - 1.0 - i))
        ret[h, :, o + 1] = np.exp(lg * RC)
        ret[h, :, o + 2] = np.exp(lg * LSEQ)
        ret[h, :TS, o + 3:] = np.exp(lg * (LSEQ - 1.0 - ts % LSEQ))[:, None] * (ts[:, None] // LSEQ == np.arange(NSEQ))
    out["c_ret"] = ret
    return {k: np.ascontiguousarray(v, dtype=np.float32) for k, v in out.items()}


def columns(w):
    k, n = w.shape
    return np.ascontiguousarray(w.reshape(k // P, P, n // P, P).transpose(2, 1, 0, 3))


def features(v):
    return np.ascontiguousarray(v.reshape(-1, P).T)


def lay_out(i):
    A = {k: np.asarray(v) for k, v in i.items()}
    out = constants()
    x = np.concatenate([A["x_prompt"].reshape(TP, D), A["x_sample"].reshape(TS, D)])
    out["x"] = np.ascontiguousarray(x.T.reshape(DC, P, T).transpose(1, 0, 2))
    w = A["w_in"][0]
    out["w_rkv"] = np.ascontiguousarray(columns(w[:, :3072]).reshape(3, PAIRS, P, DC, P).transpose(1, 0, 2, 3, 4))
    out["w_lora"] = np.ascontiguousarray(w[:, 3072:3360].reshape(DC, P, LORA).transpose(1, 0, 2))
    out["w_low2"] = np.ascontiguousarray(np.concatenate(
        [np.concatenate([A["w_w2"][0], A["w_a2"][0]]).reshape(P, PAIRS, P), A["w_g2"][0][:P].reshape(P, PAIRS, P)], 2)
        .transpose(1, 0, 2))
    out["w_low3"] = np.ascontiguousarray(A["w_g2"][0][P:].reshape(32, PAIRS, P).transpose(1, 0, 2))
    mu = A["mu_shift"][0]
    out["w_par"] = np.ascontiguousarray(np.stack(
        [features(mu[0:1024]), features(mu[1024:2048]), features(mu[2048:3072])]
        + [features(A[n][0]) for n in ("w0", "a0", "k_k", "k_a", "r_k", "lnx_w", "lnx_b")], 2))

    def with_lora(rows):
        n = rows.shape[0]
        r = rows[:, :3072].reshape(n, 3, PAIRS, P).transpose(3, 2, 1, 0).reshape(P, 3 * PAIRS, n)
        l = np.zeros((P, 3, n), np.float32)
        l[:, 0], l[:, 1], l[:32, 2] = rows[:, 3072:3200].T, rows[:, 3200:3328].T, rows[:, 3328:].T
        return np.ascontiguousarray(np.concatenate([r, l], 1))

    out["lora_mu"] = np.ascontiguousarray(with_lora(mu[None])[:, 3 * PAIRS:, 0])
    out["shift_in"] = with_lora(A["state_shift"][0])
    out["wkv_in"] = np.ascontiguousarray(A["state_wkv"][0].reshape(NSEQ, PAIRS, 2, HEAD, HEAD)
                                         .transpose(1, 2, 4, 0, 3).reshape(PAIRS, P, NSEQ, HEAD))
    out["g_norm1"] = features(A["norm1"][0])
    out["g_norm2"] = features(A["norm2"][0])
    out["g_normf"] = features(A["norm_f"])
    q0, k0, v0, g0, m0 = 3360, 3360 + 1024, 3360 + 2048, 3360 + 4096, 3360 + 6144
    gate = columns(w[:, g0:m0]).reshape(HB, 2, P, DC, P)
    out["w_qkg"] = np.ascontiguousarray(np.concatenate(
        [columns(w[:, q0:k0])[:, None], columns(w[:, k0:v0])[:, None], gate], 1))
    out["w_v"] = np.ascontiguousarray(w[:, v0:g0].reshape(DC, P, HB, VH).transpose(2, 1, 0, 3))
    out["ret_in"] = np.ascontiguousarray(A["state_ret"][0].transpose(1, 2, 0, 3))
    out["w_ga"], out["w_gb"] = columns(w[:, m0:m0 + D]), columns(w[:, m0 + D:])
    out["w_pa"], out["w_pb"], out["w_out"] = (columns(A[n][0]) for n in ("w_pa", "w_pb", "w_out"))
    out["c_iota"] = np.ascontiguousarray(np.broadcast_to(np.arange(P, dtype=np.float32), (P, P)))
    out["w_q"] = columns(A["peer_wq"][0])
    out["keys"] = np.ascontiguousarray(A["peer_keys"][0].transpose(3, 0, 1, 2).reshape(P, 2 * PH, NK))
    out["peer_u"] = np.ascontiguousarray(A["peer_u"][0].reshape(ROWS, P, DC, P).transpose(0, 3, 2, 1))
    out["peer_v"] = np.ascontiguousarray(A["peer_v"][0].reshape(ROWS, P, DC, P))
    return out


OUTS = {"y": (P, DC, T), "ret_out": (HB, P, 1 + NSEQ, VH), "shift_out": (P, 3 * PAIRS + 3, 1 + NSEQ), "wkv_out": (PAIRS, P, 1 + NSEQ, HEAD)}


def build(nc, a):
    K = Kit()
    with ExitStack() as ctx:
        K.ps = ctx.enter_context(nc.psum_tensor("ps", [P, 8, 512], F32))
        K.ones = ctx.enter_context(nc.sbuf_tensor("ones", [P, P], F32))
        K.ident = ctx.enter_context(nc.sbuf_tensor("ident", [P, P], F32))
        K.half30 = ctx.enter_context(nc.sbuf_tensor("half30", [P, 1], F32))
        K.hn = ctx.enter_context(nc.sbuf_tensor("hn", [P, DC, T], F32))
        K.oa = nc.dram_tensor("oa", (PAIRS, P, T), F32, kind="Internal").ap()
        K.ob = nc.dram_tensor("ob", (HB, P, 2, T), F32, kind="Internal").ap()
        g1 = ctx.enter_context(nc.sbuf_tensor("g1", [P, DC], F32))
        s_c = ctx.enter_context(nc.semaphore("constants"))
        s_1 = ctx.enter_context(nc.semaphore("ones_made"))
        with nc.Block() as block:
            @block.sync
            def _(sp):
                for dst, src in ((K.ident, "c_ident"), (K.half30, "c_half30"), (g1, "g_norm1")):
                    sp.dma_start(dst[:, :], a[src]).then_inc(s_c, 16)
                sp.wait_ge(s_c, 48)

            @block.gpsimd
            def _(pool):
                pool.memset(K.ones[:, :], 1.0).then_inc(s_1, 1)
                pool.wait_ge(s_1, 1)
        with nc.sbuf_tensor("x1a", [P, DC, T], F32) as xt:
            norm_stage(nc, K, "n1", xt, K.hn, g1, load=a["x"])
        rwkv_stage(nc, K, a)
        ret_stage(nc, K, a)
        x1 = K.hn
        g2 = ctx.enter_context(nc.sbuf_tensor("g2", [P, 2, DC], F32))
        with nc.sbuf_tensor("m", [P, DC, T], F32) as m:
            merge_stage(nc, K, a, m)
            out_stage(nc, K, a, m, x1)
        s_g = ctx.enter_context(nc.semaphore("gains"))
        with nc.Block() as block:
            @block.sync
            def _(sp):
                for n, src in enumerate(("g_norm2", "g_normf")):
                    sp.dma_start(g2[:, n, :], a[src]).then_inc(s_g, 16)
                sp.wait_ge(s_g, 32)
        K.gates = nc.dram_tensor("gates", (P, T // TC, ROWS, TC), F32, kind="Internal").ap()
        with (nc.sbuf_tensor("hn_high", [P, DC, T], F32R) as K.hh,
              nc.sbuf_tensor("hn_low", [P, DC, T], F32R) as K.hl):
            with nc.sbuf_tensor("hn2", [P, DC, T], F32) as hn2:
                norm_stage(nc, K, "n2", x1, hn2, g2[:, 0, :], parts=(K.hh, K.hl))
            with nc.sbuf_tensor("slots", [P, 3, NTT * P], F32) as slots:
                with (nc.sbuf_tensor("top_v", [P, NTT, 2 * PH, TOPK], F32) as top_v,
                      nc.sbuf_tensor("top_i", [P, NTT, 2 * PH, TOPK], F32) as top_i):
                    route_stage(nc, K, a, top_v, top_i)
                    pick_stage(nc, K, a, top_v, top_i, slots)
                gates_stage(nc, K, a, slots)
            experts_stage(nc, K, a, x1)
        with nc.sbuf_tensor("y_sb", [P, DC, T], F32) as y:
            norm_stage(nc, K, "nf", x1, y, g2[:, 1, :], store=a["y"])


def kernel(**inputs):
    import concourse.bacc as bacc
    from concourse.bass_utils import run_bass_kernel_spmd

    nc = bacc.Bacc("TRN2", target_bir_lowering=False, num_devices=1)
    arrays = lay_out(inputs)
    a = {n: nc.dram_tensor(n, v.shape, F32, kind="ExternalInput").ap() for n, v in arrays.items()}
    a.update({n: nc.dram_tensor(n, s, F32, kind="ExternalOutput").ap() for n, s in OUTS.items()})
    build(nc, a)
    got = run_bass_kernel_spmd(nc, [arrays], core_ids=[0]).results[0]
    y = np.ascontiguousarray(got["y"].transpose(2, 1, 0).reshape(T, D))
    sh = got["shift_out"]
    rkv = sh[:, :3 * PAIRS].reshape(P, PAIRS, 3, 1 + NSEQ).transpose(3, 2, 1, 0).reshape(1 + NSEQ, 3 * PAIRS * P)
    lora = [sh[:n, 3 * PAIRS + t].T for t, n in enumerate((P, P, 32))]
    shift = np.ascontiguousarray(np.concatenate([rkv] + lora, 1))
    wkv = np.ascontiguousarray(got["wkv_out"].reshape(PAIRS, 2, HEAD, 1 + NSEQ, HEAD).transpose(3, 0, 1, 4, 2)
                               .reshape(1 + NSEQ, 2 * PAIRS, HEAD, HEAD))
    ret = np.ascontiguousarray(got["ret_out"].transpose(2, 0, 1, 3))
    return (y[:TP].reshape(1, TP, D), y[TP:].reshape(NSEQ, LSEQ, D), shift[None, :1], wkv[None, :1], ret[None, :1],
            shift[None, 1:], wkv[None, 1:], ret[None, 1:])
```

```python
from contextlib import ExitStack
import numpy as np
import concourse.bass as bass
from concourse import mybir

F32 = mybir.dt.float32
F32R = mybir.dt.float32r
U32 = mybir.dt.uint32
ALU = mybir.AluOpType
ACT = mybir.ActivationFunctionType
AX = mybir.AxisListType

P = 128
D = 2048
DC = D // P
TP = 512
NSEQ, LSEQ = 8, 8
TS = NSEQ * LSEQ
T = TP + TS
HT = T // 2
HEAD = 64
PAIRS = 8
C = 64
NCH = T // C
GRP = 3
PAST = 4096
PH = 8
NK = 128
TOPK = 16
NTT = -(-T // P)
LEAST = -3.0e38
TC = 48
LORA = 288
HB = 8
RC = 128
NRC = TP // RC
VH = 256
ROWS = 128
RET_CON = T + RC + TS + 3 + NSEQ
DECAY = float(np.exp(-0.5))
EPS = 1e-6
GN_EPS = 64e-5


class Steps:

    def __init__(self, sem, names):
        self.sem, self.names, self.n = sem, {x: k + 1 for k, x in enumerate(names)}, len(names)
        self.told = 0

    def ahead(self, eng):
        eng.sem_inc(self.sem, self.n)

    def of(self, i, name, back=0):
        return (i + (1 - back)) * self.n + self.names[name]

    def last(self, i, names):
        return (i + 1) * self.n + max(self.names[x] for x in names)

    def step(self, name):
        assert self.names[name] == self.told % self.n + 1, (name, self.told)
        self.told += 1
        return self.sem


def halves(ap):
    return ap.rearrange("p (a b) -> p a b", a=2)


def project(pe, out, weight, act, k=DC):
    for c in range(k):
        for h in range(2):
            last = pe.matmul(out[:, h, :], weight[:, c, :], act[:, c, h * HT:(h + 1) * HT],
                             start=(c == 0), stop=(c == k - 1))
    return last


def project3(pe, out, wh, wl, ah, al, k=DC):
    for c in range(k):
        for h in range(2):
            t = slice(h * HT, (h + 1) * HT)
            pe.matmul(out[:, h, :], wh[:, c, :], ah[:, c, t], start=(c == 0), stop=False)
            pe.matmul(out[:, h, :], wh[:, c, :], al[:, c, t], start=False, stop=False)
        for h in range(2):
            t = slice(h * HT, (h + 1) * HT)
            last = pe.matmul(out[:, h, :], wl[:, c, :], ah[:, c, t], start=False, stop=(c == k - 1))
    return last


def overlaid(nc, name, shape, dt=F32R):
    return nc.alloc_sbuf_tensor_at(name, shape, dt, offset=nc.sbuf_base - 4 * int(np.prod(shape[1:])))


def low(dve, out, whole, high):
    return dve.tensor_tensor(out, whole, high.bitcast(F32), ALU.subtract)


def norm_stage(nc, K, tag, src, dst, gain, load=None, store=None, parts=None):
    with ExitStack() as ctx:
        ld = [ctx.enter_context(nc.semaphore(tag + f"_loaded{q}")) for q in range(4)]
        sq = ctx.enter_context(nc.semaphore(tag + "_squared"))
        ss = ctx.enter_context(nc.semaphore(tag + "_summed"))
        ms = ctx.enter_context(nc.semaphore(tag + "_mean"))
        rs = ctx.enter_context(nc.semaphore(tag + "_rstd"))
        dn = ctx.enter_context(nc.semaphore(tag + "_normed"))
        st = ctx.enter_context(nc.semaphore(tag + "_stored"))
        hi = ctx.enter_context(nc.semaphore(tag + "_high"))
        rstd = ctx.enter_context(nc.sbuf_tensor(tag + "_r", [P, T], F32))
        pz = K.ps[:, 0:2, 0:HT]
        block = ctx.enter_context(nc.Block())

        @block.sync
        def _(sp):
            if load is not None:
                for q in range(4):
                    sp.dma_start(src[:, 4 * q:4 * q + 4, :], load[:, 4 * q:4 * q + 4, :]).then_inc(ld[q], 16)
            if store is not None:
                for q in range(4):
                    sp.wait_ge(dn, 4 * q + 4)
                    sp.dma_start(store[:, 4 * q:4 * q + 4, :], dst[:, 4 * q:4 * q + 4, :]).then_inc(st, 16)
                sp.wait_ge(st, 64)

        @block.scalar
        def _(act):
            for c in range(DC):
                if load is not None and c % 4 == 0:
                    act.wait_ge(ld[c // 4], 16)
                act.activation(dst[:, c, :], src[:, c, :], ACT.Square).then_inc(sq, 1)
            act.wait_ge(ms, 1)
            act.activation(rstd[:, :], rstd[:, :], ACT.Ln)
            act.drain()
            act.activation(rstd[:, :], rstd[:, :], ACT.Exp, scale=-0.5).then_inc(rs, 1)
            for c in range(DC if parts else 0):
                act.wait_ge(dn, c + 1)
                act.copy(parts[0][:, c, :], dst[:, c, :]).then_inc(hi, 1)

        @block.tensor
        def _(pe):
            for c in range(DC):
                pe.wait_ge(sq, c + 1)
                for h in range(2):
                    last = pe.matmul(pz[:, h, :], K.ones[:, :], dst[:, c, h * HT:(h + 1) * HT],
                                     start=(c == 0), stop=(c == DC - 1))
            last.then_inc(ss, 1)

        @block.vector
        def _(dve):
            dve.wait_ge(ss, 1)
            dve.tensor_scalar(halves(rstd[:, :]), pz, 1.0 / D, EPS, ALU.mult, ALU.add).then_inc(ms, 1)
            dve.wait_ge(rs, 1)
            for c in range(DC):
                dve.scalar_tensor_tensor(out=dst[:, c, :], in0=src[:, c, :], scalar=gain[:, c:c + 1],
                                         in1=rstd[:, :], op0=ALU.mult, op1=ALU.mult).then_inc(dn, 1)
            for c in range(DC if parts else 0):
                dve.wait_ge(hi, c + 1)
                dve.tensor_tensor(parts[1][:, c, :], dst[:, c, :], parts[0][:, c, :].bitcast(F32), ALU.subtract)


def inverse_plan():
    return [
        ("f2", "F", "f", "A", "G", None),
        ("F2", "f", "F", "B", None, None),
        ("f4", "B", "A", "E", None, None),
        ("F4", "A", "B", "H", "J", None),
        ("D1", "G", "IF", "L", None, None),
        ("f8", "H", "E", None, "A", None),
        ("D2", "J", "A", "B", None, None),
        ("D", "L", "B", "G", None, None),
        ("DT", "B", "L", "E", None, None),
        ("e", "E", "o", "H", None, None),
        ("eT", "o", "E", "A", None, "J"),
        ("e2", "H", "A", None, "L", None),
        ("h", "L", "G", "B", None, None),
        ("Z", "J", "B", "Z", None, None),
    ]


def rwkv_stage(nc, K, a):
    with ExitStack() as ctx:
        def sb(name, shape):
            return ctx.enter_context(nc.sbuf_tensor("rwkv_" + name, shape, F32))

        def sem(name):
            return ctx.enter_context(nc.semaphore("rwkv_" + name))

        ring = sb("weights", [P, 3, DC, P])
        lora_w = ring[:, :, :, :].rearrange("p a b c -> p (a b c)")[:, 0:DC * LORA]\
            .rearrange("p (c n) -> p c n", c=DC)
        low2 = sb("low2", [P, 2 * P])
        low3 = sb("low3", [32, P])
        s0 = sb("s0", [P, NSEQ, HEAD])
        par = sb("par", [P, PAIRS, 10])
        lmu = sb("lmu", [P, 3])
        shin = sb("shin", [P, PAIRS * 3 + 3, NSEQ])
        shout = sb("shout", [P, PAIRS * 3 + 3, 1 + NSEQ])
        one0 = sb("one0", [P, T])
        mask = sb("mask", [P, 2, 4, P])
        moff = sb("moff", [P, P])
        mlow = sb("mlow", [P, 2, P])
        mseq = sb("mseq", [P, NSEQ])
        blk = sb("blk", [P, P])
        sel = sb("sel", [P, C])
        zx = sb("zx", [P, 3, 1 + TP + NSEQ * (LSEQ + 1)])
        dif = sb("dif", [P, T])
        rs, ks, vs = sb("rs", [P, T]), sb("ks", [P, T]), sb("vs", [P, T])
        lo0, lo1, lo2 = sb("lo0", [P, T]), sb("lo1", [P, T]), sb("lo2", [32, T])
        kk, ksq, cs, cse = sb("kk", [P, T]), sb("ksq", [P, T]), sb("cs", [P, T]), sb("cse", [P, T])
        sg, at, winc, gg = sb("sg", [P, T]), sb("at", [P, T]), sb("winc", [P, T]), sb("gg", [P, T])
        kf, bb, rk = sb("kf", [P, T]), sb("bb", [P, T]), sg
        pads = {x: sb("pad_" + x, [P, NCH, P]) for x in "pqbkv"}
        xm = sb("xm", [P, NCH, 4, P])
        off = sb("off", [P, NCH, P])
        low = sb("low", [P, NCH, P])
        ilow = sb("ilow", [P, GRP, P])
        tok = sb("tok", [P, NCH, 320])
        zz = sb("zz", [P, NCH, P])
        mats = {x: sb("m" + x, [P, GRP, P]) for x in "ABEGHJL"}
        st = sb("st", [P, 2, HEAD])
        rn, uu = sb("rn", [P, HEAD]), sb("uu", [P, HEAD])
        yy = sb("yy", [P, NCH, HEAD])
        big = um = cs[:, 0:NSEQ * HEAD].rearrange("p (b v) -> p b v", b=NSEQ)
        vm = cse[:, 0:NSEQ * HEAD].rearrange("p (b v) -> p b v", b=NSEQ)
        r1, y1 = sb("r1", [P, HEAD]), sb("y1", [P, HEAD])
        so = sb("so", [P, NSEQ, HEAD])
        gm, gv = sb("gm", [P, NCH]), sb("gv", [P, NCH])
        ypad = pads["b"]
        oo = sb("oo", [P, T])
        ident = K.ident

        groups = [range(g * GRP, (g + 1) * GRP) for g in range(NCH // GRP)]
        plan = inverse_plan()
        inv = [f"{g}_{x[0]}" for g in range(len(groups)) for x in plan]
        chain = [f"{x}{c}" for c in range(NCH - 1) for x in "RUSY"]
        pe_s = Steps(sem("tensor"), ["w", "a", "g", "ss", "bon"]
                     + [f"{x}{c}" for c in range(NCH) for x in "xt"] + inv + chain
                     + ["sR", "s8", "sY", "sU", "sV", "sS", "yT"])
        v_s = Steps(sem("vector"), ["sh_r", "sh_k", "ksq", "sh_v", "cse", "max", "rp", "b", "pq"]
                    + [f"{x}{c}" for c in range(NCH) for x in ("mx", "mt")]
                    + [y for g in range(len(groups))
                       for y in [f"il{g}"] + [f"{g}_{x[0]}" for x in plan if x[4] or x[5]]]
                    + [f"{x}{c}" for c in range(NCH - 1) for x in ("R", "U", "S")]
                    + ["sR", "s8", "sY", "sU", "sUm", "sV", "sS", "var", "ypad", "oa"])
        a_s = Steps(sem("scalar"), ["sg", "at", "gg", "rkk", "exp"]
                    + [f"tv{c}" for c in range(NCH)]
                    + [f"{g}_{x[0]}" for g in range(len(groups)) for x in plan if x[3]]
                    + [f"Y{c}" for c in range(NCH - 1)] + ["rstd"])
        p_s = Steps(sem("pool"), ["bp", "kp", "vp"])
        made, copied = Steps(sem("made"), "rkv"), Steps(sem("copied"), "rkv")
        rows_in, rows_out = Steps(sem("rows_in"), "rkv"), Steps(sem("rows_out"), "rkv")
        POINTS = len(groups) * len(plan)
        BEFORE, AFTER = 20, 82
        pieces = [BEFORE + (AFTER - BEFORE) * (n + 1) // (POINTS + 4 * NCH - 4) for n in range(POINTS + 4 * NCH - 4)]
        ends = {x: next(n for n, done in enumerate(pieces) if done >= e) for x, e in (("r", 32), ("k", 64))}
        assert ends["r"] < POINTS <= ends["k"]
        consts = sem("consts")
        lw = sem("lora_weights")
        wt = [sem("tile_" + x) for x in "rkv"]
        small = sem("small_weights")
        stored = sem("stored")
        shst = sem("shift_stored")
        lz = sem("lora_projected")
        lin = sem("lora_shift_in")
        lev = sem("lora_evacuated")
        lsh = sem("lora_shifted")
        ldn = sem("lora_done")
        lout = sem("lora_shift_out")
        padz = sem("pads_zeroed")
        Z = [K.ps[:, 0:2, 0:HT], K.ps[:, 2:4, 0:HT]]
        X = [K.ps[:, 4 + b, :] for b in range(4)]

        def views(z, n=P):
            s = z[0:n, 1 + TP:].rearrange("p (b l) -> p b l", b=NSEQ)
            return z[0:n, 1:1 + TP], z[0:n, 0:TP], s[:, :, 1:], s[:, :, 0:LSEQ]

        def evacuate(act, z, src, n=P):
            cur, _, scur, _ = views(z, n)
            act.copy(cur[:, 0:HT], src[0:n, 0, :])
            act.copy(cur[:, HT:TP], src[0:n, 1, 0:TP - HT])
            return act.copy(scur, src[0:n, 1, TP - HT:HT].rearrange("p (b l) -> p b l", b=NSEQ))

        def shift(dve, z, mu, out, n=P):
            cur, prev, scur, sprev = views(z, n)
            dve.tensor_tensor(dif[0:n, 0:TP], prev, cur, ALU.subtract)
            dve.tensor_tensor(dif[0:n, TP:T].rearrange("p (b l) -> p b l", b=NSEQ), sprev, scur, ALU.subtract)
            dve.drain()
            dve.scalar_tensor_tensor(out=out[0:n, 0:TP], in0=dif[0:n, 0:TP], scalar=mu, in1=cur,
                                     op0=ALU.mult, op1=ALU.add)
            last = dve.scalar_tensor_tensor(
                out=out[0:n, TP:T].rearrange("p (b l) -> p b l", b=NSEQ),
                in0=dif[0:n, TP:T].rearrange("p (b l) -> p b l", b=NSEQ), scalar=mu, in1=scur,
                op0=ALU.mult, op1=ALU.add)
            return last

        def every_pair(eng, body):
            with eng.Fori(0, PAIRS - 1) as i:
                body(i, False)
            body(PAIRS - 1, True)

        def last_rows(pool, z, t, n=P):
            s = z[0:n, 1 + TP:].rearrange("p (b l) -> p b l", b=NSEQ)
            pool.tensor_copy(shout[0:n, t, 0:1], z[0:n, TP:TP + 1])
            return pool.tensor_copy(shout[0:n, t, 1:1 + NSEQ], s[:, :, LSEQ])

        def first_rows(pool, z, t, n=P):
            s = z[0:n, 1 + TP:].rearrange("p (b l) -> p b l", b=NSEQ)
            return pool.tensor_copy(s[:, :, 0], shin[0:n, t, :])

        block = ctx.enter_context(nc.Block())

        @block.sync
        def _(sp):
            sp.dma_start(lora_w, a["w_lora"]).then_inc(lw, 16)
            for dst, src in ((par, "w_par"), (lmu, "lora_mu"), (shin, "shift_in"), (one0, "c_one0"),
                             (mask, "c_mask"), (moff, "c_moff"), (mlow, "c_mlow"), (mseq, "c_mseq"),
                             (blk, "c_blk"), (sel, "c_sel")):
                sp.dma_start(dst[:], a[src]).then_inc(consts, 16)
            sp.wait_ge(lz, 3)
            with sp.Fori(0, PAIRS) as i:
                for t, x in enumerate("rkv"):
                    sp.wait_ge(made.sem, made.of(i, x, 1))
                    sp.dma_start(ring[:, t, :, :], a["w_rkv"][i, t]).then_inc(wt[t], 16)
                sp.wait_ge(pe_s.sem, pe_s.of(i, "g", 1))
                sp.dma_start(low2[:, :], a["w_low2"][i]).then_inc(small, 16)
                sp.dma_start(low3[:, :], a["w_low3"][i]).then_inc(small, 16)
                sp.wait_ge(pe_s.sem, pe_s.of(i, "sS", 1))
                sp.dma_start(s0[:, :, :], a["wkv_in"][i]).then_inc(small, 16)

        @block.gpsimd
        def _(pool):
            p_s.ahead(pool)
            rows_in.ahead(pool)
            rows_out.ahead(pool)
            for x in "pqbkv":
                pool.memset(pads[x][:, :, :], 0.0)
            pool.memset(off[:, NCH - 1, :], 0.0)
            pool.memset(zx[:, :, 0:1], 0.0)
            pool.memset(shout[:, :, :], 0.0)
            pool.drain().then_inc(padz, 1)
            pool.wait_ge(consts, 160)
            for t, n in ((0, P), (1, P), (2, 32)):
                if t == 2:
                    pool.wait_ge(lsh, 1)
                first_rows(pool, zx[:, t % 2, :], PAIRS * 3 + t, n).then_inc(lin, 1)
                pool.drain()
                if t == 1:
                    pool.wait_ge(lev, 1)
                    last_rows(pool, zx[:, 0, :], PAIRS * 3, P).then_inc(lout, 1)
            for t, n in ((1, P), (2, 32)):
                pool.wait_ge(lev, t + 1)
                last_rows(pool, zx[:, t % 2, :], PAIRS * 3 + t, n).then_inc(lout, 1)
                pool.drain()

            def rows(i):
                for t, x in enumerate("rkv"):
                    pool.wait_ge(v_s.sem, v_s.of(i, "sh_" + x, 1))
                    first_rows(pool, zx[:, t, :], 3 * i + t).then_inc(rows_in.step(x), 1)
                    pool.drain()
                for t, x in enumerate("rkv"):
                    pool.wait_ge(copied.sem, copied.of(i, x))
                    last_rows(pool, zx[:, t, :], 3 * i + t).then_inc(rows_out.step(x), 1)
                    pool.drain()

            pool.wait_ge(lsh, 3)
            rows(0)

            def body(i, last):
                def pad(x, p0, p1):
                    for h in range(2):
                        r = slice(HEAD * h, HEAD * h + HEAD)
                        o = pads[x][r, :, C * h:C * h + C]
                        u = p0[r, :].rearrange("p (c t) -> p c t", c=NCH)
                        if p1 is None:
                            last = pool.tensor_copy(o, u)
                        else:
                            last = pool.tensor_tensor(o, u, p1[r, :].rearrange("p (c t) -> p c t", c=NCH), ALU.mult)
                        if h == 0:
                            pool.drain()
                    return last

                pool.wait_ge(pe_s.sem, pe_s.of(i, "yT", 1))
                pool.wait_ge(a_s.sem, a_s.of(i, "exp"))
                pool.wait_ge(v_s.sem, v_s.of(i, "b"))
                pad("b", bb, cs).then_inc(p_s.step("bp"), 1)
                pool.drain()
                pad("k", kf, cs).then_inc(p_s.step("kp"), 1)
                pool.drain()
                pad("v", vs, None).then_inc(p_s.step("vp"), 1)
                pool.drain()
                if not last:
                    rows(i + 1)
            every_pair(pool, body)

        @block.scalar
        def _(act):
            a_s.ahead(act)
            copied.ahead(act)
            act.sem_inc(stored, 48)
            for t, n in ((0, P), (1, P), (2, 32)):
                act.wait_ge(lz, t + 1)
                act.wait_ge(padz, 1)
                if t == 2:
                    act.wait_ge(lsh, 1)
                    act.wait_ge(lout, 1)
                evacuate(act, zx[:, t % 2, :], Z[t % 2], n).then_inc(lev, 1)
            act.wait_ge(lsh, 3)
            act.activation(lo0[0:64, :], lo0[0:64, :], ACT.Tanh)
            act.activation(lo1[:, :], lo1[:, :], ACT.Sigmoid)
            act.activation(lo2[:, :], lo2[:, :], ACT.Sigmoid).then_inc(ldn, 1)

            def copy_out(i, x):
                act.wait_ge(made.sem, made.of(i, x))
                act.wait_ge(v_s.sem, v_s.of(i, "sh_" + x, 1))
                act.wait_ge(rows_out.sem, rows_out.of(i, x, 1))
                evacuate(act, zx[:, "rkv".index(x), :], Z[0]).then_inc(copied.step(x), 1)

            act.wait_ge(lout, 3)
            for x in "rkv":
                copy_out(0, x)

            def body(i, last):
                act.wait_ge(pe_s.sem, pe_s.of(i, "w"))
                act.wait_ge(v_s.sem, v_s.of(i, "oa", 1))
                act.activation(halves(sg[:, :]), Z[1], ACT.Sigmoid, bias=par[:, i, 3:4]).then_inc(a_s.step("sg"), 1)
                act.wait_ge(pe_s.sem, pe_s.of(i, "a"))
                act.activation(halves(at[:, :]), Z[0], ACT.Sigmoid, bias=par[:, i, 4:5]).then_inc(a_s.step("at"), 1)
                act.wait_ge(pe_s.sem, pe_s.of(i, "g"))
                act.copy(halves(gg[:, :]), Z[1]).then_inc(a_s.step("gg"), 1)
                act.wait_ge(v_s.sem, v_s.of(i, "max"))
                act.activation(rk[:, :], rk[:, :], ACT.Ln, scale=float(2 ** 30))
                act.drain()
                act.activation(rk[:, :], rk[:, :], ACT.Exp, scale=-0.5, bias=K.half30[:, 0:1]).then_inc(a_s.step("rkk"), 1)
                act.activation(winc[:, :], cs[:, :], ACT.Exp, scale=-DECAY)
                act.activation(cse[:, :], cse[:, :], ACT.Exp, scale=-DECAY)
                act.drain()
                act.activation(cs[:, :], cs[:, :], ACT.Exp, scale=DECAY).then_inc(a_s.step("exp"), 1)
                for c in range(NCH):
                    act.wait_ge(v_s.sem, v_s.of(i, f"mt{c}"))
                    act.copy(tok[:, c, :], X[2 + c % 2][:, P:P + 320]).then_inc(a_s.step(f"tv{c}"), 1)
                for g, cc in enumerate(groups):
                    for n, (name, _, _, to, _, _) in enumerate(plan):
                        if to:
                            act.wait_ge(pe_s.sem, pe_s.of(i, f"{g}_{name}"))
                            dst = zz[:, cc[0]:cc[-1] + 1, :] if to == "Z" else mats[to][:, :, :]
                            src = X[(g * len(plan) + n) % 4][:, 0:GRP * P].rearrange("p (a b) -> p a b", a=GRP)
                            act.copy(dst, src).then_inc(a_s.step(f"{g}_{name}"), 1)
                        point = g * len(plan) + n
                        if not last and point == ends["r"]:
                            copy_out(i + 1, "r")
                for c in range(NCH - 1):
                    if not last and c == (ends["k"] - POINTS) // 4:
                        copy_out(i + 1, "k")
                    act.wait_ge(pe_s.sem, pe_s.of(i, f"Y{c}"))
                    act.copy(yy[:, c, :], X[2][:, 0:HEAD]).then_inc(a_s.step(f"Y{c}"), 1)
                act.wait_ge(v_s.sem, v_s.of(i, "var"))
                act.activation(gv[:, :], gv[:, :], ACT.Ln)
                act.drain()
                act.activation(gv[:, :], gv[:, :], ACT.Exp, scale=-0.5).then_inc(a_s.step("rstd"), 1)
                if not last:
                    copy_out(i + 1, "v")
                act.wait_ge(v_s.sem, v_s.of(i, "oa"))
                act.dma_start(K.oa[i], oo[:, :]).then_inc(stored, 16)
                act.dma_start(a["wkv_out"][i, :, 0, :], st[:, 0, :]).then_inc(stored, 16)
                act.dma_start(a["wkv_out"][i, :, 1:1 + NSEQ, :], so[:, :, :]).then_inc(stored, 16)
            every_pair(act, body)
            act.wait_ge(rows_out.sem, rows_out.of(PAIRS - 1, "v"))
            act.dma_start(a["shift_out"], shout[:, :, :]).then_inc(shst, 16)
            act.wait_ge(shst, 16)
            act.wait_ge(stored, 48 * PAIRS + 48)

        @block.tensor
        def _(pe):
            pe_s.ahead(pe)
            made.ahead(pe)
            pe.wait_ge(lw, 16)
            for t, n in ((0, P), (1, P), (2, 32)):
                if t == 2:
                    pe.wait_ge(lev, 1)
                for c in range(DC):
                    for h in range(2):
                        last = pe.matmul(Z[t % 2][0:n, h, :], lora_w[:, c, P * t:P * t + n],
                                         K.hn[:, c, h * HT:(h + 1) * HT], start=(c == 0), stop=(c == DC - 1))
                last.then_inc(lz, 1)
            pe.wait_ge(lev, 3)
            pe.wait_ge(ldn, 1)
            pe.wait_ge(consts, 160)

            def project_pieces(i, lo, hi):
                for m in range(lo, hi):
                    t, c, h = m // 32, m % 32 // 2, m % 2
                    if m % 32 == 0:
                        pe.wait_ge(wt[t], 16 * i + 16)
                        if t:
                            pe.wait_ge(copied.sem, copied.of(i, "rkv"[t - 1]))
                    last = pe.matmul(Z[0][:, h, :], ring[:, t, c, :], K.hn[:, c, h * HT:(h + 1) * HT],
                                     start=(c == 0), stop=(c == DC - 1))
                    if m % 32 == 31:
                        last.then_inc(made.step("rkv"[t]), 1)

            project_pieces(0, 0, 96)

            def body(i, last_pair):
                pe.wait_ge(small, 48 * i + 48)
                pe.wait_ge(v_s.sem, v_s.of(i, "oa", 1))
                pe.wait_ge(copied.sem, copied.of(i, "v"))
                for x, z in (("w", 1), ("a", 0), ("g", 1)):
                    if x == "g":
                        pe.wait_ge(a_s.sem, a_s.of(i, "sg"))
                    for h in range(2):
                        tt = slice(h * HT, (h + 1) * HT)
                        if x == "w":
                            last = pe.matmul(Z[z][:, h, :], low2[0:64, 0:P], lo0[0:64, tt], start=True, stop=True)
                        elif x == "a":
                            last = pe.matmul(Z[z][:, h, :], low2[64:P, 0:P], lo0[64:P, tt], start=True, stop=True)
                        else:
                            pe.matmul(Z[z][:, h, :], low2[:, P:2 * P], lo1[:, tt], start=True, stop=False)
                            last = pe.matmul(Z[z][:, h, :], low3[:, :], lo2[:, tt], start=False, stop=True)
                    last.then_inc(pe_s.step(x), 1)
                for x, z, ev, src, after in (("ss", 0, "at", ksq, "ksq"), ("bon", 1, "gg", dif, "rp")):
                    pe.wait_ge(a_s.sem, a_s.of(i, ev))
                    pe.wait_ge(v_s.sem, v_s.of(i, after))
                    for h in range(2):
                        last = pe.matmul(Z[z][:, h, :], blk[:, :], src[:, h * HT:(h + 1) * HT], start=True, stop=True)
                    last.then_inc(pe_s.step(x), 1)
                if not last_pair:
                    project_pieces(i + 1, 0, BEFORE)
                pe.wait_ge(v_s.sem, v_s.of(i, "pq"))
                pe.wait_ge(p_s.sem, p_s.of(i, "vp"))
                for c in range(NCH):
                    pq = {x: pads[x][:, c, :] for x in "pqbkv"}
                    x = X[c % 2]
                    if c >= 2:
                        pe.wait_ge(v_s.sem, v_s.of(i, f"mx{c - 2}"))
                    for n, (l, r) in enumerate(("bp", "kp", "bq", "kq")):
                        last = pe.matmul(x[:, P * n:P * n + P], pq[l], pq[r], start=True, stop=True)
                    last.then_inc(pe_s.step(f"x{c}"), 1)
                    x = X[2 + c % 2]
                    if c >= 2:
                        pe.wait_ge(v_s.sem, v_s.of(i, f"mt{c - 2}"))
                        pe.wait_ge(a_s.sem, a_s.of(i, f"tv{c - 2}"))
                    pe.matmul(x[:, 0:P], pq["p"], pq["b"], start=True, stop=True)
                    pe.matmul(x[:, P:P + C], pq["v"], sel[:, :], start=True, stop=True)
                    pe.transpose(x[:, P + C:2 * P + C], pq["b"], ident[:, :])
                    pe.transpose(x[:, 2 * P + C:3 * P + C], pq["k"], ident[:, :])\
                        .then_inc(pe_s.step(f"t{c}"), 1)
                def out_of_bank(n):
                    g, (name, _, _, to, _, _) = n // len(plan), plan[n % len(plan)]
                    return ([f"{g}_{name}"], []) if to else ([], [f"{g}_{name}"])

                for g, cc in enumerate(groups):
                    for n, (name, l, r, _, _, _) in enumerate(plan):
                        at_bank = g * len(plan) + n
                        by_act, by_dve = out_of_bank(at_bank - 4) if at_bank >= 4 else ([], [])
                        for m in (l, r):
                            by = [k for k in range(n) if m in plan[k][3:6]]
                            if by and m == plan[by[-1]][3]:
                                by_act = by_act + [f"{g}_{plan[by[-1]][0]}"]
                            elif by:
                                by_dve = by_dve + [f"{g}_{plan[by[-1]][0]}"]
                        if n == 0:
                            by_dve = by_dve + [f"il{g}"]
                        if at_bank == 0:
                            by_act = by_act + [f"tv{NCH - 1}"]
                        if by_act:
                            pe.wait_ge(a_s.sem, a_s.last(i, by_act))
                        if by_dve:
                            pe.wait_ge(v_s.sem, v_s.last(i, by_dve))
                        for k, c in enumerate(cc):
                            given = {"f": xm[:, c, 0, :], "F": low[:, c, :], "IF": ilow[:, k, :], "o": off[:, c, :]}
                            ml, mr = (given[m] if m in given else mats[m][:, k, :] for m in (l, r))
                            last = pe.matmul(X[at_bank % 4][:, P * k:P * k + P], ml, mr, start=True, stop=True)
                        last.then_inc(pe_s.step(f"{g}_{name}"), 1)
                        if not last_pair:
                            project_pieces(i + 1, pieces[at_bank - 1] if at_bank else BEFORE, pieces[at_bank])
                freed = [out_of_bank(len(groups) * len(plan) - 1 - n) for n in range(4)]
                pe.wait_ge(a_s.sem, a_s.last(i, sum((x for x, _ in freed), [])))
                pe.wait_ge(v_s.sem, v_s.last(i, sum((x for _, x in freed), [])))

                def between(n):
                    if not last_pair:
                        project_pieces(i + 1, pieces[POINTS + n - 1], pieces[POINTS + n])

                for c in range(NCH - 1):
                    s = st[:, c % 2, :]
                    v, b, k = tok[:, c, 0:C], tok[:, c, C:C + P], tok[:, c, C + P:C + 2 * P]
                    if c:
                        pe.wait_ge(v_s.sem, v_s.of(i, f"S{c - 1}"))
                        pe.matmul(X[0][:, 0:HEAD], pads["p"][:, c, :], s, start=True, stop=False)
                    pe.matmul(X[0][:, 0:HEAD], xm[:, c, 1, :], v, start=(c == 0), stop=True)\
                        .then_inc(pe_s.step(f"R{c}"), 1)
                    between(4 * c)
                    pe.wait_ge(v_s.sem, v_s.of(i, f"R{c}"))
                    pe.matmul(X[1][:, 0:HEAD], zz[:, c, :], rn[:, :], start=True, stop=True)\
                        .then_inc(pe_s.step(f"U{c}"), 1)
                    between(4 * c + 1)
                    pe.wait_ge(v_s.sem, v_s.of(i, f"U{c}"))
                    if c:
                        pe.matmul(X[3][:, 0:HEAD], ident[:, :], s, start=True, stop=False)
                    pe.matmul(X[3][:, 0:HEAD], b, uu[:, :], start=(c == 0), stop=False)
                    pe.matmul(X[3][:, 0:HEAD], k, v, start=False, stop=True).then_inc(pe_s.step(f"S{c}"), 1)
                    between(4 * c + 2)
                    if c:
                        pe.wait_ge(a_s.sem, a_s.of(i, f"Y{c - 1}"))
                        pe.matmul(X[2][:, 0:HEAD], pads["q"][:, c, :], s, start=True, stop=False)
                    pe.matmul(X[2][:, 0:HEAD], xm[:, c, 2, :], uu[:, :], start=(c == 0), stop=False)
                    pe.matmul(X[2][:, 0:HEAD], xm[:, c, 3, :], v, start=False, stop=True)\
                        .then_inc(pe_s.step(f"Y{c}"), 1)
                    between(4 * c + 3)

                c = NCH - 1
                v, b, k = tok[:, c, 0:C], tok[:, c, C:C + P], tok[:, c, C + P:C + 2 * P]
                flat = s0[:, :, :].rearrange("p b v -> p (b v)")
                pe.matmul(X[0], pads["p"][:, c, :], flat, start=True, stop=True).then_inc(pe_s.step("sR"), 1)
                pe.matmul(X[1][:, 0:HEAD], xm[:, c, 1, :], v, start=True, stop=True).then_inc(pe_s.step("s8"), 1)
                pe.wait_ge(a_s.sem, a_s.of(i, f"Y{NCH - 2}"))
                pe.matmul(X[2], pads["q"][:, c, :], flat, start=True, stop=True).then_inc(pe_s.step("sY"), 1)
                pe.wait_ge(v_s.sem, v_s.of(i, "s8"))
                pe.matmul(X[3][:, 0:HEAD], zz[:, c, :], rn[:, :], start=True, stop=True)\
                    .then_inc(pe_s.step("sU"), 1)
                pe.wait_ge(v_s.sem, v_s.of(i, "sU"))
                pe.matmul(X[1][:, 0:HEAD], xm[:, c, 2, :], uu[:, :], start=True, stop=False)
                pe.matmul(X[1][:, 0:HEAD], xm[:, c, 3, :], v, start=False, stop=True)\
                    .then_inc(pe_s.step("sV"), 1)
                pe.wait_ge(v_s.sem, v_s.of(i, "sUm"))
                pe.matmul(X[0], ident[:, :], flat, start=True, stop=False)
                pe.matmul(X[0], b, cs[:, 0:NSEQ * HEAD], start=False, stop=False)
                pe.matmul(X[0], k, cse[:, 0:NSEQ * HEAD], start=False, stop=True)\
                    .then_inc(pe_s.step("sS"), 1)
                if not last_pair:
                    project_pieces(i + 1, AFTER, 96)
                pe.wait_ge(v_s.sem, v_s.of(i, "ypad"))
                for c in range(NCH):
                    o = X[c // 5][:, C * (c % 5):C * (c % 5) + C]
                    last = pe.matmul(o, ypad[:, c, :], sel[:, :], start=True, stop=True)
                last.then_inc(pe_s.step("yT"), 1)
            every_pair(pe, body)

        @block.vector
        def _(dve):
            v_s.ahead(dve)
            dve.wait_ge(consts, 160)
            for t, (n, out) in enumerate(((P, lo0), (P, lo1), (32, lo2))):
                dve.wait_ge(lev, t + 1)
                dve.wait_ge(lin, t + 1)
                shift(dve, zx[:, t % 2, :], lmu[0:n, t:t + 1], out, n).then_inc(lsh, 1)
                dve.drain()
            dve.wait_ge(padz, 1)

            def body(i, last_pair):
                def mul_pads(x, p0, p1):
                    for h in range(2):
                        r = slice(HEAD * h, HEAD * h + HEAD)
                        last = dve.tensor_tensor(pads[x][r, :, C * h:C * h + C],
                                                 p0[r, :].rearrange("p (c t) -> p c t", c=NCH),
                                                 p1[r, :].rearrange("p (c t) -> p c t", c=NCH), ALU.mult)
                    return last

                def shifted(x, slot, mu, out):
                    dve.wait_ge(copied.sem, copied.of(i, x))
                    dve.wait_ge(rows_in.sem, rows_in.of(i, x))
                    shift(dve, zx[:, slot, :], par[:, i, mu:mu + 1], out).then_inc(v_s.step("sh_" + x), 1)
                    dve.drain()

                shifted("r", 0, 0, rs)
                shifted("k", 1, 1, ks)
                dve.tensor_scalar(kk[:, :], ks[:, :], par[:, i, 5:6], None, ALU.mult)
                dve.drain()
                dve.tensor_tensor(ksq[:, :], kk[:, :], kk[:, :], ALU.mult).then_inc(v_s.step("ksq"), 1)
                dve.drain()
                shifted("v", 2, 2, vs)
                dve.wait_ge(a_s.sem, a_s.of(i, "sg"))
                dve.tensor_tensor_scan(cs[:, :], one0[:, :], sg[:, :], 0.0, ALU.mult, ALU.add)
                dve.drain()
                dve.tensor_tensor(cse[:, :], cs[:, :], sg[:, :], ALU.subtract).then_inc(v_s.step("cse"), 1)
                dve.drain()
                dve.wait_ge(pe_s.sem, pe_s.of(i, "ss"))
                dve.tensor_scalar(halves(rk[:, :]), Z[0], 1e-24, None, ALU.max).then_inc(v_s.step("max"), 1)
                dve.drain()
                dve.wait_ge(a_s.sem, a_s.of(i, "at"))
                dve.tensor_scalar(bb[:, :], at[:, :], 1.0, par[:, i, 6:7], ALU.subtract, ALU.mult)
                dve.drain()
                dve.scalar_tensor_tensor(out=kf[:, :], in0=bb[:, :], scalar=1.0, in1=ks[:, :],
                                         op0=ALU.add, op1=ALU.mult)
                dve.drain()
                dve.scalar_tensor_tensor(out=dif[:, :], in0=rs[:, :], scalar=par[:, i, 7:8], in1=kf[:, :],
                                         op0=ALU.mult, op1=ALU.mult).then_inc(v_s.step("rp"), 1)
                dve.drain()
                dve.wait_ge(a_s.sem, a_s.of(i, "rkk"))
                dve.tensor_tensor(kk[:, :], kk[:, :], rk[:, :], ALU.mult)
                dve.drain()
                dve.tensor_tensor(bb[:, :], kk[:, :], at[:, :], ALU.mult).then_inc(v_s.step("b"), 1)
                dve.drain()
                dve.wait_ge(a_s.sem, a_s.of(i, "exp"))
                mul_pads("p", kk, cse)
                mul_pads("q", rs, winc).then_inc(v_s.step("pq"), 1)
                dve.drain()
                for c in range(NCH):
                    kind = c // (NCH - 1)
                    dve.wait_ge(pe_s.sem, pe_s.of(i, f"x{c}"))
                    if kind == 0:
                        dve.tensor_tensor(off[:, c, :], X[c % 2][:, 0:P], moff[:, :], ALU.mult)
                    dve.tensor_tensor(xm[:, c, :, :], X[c % 2].rearrange("p (a b) -> p a b", a=4),
                                      mask[:, kind, :, :], ALU.mult).then_inc(v_s.step(f"mx{c}"), 1)
                    dve.drain()
                    dve.wait_ge(pe_s.sem, pe_s.of(i, f"t{c}"))
                    dve.tensor_tensor(low[:, c, :], X[2 + c % 2][:, 0:P], mlow[:, kind, :], ALU.mult)\
                        .then_inc(v_s.step(f"mt{c}"), 1)
                dve.drain()
                eye = ident[:, :].unsqueeze(1)
                for g, cc in enumerate(groups):
                    dve.scalar_tensor_tensor(out=ilow[:, :, :], in0=low[:, cc[0]:cc[-1] + 1, :], scalar=-1.0,
                                             in1=eye.broadcast_to([P, GRP, P]), op0=ALU.mult, op1=ALU.add)\
                        .then_inc(v_s.step(f"il{g}"), 1)
                    dve.drain()
                    for n, (name, _, _, to, plus, minus) in enumerate(plan):
                        if plus or minus:
                            src = X[(g * len(plan) + n) % 4][:, 0:GRP * P].rearrange("p (a b) -> p a b", a=GRP)
                            if to:
                                src = mats[to][:, :, :]
                                dve.wait_ge(a_s.sem, a_s.of(i, f"{g}_{name}"))
                            else:
                                dve.wait_ge(pe_s.sem, pe_s.of(i, f"{g}_{name}"))
                            dve.scalar_tensor_tensor(out=mats[plus or minus][:, :, :], in0=src,
                                                     scalar=1.0 if plus else -1.0,
                                                     in1=eye.broadcast_to([P, GRP, P]), op0=ALU.mult, op1=ALU.add)\
                                                         .then_inc(v_s.step(f"{g}_{name}"), 1)
                            dve.drain()
                dve.wait_ge(stored, 48 * i + 48)
                for c in range(NCH - 1):
                    dve.wait_ge(pe_s.sem, pe_s.of(i, f"R{c}"))
                    dve.tensor_scalar(rn[:, :], X[0][:, 0:HEAD], -1.0, None, ALU.mult).then_inc(v_s.step(f"R{c}"), 1)
                    dve.drain()
                    dve.wait_ge(pe_s.sem, pe_s.of(i, f"U{c}"))
                    dve.tensor_copy(uu[:, :], X[1][:, 0:HEAD]).then_inc(v_s.step(f"U{c}"), 1)
                    dve.drain()
                    dve.wait_ge(pe_s.sem, pe_s.of(i, f"S{c}"))
                    end = C * c + C - 1
                    dve.tensor_scalar(st[:, (c + 1) % 2, :], X[3][:, 0:HEAD], winc[:, end:end + 1], None, ALU.mult)\
                        .then_inc(v_s.step(f"S{c}"), 1)
                    dve.drain()
                seq = mseq[:, :].unsqueeze(2).broadcast_to([P, NSEQ, HEAD])

                def own_rows(bank, out):
                    dve.tensor_tensor(big[:, :, :], bank.rearrange("p (b v) -> p b v", b=NSEQ), seq, ALU.mult)
                    dve.drain()
                    return dve.tensor_reduce(out[:, :], big[:, :, :].rearrange("p b v -> p v b"), AX.X, ALU.add)

                dve.wait_ge(pe_s.sem, pe_s.of(i, "sR"))
                own_rows(X[0], r1).then_inc(v_s.step("sR"), 1)
                dve.drain()
                dve.wait_ge(pe_s.sem, pe_s.of(i, "s8"))
                dve.scalar_tensor_tensor(out=rn[:, :], in0=X[1][:, 0:HEAD], scalar=-1.0, in1=r1[:, :],
                                         op0=ALU.mult, op1=ALU.subtract).then_inc(v_s.step("s8"), 1)
                dve.drain()
                dve.wait_ge(pe_s.sem, pe_s.of(i, "sY"))
                own_rows(X[2], y1).then_inc(v_s.step("sY"), 1)
                dve.drain()
                dve.wait_ge(pe_s.sem, pe_s.of(i, "sU"))
                dve.tensor_copy(uu[:, :], X[3][:, 0:HEAD]).then_inc(v_s.step("sU"), 1)
                dve.drain()
                for dst, src in ((um, uu[:, :]), (vm, tok[:, NCH - 1, 0:C])):
                    last = dve.tensor_tensor(dst[:, :, :], src.unsqueeze(1).broadcast_to([P, NSEQ, HEAD]), seq, ALU.mult)
                last.then_inc(v_s.step("sUm"), 1)
                dve.drain()
                dve.wait_ge(pe_s.sem, pe_s.of(i, "sV"))
                dve.tensor_tensor(yy[:, NCH - 1, :], X[1][:, 0:HEAD], y1[:, :], ALU.add).then_inc(v_s.step("sV"), 1)
                dve.drain()
                dve.wait_ge(pe_s.sem, pe_s.of(i, "sS"))
                last_w = winc[:, TP + LSEQ - 1:T:LSEQ].unsqueeze(2).broadcast_to([P, NSEQ, HEAD])
                dve.tensor_tensor(so[:, :, :], X[0].rearrange("p (b v) -> p b v", b=NSEQ), last_w, ALU.mult)\
                    .then_inc(v_s.step("sS"), 1)
                dve.drain()
                dve.wait_ge(a_s.sem, a_s.of(i, f"Y{NCH - 2}"))
                dve.tensor_reduce(gm[:, :], yy[:, :, :], AX.X, ALU.add)
                dve.drain()
                dve.tensor_scalar(gm[:, :], gm[:, :], 1.0 / HEAD, None, ALU.mult)
                dve.drain()
                gmb = gm[:, :].unsqueeze(2).broadcast_to([P, NCH, HEAD])
                dve.tensor_tensor(yy[:, :, :], yy[:, :, :], gmb, ALU.subtract)
                dve.drain()
                y2 = dif[:, :].rearrange("p (c v) -> p c v", c=NCH)
                dve.tensor_tensor(y2, yy[:, :, :], yy[:, :, :], ALU.mult)
                dve.drain()
                dve.tensor_reduce(gv[:, :], y2, AX.X, ALU.add)
                dve.drain()
                dve.tensor_scalar(gv[:, :], gv[:, :], 1.0 / HEAD, GN_EPS, ALU.mult, ALU.add).then_inc(v_s.step("var"), 1)
                dve.drain()
                dve.wait_ge(a_s.sem, a_s.of(i, "rstd"))
                for h in range(2):
                    r = slice(HEAD * h, HEAD * h + HEAD)
                    last = dve.tensor_tensor(ypad[r, :, HEAD * h:HEAD * h + HEAD], yy[r, :, :],
                                             gv[r, :].unsqueeze(2).broadcast_to([HEAD, NCH, HEAD]), ALU.mult)
                last.then_inc(v_s.step("ypad"), 1)
                dve.drain()
                dve.tensor_tensor(halves(ksq[:, :]), Z[1], halves(vs[:, :]), ALU.mult)
                dve.wait_ge(pe_s.sem, pe_s.of(i, "yT"))
                for b, lo, hi in ((0, 0, 5 * C), (1, 5 * C, T)):
                    dve.tensor_scalar(kk[:, lo:hi], X[b][:, 0:hi - lo], par[:, i, 8:9], par[:, i, 9:10],
                                      ALU.mult, ALU.add)
                dve.drain()
                dve.tensor_tensor(kk[:, :], kk[:, :], ksq[:, :], ALU.add)
                dve.drain()
                dve.tensor_tensor(oo[:, :], kk[:, :], gg[:, :], ALU.mult).then_inc(v_s.step("oa"), 1)
                dve.drain()
            every_pair(dve, body)


def ret_stage(nc, K, a):
    with ExitStack() as ctx:
        def sb(name, shape, dt=F32):
            return ctx.enter_context(nc.sbuf_tensor("ret_" + name, shape, dt))

        def sem(name):
            return ctx.enter_context(nc.semaphore("ret_" + name))

        TILES = ["q", "k", "v0", "v1", "g0", "g1"]
        raw = sb("w", [P, 2, DC, P])
        wh, wl = sb("wh", [P, 2, DC, P], F32R), sb("wl", [P, 2, DC, P], F32R)
        vf = sb("vf", [P, 2, T])
        con = sb("con", [P, RET_CON])
        cos, sin, perm = sb("cos", [P, T]), sb("sin", [P, T]), sb("perm", [P, P])
        qr, kr, tmp = sb("qr", [P, T]), sb("kr", [P, T]), sb("tmp", [P, T])
        qt, kt, qd = sb("qt", [P, T]), sb("kt", [P, T]), sb("qd", [P, T])
        vt = sb("vt", [P, NRC + 1, VH])
        sm = sb("sm", [P, NRC + 1, RC])
        kd = sb("kd", [P, NRC, P])
        kds = sb("kds", [TS, NSEQ, P])
        rst = sb("rst", [P, 2, VH])
        r0, rout = sb("r0", [P, NSEQ, VH]), sb("rout", [P, NSEQ, VH])
        ot, o2, gate, ob = (sb(x, [P, 2, T]) for x in ("ot", "o2", "gate", "ob"))
        rstd = sb("rstd", [P, T])
        qdec, dm, dms = con[:, 0:T], con[:, T:T + RC], con[0:TS, T + RC:T + RC + TS]
        o = T + RC + TS
        kdec, gc, gs, kdecs = con[:, o:o + 1], con[:, o + 1:o + 2], con[:, o + 2:o + 3], con[0:TS, o + 3:o + 3 + NSEQ]
        NT = NRC + 1
        pe_s = Steps(sem("tensor"), ["q", "k", "v0", "v1", "swq", "swk", "g0", "g1", "t0", "t1", "t2"]
                     + [f"s{c}" for c in range(NT)] + [x for c in range(NRC) for x in (f"o{c}", f"R{c}")]
                     + [f"o{NRC}"] + [f"RS{p}" for p in range(4)] + ["ss"])
        v_s = Steps(sem("vector"), ["lv0", "lv1", "lg0", "q", "k", "lg1"] + [f"s{c}" for c in range(NT)] + ["lq"]
                    + [f"R{c}" for c in range(NRC)] + [f"RS{p}" for p in range(4)] + ["lk", "ms", "ob"])
        a_s = Steps(sem("scalar"), ["q", "hv0", "k", "hv1", "v0", "hg0", "v1", "hg1", "g0", "hq", "g1",
                                    "vt0", "vt1", "vt2", "hk"] + [f"o{c}" for c in range(NT)] + ["sq", "rstd"])
        wts = [sem("w_even"), sem("w_odd")]
        split_h, split_l, first = sem("hn_high"), sem("hn_low"), sem("first_parts")
        cons, consts, r0s, stored = sem("head_consts"), sem("consts"), sem("state_in"), sem("stored")
        Z = [K.ps[:, 2 * n:2 * n + 2, 0:HT] for n in range(4)]
        X = [K.ps[:, 4 + b, :] for b in range(4)]

        def chunk(c):
            return slice(RC * c, RC * c + (RC if c < NRC else TS))

        def every_head(eng, body):
            with eng.Fori(0, HB - 1) as i:
                body(i, False)
            body(HB - 1, True)

        def parts(x):
            slot = TILES.index(x) % 2
            return raw[:, slot, :, :], wh[:, slot, :, :], wl[:, slot, :, :]

        block = ctx.enter_context(nc.Block())

        @block.sync
        def _(sp):
            for dst, src in ((cos, "c_cos"), (sin, "c_sin"), (perm, "c_perm")):
                sp.dma_start(dst[:, :], a[src]).then_inc(consts, 16)

            def load(i, x):
                t = TILES.index(x)
                sp.dma_start(raw[:, t % 2, :, :], a["w_ret"][i, t]).then_inc(wts[t % 2], 16)

            load(0, "q")
            load(0, "k")

            def body(i, last):
                for x, before, back in (("v0", "lq", 1), ("v1", "lk", 1)):
                    sp.wait_ge(v_s.sem, v_s.of(i, before, back))
                    load(i, x)
                sp.wait_ge(v_s.sem, v_s.of(i, "ms", 1))
                sp.dma_start(con[:, :], a["c_ret"][i]).then_inc(cons, 16)
                sp.dma_start(r0[:, :, :], a["ret_in"][i]).then_inc(r0s, 16)
                for x, before in (("g0", "lv0"), ("g1", "lv1")):
                    sp.wait_ge(v_s.sem, v_s.of(i, before))
                    load(i, x)
                for x, before in (("q", "lg0"), ("k", "lg1")):
                    if not last:
                        sp.wait_ge(v_s.sem, v_s.of(i, before))
                        load(i + 1, x)
            every_head(sp, body)

        @block.tensor
        def _(pe):
            pe_s.ahead(pe)
            pe.wait_ge(consts, 48)
            pe.wait_ge(split_l, DC)

            def body(i, last_head):
                def matrix(x, z, back=0):
                    slot = TILES.index(x) % 2
                    if x != "q":
                        pe.wait_ge(v_s.sem, v_s.of(i, "l" + x, back))
                    project3(pe, Z[z], wh[:, slot, :, :], wl[:, slot, :, :], K.high, K.low).then_inc(pe_s.step(x), 1)

                def swap(x, z, src):
                    pe.wait_ge(a_s.sem, a_s.of(i, x))
                    for h in range(2):
                        last = pe.matmul(Z[z][:, h, :], perm[:, :], src[:, h * HT:(h + 1) * HT], start=True, stop=True)
                    last.then_inc(pe_s.step("sw" + x), 1)

                pe.wait_ge(v_s.sem, v_s.of(i, "ms", 1))
                matrix("q", 0, 1)
                matrix("k", 1, 1)
                matrix("v0", 2)
                matrix("v1", 3)
                swap("q", 0, qr)
                swap("k", 1, kr)
                pe.wait_ge(a_s.sem, a_s.of(i, "v0"))
                matrix("g0", 2)
                pe.wait_ge(a_s.sem, a_s.of(i, "v1"))
                matrix("g1", 3)
                pe.wait_ge(v_s.sem, v_s.of(i, "k"))
                for c in range(NT):
                    n = RC if c < NRC else TS
                    for h in range(2):
                        o = VH * (c % 2) + P * h
                        last = pe.transpose(K.ps[0:n, c // 2, o:o + P], vf[:, h, chunk(c)], K.ident[:, :])
                    if c % 2 or c == NRC:
                        last.then_inc(pe_s.step(f"t{c // 2}"), 1)
                pe.wait_ge(a_s.sem, a_s.of(i, "g1"))
                for c in range(NT):
                    if c >= 2:
                        pe.wait_ge(v_s.sem, v_s.of(i, f"s{c - 2}"))
                    n = RC if c < NRC else TS
                    pe.matmul(X[2 + c % 2][0:n, 0:n], kt[:, chunk(c)], qt[:, chunk(c)], start=True, stop=True)
                    pe.transpose(X[2 + c % 2][0:n, RC:RC + P], kt[:, chunk(c)], K.ident[:, :])\
                        .then_inc(pe_s.step(f"s{c}"), 1)
                for c in range(NRC):
                    pe.wait_ge(v_s.sem, v_s.of(i, f"R{c - 1}" if c else f"s{NRC}"))
                    pe.wait_ge(a_s.sem, a_s.of(i, f"o{c - 1}" if c else "vt2"))
                    for h in range(2):
                        y = X[0][:, RC * h:RC * h + RC]
                        last = pe.matmul(y, vt[:, c, P * h:P * h + P], sm[:, c, :], start=True, stop=(c == 0))
                        if c:
                            last = pe.matmul(y, rst[:, c % 2, P * h:P * h + P], qd[:, chunk(c)], start=False, stop=True)
                    last.then_inc(pe_s.step(f"o{c}"), 1)
                    pe.matmul(X[1][:, 0:VH], kd[:, c, :], vt[:, c, :], start=True, stop=True)\
                        .then_inc(pe_s.step(f"R{c}"), 1)
                pe.wait_ge(a_s.sem, a_s.of(i, f"o{NRC - 1}"))
                pe.wait_ge(r0s, 16 * i + 16)
                for h in range(2):
                    y = X[0][:, TS * h:TS * h + TS]
                    pe.matmul(y, vt[0:TS, NRC, P * h:P * h + P], sm[0:TS, NRC, 0:TS], start=True, stop=False)
                    for b in range(NSEQ):
                        q = slice(TP + LSEQ * b, TP + LSEQ * b + LSEQ)
                        last = pe.matmul(y[:, LSEQ * b:LSEQ * b + LSEQ], r0[:, b, P * h:P * h + P], qd[:, q],
                                         start=False, stop=(b == NSEQ - 1))
                last.then_inc(pe_s.step(f"o{NRC}"), 1)
                for p in range(4):
                    pe.wait_ge(v_s.sem, v_s.of(i, f"R{NRC - 1}" if p < 3 else "RS0"))
                    for b in (2 * p, 2 * p + 1):
                        last = pe.matmul(X[1 + p % 3][:, VH * (b % 2):VH * (b % 2) + VH], kds[:, b, :],
                                         vt[0:TS, NRC, :], start=True, stop=True)
                    last.then_inc(pe_s.step(f"RS{p}"), 1)
                pe.wait_ge(a_s.sem, a_s.of(i, "sq"))
                for h in range(2):
                    for k in range(2):
                        last = pe.matmul(Z[0][:, h, :], K.ones[:, :], o2[:, k, h * HT:(h + 1) * HT],
                                         start=(k == 0), stop=(k == 1))
                last.then_inc(pe_s.step("ss"), 1)
            every_head(pe, body)

        @block.scalar
        def _(act):
            a_s.ahead(act)
            act.sem_inc(stored, 48)
            for c in range(DC):
                act.copy(K.high[:, c, :], K.hn[:, c, :]).then_inc(split_h, 1)
            for n, x in enumerate(("q", "k")):
                w, high, _ = parts(x)
                act.wait_ge(wts[n], 16)
                act.copy(high, w).then_inc(first, 1)

            def body(i, last):
                def done(x):
                    act.wait_ge(pe_s.sem, pe_s.of(i, x))

                def high(x, turn=0):
                    t = TILES.index(x)
                    w, hi, _ = parts(x)
                    if turn and last:
                        act.drain().then_inc(a_s.step("h" + x), 1)
                    else:
                        act.wait_ge(wts[t % 2], 48 * (i + turn) + 16 * (t // 2) + 16)
                        act.copy(hi, w).then_inc(a_s.step("h" + x), 1)

                done("q")
                act.copy(halves(qr[:, :]), Z[0]).then_inc(a_s.step("q"), 1)
                high("v0")
                done("k")
                act.activation(halves(kr[:, :]), Z[1], ACT.Copy, scale=float(P) ** -0.5).then_inc(a_s.step("k"), 1)
                high("v1")
                for h in range(2):
                    done(f"v{h}")
                    act.copy(halves(vf[:, h, :]), Z[2 + h]).then_inc(a_s.step(f"v{h}"), 1)
                    high(f"g{h}")
                done("g0")
                act.wait_ge(v_s.sem, v_s.of(i, "ob", 1))
                act.activation(halves(gate[:, 0, :]), Z[2], ACT.Silu).then_inc(a_s.step("g0"), 1)
                high("q", 1)
                done("g1")
                act.activation(halves(gate[:, 1, :]), Z[3], ACT.Silu).then_inc(a_s.step("g1"), 1)
                for b in range(2):
                    done(f"t{b}")
                    act.copy(vt[:, 2 * b:2 * b + 2, :], K.ps[:, b, :].rearrange("p (c v) -> p c v", c=2))\
                        .then_inc(a_s.step(f"vt{b}"), 1)
                done("t2")
                act.copy(vt[0:TS, NRC, :], K.ps[0:TS, 2, 0:VH]).then_inc(a_s.step("vt2"), 1)
                high("k", 1)
                for c in range(NT):
                    n = RC if c < NRC else TS
                    act.wait_ge(pe_s.sem, pe_s.of(i, f"o{c}"))
                    act.copy(ot[:, :, chunk(c)], X[0][:, 0:2 * n].rearrange("p (h t) -> p h t", h=2))\
                        .then_inc(a_s.step(f"o{c}"), 1)
                act.drain()
                act.activation(o2[:, :, :], ot[:, :, :], ACT.Square).then_inc(a_s.step("sq"), 1)
                act.wait_ge(v_s.sem, v_s.of(i, "ms"))
                act.activation(rstd[:, :], rstd[:, :], ACT.Ln)
                act.drain()
                act.activation(rstd[:, :], rstd[:, :], ACT.Exp, scale=-0.5).then_inc(a_s.step("rstd"), 1)
                act.wait_ge(v_s.sem, v_s.of(i, "ob"))
                act.dma_start(K.ob[i], ob[:, :, :]).then_inc(stored, 16)
                act.dma_start(a["ret_out"][i, :, 0, :], rst[:, NRC % 2, :]).then_inc(stored, 16)
                act.dma_start(a["ret_out"][i, :, 1:1 + NSEQ, :], rout[:, :, :]).then_inc(stored, 16)
            every_head(act, body)
            act.wait_ge(stored, 48 * HB + 48)

        @block.vector
        def _(dve):
            for c in range(DC):
                dve.wait_ge(split_h, c + 1)
                low(dve, K.low[:, c, :], K.hn[:, c, :], K.high[:, c, :]).then_inc(split_l, 1)
            for n, x in enumerate(("q", "k")):
                w, hi, lo = parts(x)
                dve.wait_ge(first, n + 1)
                low(dve, lo, w, hi)
            dve.drain()
            v_s.ahead(dve)
            dve.wait_ge(consts, 48)

            def body(i, last_head):
                def lows(x, turn=0):
                    w, hi, lo = parts(x)
                    if turn and last_head:
                        dve.drain().then_inc(v_s.step("l" + x), 1)
                    else:
                        dve.wait_ge(a_s.sem, a_s.of(i, "h" + x))
                        low(dve, lo, w, hi).then_inc(v_s.step("l" + x), 1)

                lows("v0")
                lows("v1")
                lows("g0")
                dve.wait_ge(cons, 16 * i + 16)
                for x, z, src, out in (("q", 0, qr, qt), ("k", 1, kr, kt)):
                    dve.wait_ge(pe_s.sem, pe_s.of(i, "sw" + x))
                    dve.tensor_tensor(halves(tmp[:, :]), Z[z], halves(sin[:, :]), ALU.mult)
                    dve.tensor_tensor(out[:, :], src[:, :], cos[:, :], ALU.mult)
                    dve.drain()
                    last = dve.tensor_tensor(out[:, :], out[:, :], tmp[:, :], ALU.add)
                    if x == "k":
                        last = dve.tensor_tensor(qd[:, :], qt[:, :], qdec, ALU.mult)
                    last.then_inc(v_s.step(x), 1)
                    dve.drain()
                lows("g1")
                for c in range(NT):
                    n = RC if c < NRC else TS
                    x = X[2 + c % 2]
                    dve.wait_ge(pe_s.sem, pe_s.of(i, f"s{c}"))
                    dve.tensor_tensor(sm[0:n, c, 0:n], x[0:n, 0:n], dm if c < NRC else dms, ALU.mult)
                    if c < NRC:
                        last = dve.tensor_scalar(kd[:, c, :], x[:, RC:RC + P], kdec, None, ALU.mult)
                    else:
                        last = dve.tensor_tensor(kds[:, :, :], x[0:n, RC:RC + P].unsqueeze(1).broadcast_to([TS, NSEQ, P]),
                                                 kdecs.unsqueeze(2).broadcast_to([TS, NSEQ, P]), ALU.mult)
                    last.then_inc(v_s.step(f"s{c}"), 1)
                dve.drain()
                lows("q", 1)
                dve.wait_ge(stored, 48 * i + 48)
                for c in range(NRC):
                    dve.wait_ge(pe_s.sem, pe_s.of(i, f"R{c}"))
                    if c == 0:
                        last = dve.tensor_copy(rst[:, 1, :], X[1][:, 0:VH])
                    else:
                        last = dve.scalar_tensor_tensor(out=rst[:, (c + 1) % 2, :], in0=rst[:, c % 2, :], scalar=gc,
                                                        in1=X[1][:, 0:VH], op0=ALU.mult, op1=ALU.add)
                    last.then_inc(v_s.step(f"R{c}"), 1)
                    dve.drain()
                for p in range(4):
                    dve.wait_ge(pe_s.sem, pe_s.of(i, f"RS{p}"))
                    dve.scalar_tensor_tensor(out=rout[:, 2 * p:2 * p + 2, :], in0=r0[:, 2 * p:2 * p + 2, :], scalar=gs,
                                             in1=X[1 + p % 3].rearrange("p (b v) -> p b v", b=2),
                                             op0=ALU.mult, op1=ALU.add).then_inc(v_s.step(f"RS{p}"), 1)
                lows("k", 1)
                dve.wait_ge(pe_s.sem, pe_s.of(i, "ss"))
                dve.tensor_scalar(halves(rstd[:, :]), Z[0], 1.0 / VH, EPS, ALU.mult, ALU.add)\
                    .then_inc(v_s.step("ms"), 1)
                dve.tensor_tensor(ob[:, :, :], ot[:, :, :], gate[:, :, :], ALU.mult)
                dve.drain()
                dve.wait_ge(a_s.sem, a_s.of(i, "rstd"))
                dve.tensor_tensor(ob[:, :, :], ob[:, :, :], rstd[:, :].unsqueeze(1).broadcast_to([P, 2, T]), ALU.mult)\
                    .then_inc(v_s.step("ob"), 1)
                dve.drain()
            every_head(dve, body)


def merge_a_stage(nc, K, a, m):
    with ExitStack() as ctx:
        def sb(name, shape, dt=F32):
            return ctx.enter_context(nc.sbuf_tensor("ma_" + name, shape, dt))

        def sem(name):
            return ctx.enter_context(nc.semaphore("ma_" + name))

        KT = {"ga": DC, "pa": PAIRS, "gb": DC}
        oh, oa = sb("oa_high", [P, PAIRS, T], F32R), sb("oa", [P, PAIRS, T])
        ol = overlaid(nc, "ma_oa_low", [P, PAIRS, T])
        acts = {"ga": (K.high, K.low), "pa": (oh, ol), "gb": (K.high, K.low)}
        raw_g, raw_p = sb("w_g", [P, DC, P]), sb("w_p", [P, PAIRS, P])
        raw = {"ga": raw_g, "pa": raw_p, "gb": raw_g}
        high, lows = ({x: sb(y + x, [P, k, P], F32R) for x, k in KT.items()} for y in ("high_", "low_"))
        ga, gb = sb("ga", [P, T]), sb("gb", [P, T])
        Z = {x: K.ps[:, 2 * n:2 * n + 2, 0:HT] for n, x in enumerate(KT)}
        pe_s = Steps(sem("tensor"), list(KT))
        a_s = Steps(sem("scalar"), ["hgb", "ga", "hga", "hpa", "gb"])
        v_s = Steps(sem("vector"), ["lgb", "lga", "m", "lpa"])
        wt = {x: sem("w_in_" + x) for x in KT}
        loaded, stored, first = sem("loaded"), sem("stored"), sem("first_parts")
        oa_split = sem("oa_split")
        block = ctx.enter_context(nc.Block())

        def every_tile(eng, body):
            with eng.Fori(0, DC - 1) as i:
                body(i, False)
            body(DC - 1, True)

        @block.sync
        def _(sp):
            def load(i, x):
                sp.dma_start(raw[x][:, :, :], a["w_" + x][i]).then_inc(wt[x], 16)

            load(0, "ga")
            load(0, "pa")
            sp.dma_start(oa[:, :, :], K.oa.rearrange("i p t -> p i t")).then_inc(loaded, 16)

            def body(i, last):
                sp.wait_ge(v_s.sem, v_s.of(i, "lga", 1))
                load(i, "gb")
                if not last:
                    sp.wait_ge(v_s.sem, v_s.of(i, "lpa", 1))
                    load(i + 1, "pa")
                    sp.wait_ge(v_s.sem, v_s.of(i, "lgb"))
                    load(i + 1, "ga")
                sp.wait_ge(a_s.sem, a_s.of(i, "gb"))
                sp.dma_start(K.gb[i], gb[:, :]).then_inc(stored, 16)
            sp.sem_inc(stored, 16)
            every_tile(sp, body)
            sp.wait_ge(stored, 16 * DC + 16)

        @block.tensor
        def _(pe):
            pe_s.ahead(pe)

            def body(i, last):
                for x, part, back, of, read in (("ga", "lga", 1, a_s, "ga"), ("pa", "lpa", 1, None, None),
                                                ("gb", "lgb", 0, a_s, "gb")):
                    if x == "pa":
                        pe.wait_ge(oa_split, 1)
                    pe.wait_ge(v_s.sem, v_s.of(i, part, back))
                    if of:
                        pe.wait_ge(of.sem, of.of(i, read, 1))
                    project3(pe, Z[x], high[x], lows[x], *acts[x], k=KT[x]).then_inc(pe_s.step(x), 1)
            every_tile(pe, body)

        @block.scalar
        def _(act):
            for x in ("ga", "pa"):
                act.wait_ge(wt[x], 16)
                act.copy(high[x][:, :, :], raw[x][:, :, :]).then_inc(first, 1)
            act.wait_ge(loaded, 16)
            act.copy(oh[:, :, :], oa[:, :, :]).then_inc(first, 1)
            a_s.ahead(act)

            def body(i, last):
                def part(x, turn):
                    if turn and last:
                        act.drain().then_inc(a_s.step("h" + x), 1)
                    else:
                        act.wait_ge(pe_s.sem, pe_s.of(i, x, 1 - turn))
                        act.wait_ge(wt[x], 16 * (i + turn) + 16)
                        act.copy(high[x][:, :, :], raw[x][:, :, :]).then_inc(a_s.step("h" + x), 1)

                part("gb", 0)
                act.wait_ge(pe_s.sem, pe_s.of(i, "ga"))
                act.wait_ge(v_s.sem, v_s.of(i, "m", 1))
                act.activation(halves(ga[:, :]), Z["ga"], ACT.Sigmoid).then_inc(a_s.step("ga"), 1)
                part("ga", 1)
                part("pa", 1)
                act.wait_ge(pe_s.sem, pe_s.of(i, "gb"))
                act.wait_ge(stored, 16 * i + 16)
                act.activation(halves(gb[:, :]), Z["gb"], ACT.Sigmoid).then_inc(a_s.step("gb"), 1)
            every_tile(act, body)

        @block.vector
        def _(dve):
            for n, x in enumerate(("ga", "pa")):
                dve.wait_ge(first, n + 1)
                low(dve, lows[x][:, :, :], raw[x][:, :, :], high[x][:, :, :])
            dve.drain()
            v_s.ahead(dve)
            dve.wait_ge(first, 3)
            low(dve, ol[:, :, :], oa[:, :, :], oh[:, :, :]).then_inc(oa_split, 1)

            def body(i, last):
                def part(x, turn):
                    if turn and last:
                        dve.drain().then_inc(v_s.step("l" + x), 1)
                    else:
                        dve.wait_ge(a_s.sem, a_s.of(i, "h" + x))
                        low(dve, lows[x][:, :, :], raw[x][:, :, :], high[x][:, :, :]).then_inc(v_s.step("l" + x), 1)

                part("gb", 0)
                part("ga", 1)
                dve.wait_ge(pe_s.sem, pe_s.of(i, "pa"))
                dve.wait_ge(a_s.sem, a_s.of(i, "ga"))
                dve.tensor_tensor(halves(m[:, i, :]), halves(ga[:, :]), Z["pa"], ALU.mult).then_inc(v_s.step("m"), 1)
                part("pa", 1)
            every_tile(dve, body)


class Pairs:

    def __init__(self, nc, ctx, tag, a_names, v_names):
        def sb(name, dt=F32):
            return ctx.enter_context(nc.sbuf_tensor(tag + name, [P, 2, DC, P], dt))

        def sem(name):
            return ctx.enter_context(nc.semaphore(tag + name))

        self.raw, self.high, self.low = sb("w"), sb("w_high", F32R), sb("w_low", F32R)
        self.pe_s = Steps(sem("tensor"), ["0", "1"])
        self.a_s, self.v_s = Steps(sem("scalar"), a_names), Steps(sem("vector"), v_names)
        self.wt, self.first = [sem("w_in0"), sem("w_in1")], sem("first_parts")
        self.N = DC // 2


def every_turn(eng, n, body):
    with eng.Fori(0, n - 1) as i:
        body(i, False)
    body(n - 1, True)


def merge_b_stage(nc, K, a, m, m_low, oh, m_high):
    with ExitStack() as ctx:
        def sem(name):
            return ctx.enter_context(nc.semaphore("mb_" + name))

        ob = ctx.enter_context(nc.sbuf_tensor("mb_ob", [P, 2 * HB, T], F32))
        ol = overlaid(nc, "mb_ob_low", [P, 2 * HB, T])
        side = ctx.enter_context(nc.sbuf_tensor("mb_gate", [P, 2, T], F32))
        W = Pairs(nc, ctx, "mb_", ["h0", "r0", "h1", "r1"], ["m0", "l0", "r0", "m1", "l1", "r1"])
        pe_s, a_s, v_s = W.pe_s, W.a_s, W.v_s
        gates, loaded = [sem("gate_in0"), sem("gate_in1")], [sem(f"ob_in{q}") for q in range(4)]
        Z = [K.ps[:, 2 * u:2 * u + 2, 0:HT] for u in range(2)]
        block = ctx.enter_context(nc.Block())

        @block.sync
        def _(sp):
            for q in range(4):
                sp.dma_start(ob[:, 4 * q:4 * q + 4, :].rearrange("p (i h) t -> p i h t", h=2),
                             K.ob[2 * q:2 * q + 2].rearrange("i p h t -> p i h t")).then_inc(loaded[q], 16)
                if q < 2:
                    sp.dma_start(W.raw[:, q, :, :], a["w_pb"][q]).then_inc(W.wt[q], 16)
            for u in range(2):
                sp.dma_start(side[:, u, :], K.gb[u]).then_inc(gates[u], 16)
            with sp.Fori(0, W.N - 1) as i:
                for u in range(2):
                    sp.wait_ge(v_s.sem, v_s.of(i, f"l{u}", 1))
                    sp.dma_start(W.raw[:, u, :, :], a["w_pb"][2 * i + 2 + u]).then_inc(W.wt[u], 16)
                    sp.wait_ge(v_s.sem, v_s.of(i, f"m{u}"))
                    sp.dma_start(side[:, u, :], K.gb[2 * i + 2 + u]).then_inc(gates[u], 16)

        @block.tensor
        def _(pe):
            pe_s.ahead(pe)

            def body(i, last):
                for u in range(2):
                    pe.wait_ge(v_s.sem, v_s.of(i, f"l{u}", 1))
                    project3(pe, Z[u], W.high[:, u, :, :], W.low[:, u, :, :], oh, ol).then_inc(pe_s.step(str(u)), 1)
            every_turn(pe, W.N, body)

        @block.scalar
        def _(act):
            for q in range(4):
                s = slice(4 * q, 4 * q + 4)
                act.wait_ge(loaded[q], 16)
                act.copy(oh[:, s, :], ob[:, s, :]).then_inc(W.first, 1)
                if q < 2:
                    act.wait_ge(W.wt[q], 16)
                    act.copy(W.high[:, q, :, :], W.raw[:, q, :, :]).then_inc(W.first, 1)
            a_s.ahead(act)

            def body(i, last):
                for u in range(2):
                    if last:
                        act.drain().then_inc(a_s.step(f"h{u}"), 1)
                    else:
                        act.wait_ge(pe_s.sem, pe_s.of(i, str(u)))
                        act.wait_ge(W.wt[u], 16 * i + 32)
                        act.copy(W.high[:, u, :, :], W.raw[:, u, :, :]).then_inc(a_s.step(f"h{u}"), 1)
                    act.wait_ge(v_s.sem, v_s.of(i, f"m{u}"))
                    act.copy(m_high[:, 2 * i + u, :], m[:, 2 * i + u, :]).then_inc(a_s.step(f"r{u}"), 1)
            every_turn(act, W.N, body)

        @block.vector
        def _(dve):
            for q in range(4):
                s = slice(4 * q, 4 * q + 4)
                dve.wait_ge(W.first, (1, 3, 5, 6)[q])
                low(dve, ol[:, s, :], ob[:, s, :], oh[:, s, :])
                if q < 2:
                    dve.wait_ge(W.first, 2 * q + 2)
                    low(dve, W.low[:, q, :, :], W.raw[:, q, :, :], W.high[:, q, :, :])
            dve.drain()
            v_s.ahead(dve)

            def body(i, last):
                for u in range(2):
                    total = m[:, 2 * i + u, :]
                    dve.wait_ge(pe_s.sem, pe_s.of(i, str(u)))
                    dve.wait_ge(gates[u], 16 * i + 16)
                    dve.tensor_tensor(halves(side[:, u, :]), halves(side[:, u, :]), Z[u], ALU.mult)
                    dve.drain()
                    dve.tensor_tensor(total, total, side[:, u, :], ALU.add).then_inc(v_s.step(f"m{u}"), 1)
                    if last:
                        dve.drain().then_inc(v_s.step(f"l{u}"), 1)
                    else:
                        dve.wait_ge(a_s.sem, a_s.of(i, f"h{u}"))
                        low(dve, W.low[:, u, :, :], W.raw[:, u, :, :], W.high[:, u, :, :])\
                            .then_inc(v_s.step(f"l{u}"), 1)
                    dve.wait_ge(a_s.sem, a_s.of(i, f"r{u}"))
                    low(dve, m_low[:, 2 * i + u, :], total, m_high[:, 2 * i + u, :]).then_inc(v_s.step(f"r{u}"), 1)
            every_turn(dve, W.N, body)


def out_stage(nc, K, a, m_high, m_low, x1):
    with ExitStack() as ctx:
        W = Pairs(nc, ctx, "out_", ["h0", "h1"], ["0", "l0", "1", "l1"])
        pe_s, a_s, v_s = W.pe_s, W.a_s, W.v_s
        loaded = ctx.enter_context(nc.semaphore("out_x_in"))
        Z = [K.ps[:, 2 * u:2 * u + 2, 0:HT] for u in range(2)]
        block = ctx.enter_context(nc.Block())

        @block.sync
        def _(sp):
            for u in range(2):
                sp.dma_start(W.raw[:, u, :, :], a["w_out"][u]).then_inc(W.wt[u], 16)
            sp.dma_start(x1[:, :, :], a["x"]).then_inc(loaded, 16)
            with sp.Fori(0, W.N - 1) as i:
                for u in range(2):
                    sp.wait_ge(v_s.sem, v_s.of(i, f"l{u}", 1))
                    sp.dma_start(W.raw[:, u, :, :], a["w_out"][2 * i + 2 + u]).then_inc(W.wt[u], 16)

        @block.tensor
        def _(pe):
            pe_s.ahead(pe)

            def body(i, last):
                for u in range(2):
                    pe.wait_ge(v_s.sem, v_s.of(i, f"l{u}", 1))
                    project3(pe, Z[u], W.high[:, u, :, :], W.low[:, u, :, :], m_high, m_low)\
                        .then_inc(pe_s.step(str(u)), 1)
            every_turn(pe, W.N, body)

        @block.scalar
        def _(act):
            for u in range(2):
                act.wait_ge(W.wt[u], 16)
                act.copy(W.high[:, u, :, :], W.raw[:, u, :, :]).then_inc(W.first, 1)
            a_s.ahead(act)
            with act.Fori(0, W.N - 1) as i:
                for u in range(2):
                    act.wait_ge(pe_s.sem, pe_s.of(i, str(u)))
                    act.wait_ge(W.wt[u], 16 * i + 32)
                    act.copy(W.high[:, u, :, :], W.raw[:, u, :, :]).then_inc(a_s.step(f"h{u}"), 1)

        @block.vector
        def _(dve):
            for u in range(2):
                dve.wait_ge(W.first, u + 1)
                low(dve, W.low[:, u, :, :], W.raw[:, u, :, :], W.high[:, u, :, :])
            dve.drain()
            v_s.ahead(dve)
            dve.wait_ge(loaded, 16)

            def body(i, last):
                for u in range(2):
                    x = halves(x1[:, 2 * i + u, :])
                    dve.wait_ge(pe_s.sem, pe_s.of(i, str(u)))
                    dve.tensor_tensor(x, x, Z[u], ALU.add).then_inc(v_s.step(str(u)), 1)
                    if last:
                        dve.drain().then_inc(v_s.step(f"l{u}"), 1)
                    else:
                        dve.wait_ge(a_s.sem, a_s.of(i, f"h{u}"))
                        low(dve, W.low[:, u, :, :], W.raw[:, u, :, :], W.high[:, u, :, :])\
                            .then_inc(v_s.step(f"l{u}"), 1)
            every_turn(dve, W.N, body)


def route_stage(nc, K, a, top_v, top_i):
    with ExitStack() as ctx:
        def sb(name, shape, dt=F32):
            return ctx.enter_context(nc.sbuf_tensor("rt_" + name, shape, dt))

        def sem(name):
            return ctx.enter_context(nc.semaphore("rt_" + name))

        w = sb("w", [P, DC, P])
        wh, wl = sb("wh", [P, 2, DC, P], F32R), sb("wl", [P, 2, DC, P], F32R)
        keys = sb("keys", [P, 2 * PH, NK])
        qt = sb("qt", [P, 2, T])
        sc = sb("sc", [P, 2, NTT, NK])
        s2 = sb("s2", [P, NTT, NK])
        val, idx = sb("val", [P, NTT, TOPK]), sb("idx", [P, NTT, TOPK], U32)
        pe_s = Steps(sem("tensor"), ["q0", "q1", "s0", "s1"])
        a_s = Steps(sem("scalar"), ["q0", "w0", "q1", "w1", "s0", "s1"])
        v_s = Steps(sem("vector"), ["w0", "w1", "met0", "0", "met1", "1"])
        wt, loaded, zeroed, first = sem("w"), sem("keys_in"), sem("zeroed"), sem("first_parts")
        block = ctx.enter_context(nc.Block())

        @block.sync
        def _(sp):
            sp.dma_start(keys[:, :, :], a["keys"]).then_inc(loaded, 16)
            sp.dma_start(w[:, :, :], a["w_q"][0]).then_inc(wt, 16)
            sp.wait_ge(first, 2)
            sp.dma_start(w[:, :, :], a["w_q"][1]).then_inc(wt, 16)
            with sp.Fori(0, PH - 1) as i:
                for u in range(2):
                    sp.wait_ge(v_s.sem, v_s.of(i, "w1", 1) if u == 0 else v_s.of(i, "w0"))
                    sp.dma_start(w[:, :, :], a["w_q"][2 * i + 2 + u]).then_inc(wt, 16)

        def every_turn(eng, body):
            with eng.Fori(0, PH - 1) as i:
                body(i, False)
            body(PH - 1, True)

        @block.gpsimd
        def _(pool):
            pool.memset(sc[:, :, NTT - 1, :], 0.0).then_inc(zeroed, 1)

        @block.tensor
        def _(pe):
            pe_s.ahead(pe)
            pe.wait_ge(loaded, 16)
            with pe.Fori(0, PH) as i:
                for u in range(2):
                    pe.wait_ge(v_s.sem, v_s.of(i, f"w{u}", 1))
                    pe.wait_ge(a_s.sem, a_s.of(i, f"q{u}", 1))
                    project3(pe, K.ps[:, 2 * u:2 * u + 2, 0:HT], wh[:, u, :, :], wl[:, u, :, :], K.hh, K.hl)\
                        .then_inc(pe_s.step(f"q{u}"), 1)
                for u in range(2):
                    pe.wait_ge(a_s.sem, a_s.last(i, [f"q{u}"]) if u else a_s.of(i, "q1"))
                    for n in range(NTT):
                        m = P if n < NTT - 1 else TS
                        last = pe.matmul(K.ps[0:m, 4 + 2 * u + n // 4, NK * (n % 4):NK * (n % 4) + NK],
                                         qt[:, u, P * n:P * n + m], keys[:, 2 * i + u, :], start=True, stop=True)
                    last.then_inc(pe_s.step(f"s{u}"), 1)

        @block.scalar
        def _(act):
            a_s.ahead(act)
            act.wait_ge(zeroed, 1)
            act.wait_ge(wt, 16)
            act.copy(wh[:, 0, :, :], w[:, :, :]).then_inc(first, 1)
            act.wait_ge(wt, 32)
            act.copy(wh[:, 1, :, :], w[:, :, :]).then_inc(first, 1)

            def body(i, last):
                for u in range(2):
                    act.wait_ge(pe_s.sem, pe_s.of(i, f"q{u}"))
                    act.copy(halves(qt[:, u, :]), K.ps[:, 2 * u:2 * u + 2, 0:HT]).then_inc(a_s.step(f"q{u}"), 1)
                    if last:
                        act.drain().then_inc(a_s.step(f"w{u}"), 1)
                    else:
                        act.wait_ge(wt, 32 * i + 16 * u + 48)
                        act.copy(wh[:, u, :, :], w[:, :, :]).then_inc(a_s.step(f"w{u}"), 1)
                for u in range(2):
                    act.wait_ge(pe_s.sem, pe_s.of(i, f"s{u}"))
                    act.wait_ge(v_s.sem, v_s.of(i, str(u), 1))
                    act.copy(sc[:, u, 0:4, :], K.ps[:, 4 + 2 * u, :].rearrange("p (n k) -> p n k", n=4))
                    act.copy(sc[0:TS, u, 4, :], K.ps[0:TS, 5 + 2 * u, 0:NK]).then_inc(a_s.step(f"s{u}"), 1)
            every_turn(act, body)

        @block.vector
        def _(dve):
            dve.wait_ge(first, 1)
            dve.tensor_tensor(wl[:, 0, :, :], w[:, :, :], wh[:, 0, :, :].bitcast(F32), ALU.subtract).then_inc(first, 1)
            dve.wait_ge(first, 3)
            dve.tensor_tensor(wl[:, 1, :, :], w[:, :, :], wh[:, 1, :, :].bitcast(F32), ALU.subtract)
            dve.drain()
            v_s.ahead(dve)

            def body(i, last):
                for u in range(2):
                    if last:
                        dve.drain().then_inc(v_s.step(f"w{u}"), 1)
                    else:
                        dve.wait_ge(a_s.sem, a_s.of(i, f"w{u}"))
                        dve.tensor_tensor(wl[:, u, :, :], w[:, :, :], wh[:, u, :, :].bitcast(F32), ALU.subtract)\
                            .then_inc(v_s.step(f"w{u}"), 1)
                for u in range(2):
                    dve.drain()
                    dve.wait_ge(a_s.sem, a_s.of(i, f"s{u}"))
                    dve.sem_inc(v_s.step(f"met{u}"), 1)
                    for n in range(NTT):
                        dve.max(val[:, n, 0:8], sc[:, u, n, :])
                    dve.drain()
                    for n in range(NTT):
                        dve.max_index(idx[:, n, 0:8], val[:, n, 0:8], sc[:, u, n, :])
                        dve.match_replace(s2[:, n, :], val[:, n, 0:8], sc[:, u, n, :], LEAST)
                    dve.drain()
                    for n in range(NTT):
                        dve.max(val[:, n, 8:16], s2[:, n, :])
                    dve.drain()
                    for n in range(NTT):
                        dve.max_index(idx[:, n, 8:16], val[:, n, 8:16], s2[:, n, :])
                    dve.drain()
                    dve.tensor_copy(top_v[:, :, 2 * i + u, :], val[:, :, :])
                    dve.tensor_copy(top_i[:, :, 2 * i + u, :], idx[:, :, :]).then_inc(v_s.step(str(u)), 1)
                    dve.drain()
            every_turn(dve, body)


def pick_stage(nc, K, a, top_v, top_i, slots):
    with ExitStack() as ctx:
        def sb(name, shape, dt=F32):
            return ctx.enter_context(nc.sbuf_tensor("pk_" + name, shape, dt))

        def sem(name):
            return ctx.enter_context(nc.semaphore("pk_" + name))

        cand, cand2, eq = (sb(x, [P, PH, TOPK * TOPK]) for x in ("cand", "cand2", "eq"))
        flat, pos = sb("flat", [P, PH, TOPK], U32), sb("pos", [P, 2, PH, TOPK], U32)
        posf, best = sb("posf", [P, 2, PH, TOPK]), sb("best", [P, PH, TOPK])
        ids = sb("ids", [P, 3, PH, TOPK])
        total = sb("total", [P, PH])
        iota = sb("iota", [P, TOPK])
        pe_s, a_s = Steps(sem("tensor"), ["t"]), Steps(sem("scalar"), ["e", "t"])
        v_s = Steps(sem("vector"), ["d", "ids"])
        loaded = sem("iota_in")
        block = ctx.enter_context(nc.Block())

        @block.sync
        def _(sp):
            sp.dma_start(iota[:, :], a["c_iota"][:, 0:TOPK]).then_inc(loaded, 16)

        @block.vector
        def _(dve):
            v_s.ahead(dve)
            dve.wait_ge(loaded, 16)
            with dve.Fori(0, NTT) as i:
                dve.wait_ge(pe_s.sem, pe_s.of(i, "t", 1))
                dve.tensor_tensor(cand[:, :, :].rearrange("p h (x y) -> p h x y", x=TOPK),
                                  top_v[:, i, 0:2 * PH:2, :].unsqueeze(3).broadcast_to([P, PH, TOPK, TOPK]),
                                  top_v[:, i, 1:2 * PH:2, :].unsqueeze(2).broadcast_to([P, PH, TOPK, TOPK]), ALU.add)
                dve.drain()
                for h in range(PH):
                    dve.max(best[:, h, 0:8], cand[:, h, :])
                dve.drain()
                for h in range(PH):
                    dve.max_index(flat[:, h, 0:8], best[:, h, 0:8], cand[:, h, :])
                    dve.match_replace(cand2[:, h, :], best[:, h, 0:8], cand[:, h, :], LEAST)
                dve.drain()
                for h in range(PH):
                    dve.max(best[:, h, 8:16], cand2[:, h, :])
                dve.drain()
                for h in range(PH):
                    dve.max_index(flat[:, h, 8:16], best[:, h, 8:16], cand2[:, h, :])
                gate = ids[:, 2, :, :]
                dve.tensor_tensor(gate, best[:, :, :], best[:, :, 0:1].broadcast_to([P, PH, TOPK]), ALU.subtract)\
                    .then_inc(v_s.step("d"), 1)
                dve.drain()
                dve.tensor_scalar(pos[:, 0, :, :], flat[:, :, :], 4, None, ALU.logical_shift_right)
                dve.tensor_scalar(pos[:, 1, :, :], flat[:, :, :], 15, None, ALU.bitwise_and)
                dve.drain()
                dve.tensor_copy(posf[:, :, :, :], pos[:, :, :, :])
                dve.drain()
                for s in range(2):
                    e = eq[:, :, :].rearrange("p h (x y) -> p h x y", x=TOPK)
                    dve.tensor_tensor(e, posf[:, s, :, :].unsqueeze(3).broadcast_to([P, PH, TOPK, TOPK]),
                                      iota[:, :].unsqueeze(1).unsqueeze(1).broadcast_to([P, PH, TOPK, TOPK]),
                                      ALU.is_equal)
                    dve.drain()
                    dve.tensor_tensor(e, e, top_i[:, i, s:2 * PH:2, :].unsqueeze(2)
                                      .broadcast_to([P, PH, TOPK, TOPK]), ALU.mult)
                    dve.drain()
                    dve.tensor_reduce(ids[:, s, :, :], e, AX.X, ALU.add)
                    dve.drain()
                dve.wait_ge(a_s.sem, a_s.of(i, "e"))
                dve.tensor_reduce(total[:, :], gate, AX.X, ALU.add)
                dve.drain()
                dve.reciprocal(total[:, :], total[:, :])
                dve.drain()
                dve.tensor_tensor(gate, gate, total[:, :].unsqueeze(2).broadcast_to([P, PH, TOPK]), ALU.mult)\
                    .then_inc(v_s.step("ids"), 1)
                dve.drain()

        @block.scalar
        def _(act):
            a_s.ahead(act)
            with act.Fori(0, NTT) as i:
                act.wait_ge(v_s.sem, v_s.of(i, "d"))
                act.activation(ids[:, 2, :, :], ids[:, 2, :, :], ACT.Exp).then_inc(a_s.step("e"), 1)
                act.wait_ge(pe_s.sem, pe_s.of(i, "t"))
                act.copy(slots[:, :, bass.ds(P * i, P)], K.ps[:, 0, 0:3 * P].rearrange("p (s t) -> p s t", s=3))\
                    .then_inc(a_s.step("t"), 1)

        @block.tensor
        def _(pe):
            pe_s.ahead(pe)
            with pe.Fori(0, NTT) as i:
                pe.wait_ge(v_s.sem, v_s.of(i, "ids"))
                pe.wait_ge(a_s.sem, a_s.of(i, "t", 1))
                for s in range(3):
                    last = pe.transpose(K.ps[:, 0, P * s:P * s + P], ids[:, s, :, :].rearrange("p h k -> p (h k)"),
                                        K.ident[:, :])
                last.then_inc(pe_s.step("t"), 1)


def gates_stage(nc, K, a, slots):
    with ExitStack() as ctx:
        def sb(name, shape):
            return ctx.enter_context(nc.sbuf_tensor("gt_" + name, shape, F32))

        def sem(name):
            return ctx.enter_context(nc.semaphore("gt_" + name))

        iota = sb("iota", [P, P])
        hot = sb("hot", [P, 2, 16, P])
        rows = sb("rows", [P, 16, P])
        stage = sb("stage", [P, 2, ROWS, TC])
        Q = ["0", "1", "2", "3"]
        pe_s, a_s = Steps(sem("tensor"), Q), Steps(sem("scalar"), Q)
        v_s, p_s = Steps(sem("vector"), Q), Steps(sem("pool"), Q)
        loaded, stored = sem("iota_in"), [sem("stored0"), sem("stored1")]
        PER = TC // 16
        NST = T // TC // 2
        block = ctx.enter_context(nc.Block())

        @block.sync
        def _(sp):
            sp.dma_start(iota[:, :], a["c_iota"]).then_inc(loaded, 16)
            for b in range(2):
                sp.sem_inc(stored[b], 16)
            with sp.Fori(0, NST) as s:
                for b in range(2):
                    sp.wait_ge(a_s.sem, a_s.of((2 * s + b) * PER + PER - 1, "3"))
                    sp.dma_start(K.gates[:, 2 * s + b, :, :], stage[:, b, :, :]).then_inc(stored[b], 16)
            for b in range(2):
                sp.wait_ge(stored[b], 16 * NST + 16)

        def turns(eng, body):
            with eng.Fori(0, NST) as s:
                for b in range(2):
                    with eng.Fori(0, PER) as q:
                        body((2 * s + b) * PER + q, s, b, q)

        @block.vector
        def _(dve):
            v_s.ahead(dve)
            dve.wait_ge(loaded, 16)

            def body(i, s, b, q):
                for g in range(4):
                    t = slice(4 * g, 4 * g + 4)
                    dve.wait_ge(pe_s.sem, pe_s.of(i, Q[g], 1))
                    dve.tensor_tensor(hot[:, :, t, :], iota[:, :].unsqueeze(1).unsqueeze(1).broadcast_to([P, 2, 4, P]),
                                      slots[:, 0:2, bass.ds(16 * i + 4 * g, 4)].unsqueeze(3)
                                      .broadcast_to([P, 2, 4, P]), ALU.is_equal).then_inc(v_s.step(Q[g]), 1)
            turns(dve, body)

        @block.gpsimd
        def _(pool):
            p_s.ahead(pool)

            def body(i, s, b, q):
                for g in range(4):
                    t = slice(4 * g, 4 * g + 4)
                    pool.wait_ge(v_s.sem, v_s.of(i, Q[g]))
                    pool.tensor_tensor(rows[:, t, :], hot[:, 0, t, :], slots[:, 2, bass.ds(16 * i + 4 * g, 4)]
                                       .unsqueeze(2).broadcast_to([P, 4, P]), ALU.mult).then_inc(p_s.step(Q[g]), 1)
            turns(pool, body)

        @block.tensor
        def _(pe):
            pe_s.ahead(pe)

            def body(i, s, b, q):
                for g in range(4):
                    pe.wait_ge(p_s.sem, p_s.of(i, Q[g]))
                    pe.wait_ge(a_s.sem, a_s.of(i, Q[g], 1))
                    for t in range(4):
                        last = pe.matmul(K.ps[:, g, P * t:P * t + P], hot[:, 1, 4 * g + t, :], rows[:, 4 * g + t, :],
                                         start=True, stop=True)
                    last.then_inc(pe_s.step(Q[g]), 1)
            turns(pe, body)

        @block.scalar
        def _(act):
            a_s.ahead(act)

            def body(i, s, b, q):
                act.wait_ge(stored[b], 16 * s + 16)
                for g in range(4):
                    act.wait_ge(pe_s.sem, pe_s.of(i, Q[g]))
                    act.copy(stage[:, b, :, bass.ds(16 * q + 4 * g, 4)].rearrange("p i t -> p t i"),
                             K.ps[:, g, :].rearrange("p (t i) -> p t i", t=4)).then_inc(a_s.step(Q[g]), 1)
            turns(act, body)


def experts_stage(nc, K, a, x1):
    R = 2
    with ExitStack() as ctx:
        def sb(name, shape, dt=F32):
            return ctx.enter_context(nc.sbuf_tensor("ex_" + name, shape, dt))

        def sem(name):
            return ctx.enter_context(nc.semaphore("ex_" + name))

        u, uh, ul = sb("u", [P, DC, P]), sb("uh", [P, R, DC, P], F32R), sb("ul", [P, R, DC, P], F32R)
        v, vh, vl = sb("v", [P, DC, P]), sb("vh", [P, R, DC, P], F32R), sb("vl", [P, R, DC, P], F32R)
        g, h = sb("g", [P, R, T]), sb("h", [P, R, T])
        hh, hl = sb("hh", [P, R, T], F32R), sb("hl", [P, R, T], F32R)
        V = [f"V{d}" for d in range(DC)]
        pe_s = Steps(sem("tensor"), ["U1", "U0"] + V)
        a_s = Steps(sem("scalar"), ["v0", "u0", "gelu1", "h1", "v1", "u1", "gelu0", "h0"])
        v_s = Steps(sem("vector"), ["v0", "u0", "gate1", "h1", "v1", "u1", "gate0"] + V + ["h0"])
        us, vs, gs = sem("u_in"), sem("v_in"), [sem("gates_in0"), sem("gates_in1")]
        first = sem("first")
        Z = [K.ps[:, 2 * n:2 * n + 2, 0:HT] for n in range(4)]
        N = ROWS // R
        block = ctx.enter_context(nc.Block())

        def by_stage(r):
            return g[:, r, :].rearrange("p (s t) -> p s t", t=TC)

        def every_turn(eng, body):
            with eng.Fori(0, N - 1) as i:
                body(i, False)
            body(N - 1, True)

        @block.sync
        def _(sp):
            sp.dma_start(u[:, :, :], a["peer_u"][0]).then_inc(us, 16)
            sp.dma_start(by_stage(0), K.gates[:, :, 0, :]).then_inc(gs[0], 16)
            sp.wait_ge(first, 2)
            sp.dma_start(u[:, :, :], a["peer_u"][1]).then_inc(us, 16)

            def body(i, last):
                sp.wait_ge(v_s.sem, v_s.of(i, "v1", 1))
                sp.dma_start(v[:, :, :], a["peer_v"][R * i]).then_inc(vs, 16)
                sp.wait_ge(v_s.sem, v_s.of(i, "gate1", 1))
                sp.dma_start(by_stage(1), K.gates[:, :, R * i + 1, :]).then_inc(gs[1], 16)
                if not last:
                    sp.wait_ge(v_s.sem, v_s.of(i, "u1", 1))
                    sp.dma_start(u[:, :, :], a["peer_u"][R * i + 2]).then_inc(us, 16)
                sp.wait_ge(v_s.sem, v_s.of(i, "v0"))
                sp.dma_start(v[:, :, :], a["peer_v"][R * i + 1]).then_inc(vs, 16)
                if not last:
                    sp.wait_ge(v_s.sem, v_s.of(i, "u0"))
                    sp.dma_start(u[:, :, :], a["peer_u"][R * i + 3]).then_inc(us, 16)
                    sp.wait_ge(v_s.sem, v_s.of(i, "gate0", 1))
                    sp.dma_start(by_stage(0), K.gates[:, :, R * i + 2, :]).then_inc(gs[0], 16)
            every_turn(sp, body)

        @block.tensor
        def _(pe):
            pe_s.ahead(pe)
            pe.wait_ge(first, 2)
            project3(pe, Z[0], uh[:, 0, :, :], ul[:, 0, :, :], K.hh, K.hl).then_inc(first, 1)

            def body(i, last):
                pe.wait_ge(v_s.sem, v_s.of(i, "u1", 1))
                pe.wait_ge(a_s.sem, a_s.of(i, "gelu1", 1))
                project3(pe, Z[1], uh[:, 1, :, :], ul[:, 1, :, :], K.hh, K.hl).then_inc(pe_s.step("U1"), 1)
                if last:
                    pe.drain().then_inc(pe_s.step("U0"), 1)
                else:
                    pe.wait_ge(v_s.sem, v_s.of(i, "u0"))
                    pe.wait_ge(a_s.sem, a_s.of(i, "gelu0", 1))
                    project3(pe, Z[0], uh[:, 0, :, :], ul[:, 0, :, :], K.hh, K.hl).then_inc(pe_s.step("U0"), 1)
                for d in range(DC):
                    pe.wait_ge(v_s.sem, v_s.of(i, V[d - 2]) if d >= 2 else v_s.of(i, "v1"))
                    z = Z[2 + d % 2]
                    for r in range(R):
                        for n in range(2):
                            t = slice(n * HT, (n + 1) * HT)
                            pe.matmul(z[:, n, :], vh[:, r, d, :], hh[:, r, t], start=(r == 0), stop=False)
                            pe.matmul(z[:, n, :], vh[:, r, d, :], hl[:, r, t], start=False, stop=False)
                        for n in range(2):
                            t = slice(n * HT, (n + 1) * HT)
                            done = pe.matmul(z[:, n, :], vl[:, r, d, :], hh[:, r, t], start=False, stop=(r == R - 1))
                    done.then_inc(pe_s.step(V[d]), 1)
            every_turn(pe, body)

        @block.scalar
        def _(act):
            a_s.ahead(act)
            act.wait_ge(us, 16)
            act.copy(uh[:, 0, :, :], u[:, :, :]).then_inc(first, 1)
            act.wait_ge(us, 32)
            act.copy(uh[:, 1, :, :], u[:, :, :]).then_inc(us, 1)
            act.wait_ge(first, 3)
            act.activation(halves(h[:, 0, :]), Z[0], ACT.Gelu).then_inc(first, 1)
            act.wait_ge(first, 5)
            act.copy(hh[:, 0, :], h[:, 0, :]).then_inc(first, 1)

            def body(i, last):
                act.wait_ge(pe_s.sem, pe_s.of(i, V[-1], 1))
                act.wait_ge(vs, 32 * i + 16)
                act.copy(vh[:, 0, :, :], v[:, :, :]).then_inc(a_s.step("v0"), 1)
                if last:
                    act.drain().then_inc(a_s.step("u0"), 1)
                else:
                    act.wait_ge(us, 32 * i + 49)
                    act.copy(uh[:, 0, :, :], u[:, :, :]).then_inc(a_s.step("u0"), 1)
                act.wait_ge(pe_s.sem, pe_s.of(i, "U1"))
                act.activation(halves(h[:, 1, :]), Z[1], ACT.Gelu).then_inc(a_s.step("gelu1"), 1)
                act.wait_ge(v_s.sem, v_s.of(i, "gate1"))
                act.copy(hh[:, 1, :], h[:, 1, :]).then_inc(a_s.step("h1"), 1)
                act.wait_ge(vs, 32 * i + 32)
                act.copy(vh[:, 1, :, :], v[:, :, :]).then_inc(a_s.step("v1"), 1)
                if last:
                    return
                act.wait_ge(us, 32 * i + 65)
                act.copy(uh[:, 1, :, :], u[:, :, :]).then_inc(a_s.step("u1"), 1)
                act.wait_ge(pe_s.sem, pe_s.of(i, "U0"))
                act.activation(halves(h[:, 0, :]), Z[0], ACT.Gelu).then_inc(a_s.step("gelu0"), 1)
                act.wait_ge(v_s.sem, v_s.of(i, "gate0"))
                act.wait_ge(pe_s.sem, pe_s.of(i, V[-1]))
                act.copy(hh[:, 0, :], h[:, 0, :]).then_inc(a_s.step("h0"), 1)
            every_turn(act, body)

        @block.vector
        def _(dve):
            dve.wait_ge(first, 1)
            dve.tensor_tensor(ul[:, 0, :, :], u[:, :, :], uh[:, 0, :, :].bitcast(F32), ALU.subtract).then_inc(first, 1)
            dve.wait_ge(us, 33)
            dve.tensor_tensor(ul[:, 1, :, :], u[:, :, :], uh[:, 1, :, :].bitcast(F32), ALU.subtract)
            dve.wait_ge(first, 4)
            dve.wait_ge(gs[0], 16)
            dve.tensor_tensor(h[:, 0, :], h[:, 0, :], g[:, 0, :], ALU.mult).then_inc(first, 1)
            dve.wait_ge(first, 6)
            dve.tensor_tensor(hl[:, 0, :], h[:, 0, :], hh[:, 0, :].bitcast(F32), ALU.subtract)
            dve.drain()
            v_s.ahead(dve)

            def body(i, last):
                def low(name, out, src, high):
                    dve.wait_ge(a_s.sem, a_s.of(i, name))
                    dve.tensor_tensor(out, src, high.bitcast(F32), ALU.subtract).then_inc(v_s.step(name), 1)

                def gated(r, turns):
                    dve.wait_ge(a_s.sem, a_s.of(i, f"gelu{r}"))
                    dve.wait_ge(gs[r], 16 * turns + 16)
                    dve.tensor_tensor(h[:, r, :], h[:, r, :], g[:, r, :], ALU.mult).then_inc(v_s.step(f"gate{r}"), 1)

                low("v0", vl[:, 0, :, :], v[:, :, :], vh[:, 0, :, :])
                if last:
                    dve.drain().then_inc(v_s.step("u0"), 1)
                else:
                    low("u0", ul[:, 0, :, :], u[:, :, :], uh[:, 0, :, :])
                gated(1, i)
                low("h1", hl[:, 1, :], h[:, 1, :], hh[:, 1, :])
                low("v1", vl[:, 1, :, :], v[:, :, :], vh[:, 1, :, :])
                if last:
                    dve.drain().then_inc(v_s.step("u1"), 1)
                    dve.drain().then_inc(v_s.step("gate0"), 1)
                else:
                    low("u1", ul[:, 1, :, :], u[:, :, :], uh[:, 1, :, :])
                    gated(0, i + 1)
                for d in range(DC):
                    x = halves(x1[:, d, :])
                    dve.wait_ge(pe_s.sem, pe_s.of(i, V[d]))
                    dve.tensor_tensor(x, x, Z[2 + d % 2], ALU.add).then_inc(v_s.step(V[d]), 1)
                if not last:
                    low("h0", hl[:, 0, :], h[:, 0, :], hh[:, 0, :])
            every_turn(dve, body)


class Kit:
    pass


def constants():
    t = np.arange(C)
    h2, t2 = np.repeat([0, 1], C), np.tile(t, 2)
    same = h2[:, None] == h2[None, :]
    i, s = t2[:, None], t2[None, :]
    out = {}
    mask = np.zeros((P, 2, 4, P))
    b16, b8 = i // 16 == s // 16, i // LSEQ == s // LSEQ
    mask[:, 0, 0] = same & b16 & (i < s)
    mask[:, 0, 1] = same & (i < s)
    mask[:, 0, 2] = mask[:, 0, 3] = same & (i <= s)
    mask[:, 1, 0] = mask[:, 1, 1] = same & b8 & (i < s)
    mask[:, 1, 2] = mask[:, 1, 3] = same & b8 & (i <= s)
    out["c_mask"] = mask
    out["c_moff"] = same & ~b16 & (i < s)
    out["c_mlow"] = np.stack([same & b16 & (i > s), same & b8 & (i > s)], 1)
    out["c_mseq"] = t2[:, None] // LSEQ == np.arange(NSEQ)[None, :]
    one0 = np.ones((P, T))
    one0[:, 0:TP:C] = 0
    one0[:, TP::LSEQ] = 0
    out["c_one0"] = one0
    f = np.arange(P)
    out["c_blk"] = f[:, None] // HEAD == f[None, :] // HEAD
    out["c_sel"] = f[:, None] % C == np.arange(C)[None, :]
    out["c_ident"] = np.eye(P)
    out["c_half30"] = np.full((P, 1), 15 * np.log(2.0))
    pos = np.concatenate([np.arange(TP), PAST + np.tile(np.arange(LSEQ), NSEQ)]).astype(np.float32)
    inv = np.power(np.float32(10000.0), -np.linspace(0.0, 1.0, P // 2, dtype=np.float32)).astype(np.float32)
    ang = (inv[:, None] * pos[None, :]).astype(np.float32).astype(np.float64)
    out["c_cos"] = np.concatenate([np.cos(ang), np.cos(ang)])
    out["c_sin"] = np.concatenate([-np.sin(ang), np.sin(ang)])
    out["c_perm"] = f[:, None] == (f[None, :] + P // 2) % P
    ret = np.zeros((HB, P, RET_CON))
    for h in range(HB):
        lg = float(np.log(np.float32(1.0 - 2.0 ** (-5.0 - h))))
        i = np.arange(RC)
        ts = np.arange(TS)
        d = i[None, :] - i[:, None]
        ds = ts[None, :] - ts[:, None]
        own = ts[None, :] // LSEQ == ts[:, None] // LSEQ
        ret[h, :, 0:TP] = np.exp(lg * (np.arange(TP) % RC + 1.0))
        ret[h, :, TP:T] = np.exp(lg * (ts % LSEQ + 1.0))
        ret[h, :, T:T + RC] = np.where(d >= 0, np.exp(lg * np.maximum(d, 0)), 0)
        ret[h, :TS, T + RC:T + RC + TS] = np.where((ds >= 0) & own, np.exp(lg * np.maximum(ds, 0)), 0)
        o = T + RC + TS
        ret[h, :, o] = np.exp(lg * (RC - 1.0 - i))
        ret[h, :, o + 1] = np.exp(lg * RC)
        ret[h, :, o + 2] = np.exp(lg * LSEQ)
        ret[h, :TS, o + 3:] = np.exp(lg * (LSEQ - 1.0 - ts % LSEQ))[:, None] * (ts[:, None] // LSEQ == np.arange(NSEQ))
    out["c_ret"] = ret
    return {k: np.ascontiguousarray(v, dtype=np.float32) for k, v in out.items()}


def columns(w):
    k, n = w.shape
    return np.ascontiguousarray(w.reshape(k // P, P, n // P, P).transpose(2, 1, 0, 3))


def features(v):
    return np.ascontiguousarray(v.reshape(-1, P).T)


def lay_out(i):
    A = {k: np.asarray(v) for k, v in i.items()}
    out = constants()
    x = np.concatenate([A["x_prompt"].reshape(TP, D), A["x_sample"].reshape(TS, D)])
    out["x"] = np.ascontiguousarray(x.T.reshape(DC, P, T).transpose(1, 0, 2))
    w = A["w_in"][0]
    out["w_rkv"] = np.ascontiguousarray(columns(w[:, :3072]).reshape(3, PAIRS, P, DC, P).transpose(1, 0, 2, 3, 4))
    out["w_lora"] = np.ascontiguousarray(w[:, 3072:3360].reshape(DC, P, LORA).transpose(1, 0, 2))
    out["w_low2"] = np.ascontiguousarray(np.concatenate(
        [np.concatenate([A["w_w2"][0], A["w_a2"][0]]).reshape(P, PAIRS, P), A["w_g2"][0][:P].reshape(P, PAIRS, P)], 2)
        .transpose(1, 0, 2))
    out["w_low3"] = np.ascontiguousarray(A["w_g2"][0][P:].reshape(32, PAIRS, P).transpose(1, 0, 2))
    mu = A["mu_shift"][0]
    out["w_par"] = np.ascontiguousarray(np.stack(
        [features(mu[0:1024]), features(mu[1024:2048]), features(mu[2048:3072])]
        + [features(A[n][0]) for n in ("w0", "a0", "k_k", "k_a", "r_k", "lnx_w", "lnx_b")], 2))

    def with_lora(rows):
        n = rows.shape[0]
        r = rows[:, :3072].reshape(n, 3, PAIRS, P).transpose(3, 2, 1, 0).reshape(P, 3 * PAIRS, n)
        l = np.zeros((P, 3, n), np.float32)
        l[:, 0], l[:, 1], l[:32, 2] = rows[:, 3072:3200].T, rows[:, 3200:3328].T, rows[:, 3328:].T
        return np.ascontiguousarray(np.concatenate([r, l], 1))

    out["lora_mu"] = np.ascontiguousarray(with_lora(mu[None])[:, 3 * PAIRS:, 0])
    out["shift_in"] = with_lora(A["state_shift"][0])
    out["wkv_in"] = np.ascontiguousarray(A["state_wkv"][0].reshape(NSEQ, PAIRS, 2, HEAD, HEAD)
                                         .transpose(1, 2, 4, 0, 3).reshape(PAIRS, P, NSEQ, HEAD))
    out["g_norm1"] = features(A["norm1"][0])
    out["g_norm2"] = features(A["norm2"][0])
    out["g_normf"] = features(A["norm_f"])
    q0, k0, v0, g0, m0 = 3360, 3360 + 1024, 3360 + 2048, 3360 + 4096, 3360 + 6144
    value, gate = (columns(w[:, lo:hi]).reshape(HB, 2, P, DC, P) for lo, hi in ((v0, g0), (g0, m0)))
    out["w_ret"] = np.ascontiguousarray(np.concatenate(
        [columns(w[:, q0:k0])[:, None], columns(w[:, k0:v0])[:, None], value, gate], 1))
    out["ret_in"] = np.ascontiguousarray(A["state_ret"][0].transpose(1, 2, 0, 3))
    out["w_ga"], out["w_gb"] = columns(w[:, m0:m0 + D]), columns(w[:, m0 + D:])
    out["w_pa"], out["w_pb"], out["w_out"] = (columns(A[n][0]) for n in ("w_pa", "w_pb", "w_out"))
    out["c_iota"] = np.ascontiguousarray(np.broadcast_to(np.arange(P, dtype=np.float32), (P, P)))
    out["w_q"] = columns(A["peer_wq"][0])
    out["keys"] = np.ascontiguousarray(A["peer_keys"][0].transpose(3, 0, 1, 2).reshape(P, 2 * PH, NK))
    out["peer_u"] = np.ascontiguousarray(A["peer_u"][0].reshape(ROWS, P, DC, P).transpose(0, 3, 2, 1))
    out["peer_v"] = np.ascontiguousarray(A["peer_v"][0].reshape(ROWS, P, DC, P))
    return out


OUTS = {"y": (P, DC, T), "ret_out": (HB, P, 1 + NSEQ, VH), "shift_out": (P, 3 * PAIRS + 3, 1 + NSEQ), "wkv_out": (PAIRS, P, 1 + NSEQ, HEAD)}


def build(nc, a):
    K = Kit()
    with ExitStack() as ctx:
        K.ps = ctx.enter_context(nc.psum_tensor("ps", [P, 8, 512], F32))
        K.ones = ctx.enter_context(nc.sbuf_tensor("ones", [P, P], F32))
        K.ident = ctx.enter_context(nc.sbuf_tensor("ident", [P, P], F32))
        K.half30 = ctx.enter_context(nc.sbuf_tensor("half30", [P, 1], F32))
        K.hn = ctx.enter_context(nc.sbuf_tensor("hn", [P, DC, T], F32))
        K.low, m_high, K.hh = (overlaid(nc, n, [P, DC, T]) for n in ("hn_low", "m_high", "hn2_high"))
        K.oa = nc.dram_tensor("oa", (PAIRS, P, T), F32, kind="Internal").ap()
        K.ob = nc.dram_tensor("ob", (HB, P, 2, T), F32, kind="Internal").ap()
        g1 = ctx.enter_context(nc.sbuf_tensor("g1", [P, DC], F32))
        s_c = ctx.enter_context(nc.semaphore("constants"))
        s_1 = ctx.enter_context(nc.semaphore("ones_made"))
        with nc.Block() as block:
            @block.sync
            def _(sp):
                for dst, src in ((K.ident, "c_ident"), (K.half30, "c_half30"), (g1, "g_norm1")):
                    sp.dma_start(dst[:, :], a[src]).then_inc(s_c, 16)
                sp.wait_ge(s_c, 48)

            @block.gpsimd
            def _(pool):
                pool.memset(K.ones[:, :], 1.0).then_inc(s_1, 1)
                pool.wait_ge(s_1, 1)
        with nc.sbuf_tensor("x1a", [P, DC, T], F32) as xt:
            norm_stage(nc, K, "n1", xt, K.hn, g1, load=a["x"])
        rwkv_stage(nc, K, a)
        x1 = ctx.enter_context(nc.sbuf_tensor("x1", [P, DC, T], F32))
        K.high, ob_high = (overlaid(nc, n, [P, DC, T]) for n in ("hn_high", "ob_high"))
        K.gb = nc.dram_tensor("gb", (DC, P, T), F32, kind="Internal").ap()
        ret_stage(nc, K, a)
        g2 = ctx.enter_context(nc.sbuf_tensor("g2", [P, 2, DC], F32))
        with nc.sbuf_tensor("m", [P, DC, T], F32) as m:
            m_low = overlaid(nc, "m_low", [P, DC, T])
            merge_a_stage(nc, K, a, m)
            merge_b_stage(nc, K, a, m, m_low, ob_high, m_high)
            out_stage(nc, K, a, m_high, m_low, x1)
        s_g = ctx.enter_context(nc.semaphore("gains"))
        with nc.Block() as block:
            @block.sync
            def _(sp):
                for n, src in enumerate(("g_norm2", "g_normf")):
                    sp.dma_start(g2[:, n, :], a[src]).then_inc(s_g, 16)
                sp.wait_ge(s_g, 32)
        K.gates = nc.dram_tensor("gates", (P, T // TC, ROWS, TC), F32, kind="Internal").ap()
        with nc.sbuf_tensor("hn2_low", [P, DC, T], F32R) as K.hl:
            with nc.sbuf_tensor("hn2", [P, DC, T], F32) as hn2:
                norm_stage(nc, K, "n2", x1, hn2, g2[:, 0, :], parts=(K.hh, K.hl))
            with nc.sbuf_tensor("slots", [P, 3, NTT * P], F32) as slots:
                with (nc.sbuf_tensor("top_v", [P, NTT, 2 * PH, TOPK], F32) as top_v,
                      nc.sbuf_tensor("top_i", [P, NTT, 2 * PH, TOPK], F32) as top_i):
                    route_stage(nc, K, a, top_v, top_i)
                    pick_stage(nc, K, a, top_v, top_i, slots)
                gates_stage(nc, K, a, slots)
            experts_stage(nc, K, a, x1)
        with nc.sbuf_tensor("y_sb", [P, DC, T], F32) as y:
            norm_stage(nc, K, "nf", x1, y, g2[:, 1, :], store=a["y"])


def kernel(**inputs):
    import concourse.bacc as bacc
    from concourse.bass_utils import run_bass_kernel_spmd

    nc = bacc.Bacc("TRN2", target_bir_lowering=False, num_devices=1)
    arrays = lay_out(inputs)
    a = {n: nc.dram_tensor(n, v.shape, F32, kind="ExternalInput").ap() for n, v in arrays.items()}
    a.update({n: nc.dram_tensor(n, s, F32, kind="ExternalOutput").ap() for n, s in OUTS.items()})
    build(nc, a)
    got = run_bass_kernel_spmd(nc, [arrays], core_ids=[0]).results[0]
    y = np.ascontiguousarray(got["y"].transpose(2, 1, 0).reshape(T, D))
    sh = got["shift_out"]
    rkv = sh[:, :3 * PAIRS].reshape(P, PAIRS, 3, 1 + NSEQ).transpose(3, 2, 1, 0).reshape(1 + NSEQ, 3 * PAIRS * P)
    lora = [sh[:n, 3 * PAIRS + t].T for t, n in enumerate((P, P, 32))]
    shift = np.ascontiguousarray(np.concatenate([rkv] + lora, 1))
    wkv = np.ascontiguousarray(got["wkv_out"].reshape(PAIRS, 2, HEAD, 1 + NSEQ, HEAD).transpose(3, 0, 1, 4, 2)
                               .reshape(1 + NSEQ, 2 * PAIRS, HEAD, HEAD))
    ret = np.ascontiguousarray(got["ret_out"].transpose(2, 0, 1, 3))
    return (y[:TP].reshape(1, TP, D), y[TP:].reshape(NSEQ, LSEQ, D), shift[None, :1], wkv[None, :1], ret[None, :1],
            shift[None, 1:], wkv[None, 1:], ret[None, 1:])
```
